# Optimizing a Trainium2 kernel written in Bass

```python
import math
import jax, jax.numpy as jnp
from jax import lax
import numpy as np

D_MODEL = 1024
BATCH = 1
SEQ = 256
DEPTH = 2

A_HEAD_DIM = 64
A_Q_HEADS = 8
A_KV_HEADS = 2
WINDOW = 128
ROPE_THETA = 10000.0
B_HEADS = 4
B_HEAD_DIM = 128
B_CONV = 4
B_CHUNK = 64
LRU_WIDTH = D_MODEL
LRU_BLOCKS = 4
LRU_CONV = 4
LRU_C = 8.0
D_FF = 4 * D_MODEL
A_Q_W = A_Q_HEADS * A_HEAD_DIM
A_KV_W = A_KV_HEADS * A_HEAD_DIM
B_W = B_HEADS * B_HEAD_DIM
HYB_SPLITS = (A_Q_W, A_KV_W, A_KV_W, 3 * B_W, B_W, B_HEADS, B_HEADS)
HYB_PROJ = A_Q_W + 2 * A_KV_W + 4 * B_W + 2 * B_HEADS
MIX_W = A_Q_W + B_W
N_HYB = (DEPTH + 1) // 2
N_REC = DEPTH // 2
DN_ALPHA = (2 * DEPTH) ** 0.25
DN_BETA = (8 * DEPTH) ** -0.25
LN_EPS = 1e-5
NORM_EPS = 1e-6


def split_cols(t, sizes):
    out, start = [], 0
    for s in sizes:
        out.append(t[..., start:start + s])
        start += s
    return out

def layer_norm(x, g, b):
    xf = x.astype(jnp.float32)
    mu = jnp.mean(xf, axis=-1, keepdims=True)
    var = jnp.mean(jnp.square(xf - mu), axis=-1, keepdims=True)
    y = (xf - mu) * lax.rsqrt(var + LN_EPS) * g.astype(jnp.float32) + b.astype(jnp.float32)
    return y.astype(x.dtype)

def l2_normalize(x):
    xf = x.astype(jnp.float32)
    return xf * lax.rsqrt(jnp.sum(xf * xf, axis=-1, keepdims=True) + NORM_EPS)

def apply_rope(x):
    T, dh = x.shape[1], x.shape[-1]
    half = dh // 2
    inv_freq = ROPE_THETA ** (-jnp.arange(half, dtype=jnp.float32) / half)
    ang = jnp.arange(T, dtype=jnp.float32)[:, None] * inv_freq[None, :]
    cos = jnp.cos(ang)[None, :, None, :]
    sin = jnp.sin(ang)[None, :, None, :]
    xf = x.astype(jnp.float32)
    x1, x2 = xf[..., :half], xf[..., half:]
    return jnp.concatenate([x1 * cos - x2 * sin, x2 * cos + x1 * sin], axis=-1).astype(x.dtype)

def causal_dwconv(x, w, b=None):
    K = w.shape[0]
    T = x.shape[1]
    xp = jnp.pad(x, ((0, 0), (K - 1, 0), (0, 0)))
    y = sum(xp[:, j:j + T] * w[j] for j in range(K))
    if b is not None:
        y = y + b
    return y

def sliding_window_attention(q, k, v, sinks):
    f32 = jnp.float32
    bsz, T, HQ, DH = q.shape
    HKV = k.shape[2]
    G = HQ // HKV
    W = WINDOW
    NB = T // W
    qb = q.reshape(bsz, NB, W, HKV, G, DH)

    def band(t):
        prev = jnp.pad(t, ((0, 0), (W, 0), (0, 0), (0, 0)))[:, :T]
        return jnp.concatenate([prev.reshape(bsz, NB, W, HKV, DH),
                                t.reshape(bsz, NB, W, HKV, DH)], axis=2)

    kb, vb = band(k), band(v)
    s = jnp.einsum('bnqhgd,bnkhd->bnhgqk', qb, kb).astype(f32) * (DH ** -0.5)
    dist = (jnp.arange(W)[:, None] + W) - jnp.arange(2 * W)[None, :]
    in_window = (dist >= 0) & (dist < W)
    key_pos = (jnp.arange(NB)[:, None] - 1) * W + jnp.arange(2 * W)[None, :]
    mask = in_window[None] & (key_pos >= 0)[:, None, :]
    s = jnp.where(mask[None, :, None, None], s, -jnp.inf)
    sink = jnp.broadcast_to(sinks.astype(f32).reshape(1, 1, HKV, G, 1, 1), s.shape[:-1] + (1,))
    p = jax.nn.softmax(jnp.concatenate([s, sink], axis=-1), axis=-1)[..., :-1]
    o = jnp.einsum('bnhgqk,bnkhd->bnqhgd', p.astype(v.dtype), vb)
    return o.reshape(bsz, T, HQ * DH)

def gated_delta_rule(q, k, v, g, beta):
    f32 = jnp.float32
    bsz, T, H, DK = q.shape
    DV = v.shape[-1]
    C = B_CHUNK
    N = T // C

    def chunk(t):
        t = t.astype(f32).reshape((bsz, N, C, H) + t.shape[3:])
        return jnp.moveaxis(t, 3, 1)

    q = chunk(q) * (DK ** -0.5)
    k = chunk(k)
    v = chunk(v)
    g = jnp.cumsum(chunk(g), axis=-1)
    beta = chunk(beta)
    k_beta = k * beta[..., None]
    v_beta = v * beta[..., None]
    idx = jnp.arange(C)
    incl = idx[:, None] >= idx[None, :]
    strict = idx[:, None] > idx[None, :]
    diff = g[..., :, None] - g[..., None, :]
    decay_incl = jnp.exp(jnp.where(incl, diff, -jnp.inf))
    decay_strict = jnp.where(strict, decay_incl, 0.0)
    a_mat = jnp.einsum('bhnik,bhnjk->bhnij', k_beta, k) * decay_strict
    eye = jnp.eye(C, dtype=f32)
    t_mat = lax.linalg.triangular_solve(a_mat + eye, jnp.broadcast_to(eye, a_mat.shape),
                                        left_side=True, lower=True, unit_diagonal=True)
    u = jnp.einsum('bhnij,bhnjv->bhniv', t_mat, v_beta)
    w = jnp.einsum('bhnij,bhnjk->bhnik', t_mat, k_beta * jnp.exp(g)[..., None])
    qk = jnp.einsum('bhnik,bhnjk->bhnij', q, k) * decay_incl
    q_g = q * jnp.exp(g)[..., None]
    g_last = g[..., -1]
    k_tail = k * jnp.exp(g_last[..., None] - g)[..., None]
    xs = tuple(jnp.moveaxis(t, 2, 0) for t in (q_g, k_tail, u, w, qk, g_last))

    def step(S, inp):
        q_c, kt_c, u_c, w_c, qk_c, gl_c = inp
        v_new = u_c - jnp.einsum('bhck,bhkv->bhcv', w_c, S)
        o_c = jnp.einsum('bhck,bhkv->bhcv', q_c, S) + jnp.einsum('bhij,bhjv->bhiv', qk_c, v_new)
        S = S * jnp.exp(gl_c)[..., None, None] + jnp.einsum('bhck,bhcv->bhkv', kt_c, v_new)
        return S, o_c

    S0 = jnp.zeros((bsz, H, DK, DV), f32)
    _, o = lax.scan(step, S0, xs)
    return jnp.transpose(o, (1, 0, 3, 2, 4)).reshape(bsz, T, H, DV)

def hybrid_mixer(x, w_in, sinks, conv_w, a_log, dt_bias, norm_w, w_out):
    f32 = jnp.float32
    bsz, T, _ = x.shape
    proj = x @ w_in
    qa, ka, va, qkv_b, z, beta_logit, a_logit = split_cols(proj, HYB_SPLITS)
    qa = apply_rope(qa.reshape(bsz, T, A_Q_HEADS, A_HEAD_DIM))
    ka = apply_rope(ka.reshape(bsz, T, A_KV_HEADS, A_HEAD_DIM))
    va = va.reshape(bsz, T, A_KV_HEADS, A_HEAD_DIM)
    o_a = sliding_window_attention(qa, ka, va, sinks)
    qkv_b = jax.nn.silu(causal_dwconv(qkv_b, conv_w))
    qb, kb, vb = split_cols(qkv_b, (B_W, B_W, B_W))
    qb = l2_normalize(qb.reshape(bsz, T, B_HEADS, B_HEAD_DIM))
    kb = l2_normalize(kb.reshape(bsz, T, B_HEADS, B_HEAD_DIM))
    vb = vb.reshape(bsz, T, B_HEADS, B_HEAD_DIM)
    beta = jax.nn.sigmoid(beta_logit.astype(f32))
    g = -jnp.exp(a_log.astype(f32)) * jax.nn.softplus(a_logit.astype(f32) + dt_bias.astype(f32))
    o_b = gated_delta_rule(qb, kb, vb, g, beta)
    o_b = o_b * lax.rsqrt(jnp.mean(o_b * o_b, axis=-1, keepdims=True) + NORM_EPS) * norm_w.astype(f32)
    o_b = o_b * jax.nn.silu(z.astype(f32).reshape(bsz, T, B_HEADS, B_HEAD_DIM))
    o_b = o_b.reshape(bsz, T, B_W).astype(x.dtype)
    return jnp.concatenate([o_a, o_b], axis=-1) @ w_out

def rg_lru(x, w_a, b_a, w_x, b_x, lam):
    f32 = jnp.float32
    bsz, T, W = x.shape
    xh = x.reshape(bsz, T, LRU_BLOCKS, W // LRU_BLOCKS)
    r = jax.nn.sigmoid((jnp.einsum('bthi,hij->bthj', xh, w_a).reshape(bsz, T, W) + b_a).astype(f32))
    i = jax.nn.sigmoid((jnp.einsum('bthi,hij->bthj', xh, w_x).reshape(bsz, T, W) + b_x).astype(f32))
    log_a = -LRU_C * r * jax.nn.softplus(-lam.astype(f32))
    a = jnp.exp(log_a)
    b = jnp.sqrt(-jnp.expm1(2.0 * log_a)) * (i * x.astype(f32))

    def combine(c1, c2):
        a1, b1 = c1
        a2, b2 = c2
        return a1 * a2, a2 * b1 + b2

    _, h = lax.associative_scan(combine, (a, b), axis=1)
    return h.astype(x.dtype)

def recurrent_mixer(x, w_in, conv_w, conv_b, w_a, b_a, w_x, b_x, lam, w_out):
    proj = x @ w_in
    xr, gate = split_cols(proj, (LRU_WIDTH, LRU_WIDTH))
    xr = causal_dwconv(xr, conv_w, conv_b)
    h = rg_lru(xr, w_a, b_a, w_x, b_x, lam)
    return (h * jax.nn.gelu(gate)) @ w_out

def sqrelu_mlp(x, w1, w2):
    h = jax.nn.relu(x @ w1)
    return (h * h) @ w2

def first_inputs(seed: int = 0) -> dict:
    key = jax.random.key(seed)
    ks = jax.random.split(key, 24)
    f32 = jnp.float32

    def nrm(k, shape, scale):
        return jax.random.normal(k, shape, f32) * scale

    bw = LRU_WIDTH // LRU_BLOCKS
    x = nrm(ks[0], (BATCH, SEQ, D_MODEL), 1.0)
    hyb_w_in = nrm(ks[1], (N_HYB, D_MODEL, HYB_PROJ), D_MODEL ** -0.5)
    hyb_sinks = nrm(ks[2], (N_HYB, A_Q_HEADS), 0.5)
    hyb_conv_w = nrm(ks[3], (N_HYB, B_CONV, 3 * B_W), B_CONV ** -0.5)
    hyb_a_log = jnp.log(jax.random.uniform(ks[4], (N_HYB, B_HEADS), f32, 1.0, 16.0))
    dt = jnp.exp(jax.random.uniform(ks[5], (N_HYB, B_HEADS), f32, math.log(1e-3), math.log(1e-1)))
    hyb_dt_bias = dt + jnp.log(-jnp.expm1(-dt))
    hyb_norm_w = 1.0 + nrm(ks[6], (N_HYB, B_HEAD_DIM), 0.02)
    hyb_w_out = nrm(ks[7], (N_HYB, MIX_W, D_MODEL), DN_BETA * MIX_W ** -0.5)
    rec_w_in = nrm(ks[8], (N_REC, D_MODEL, 2 * LRU_WIDTH), D_MODEL ** -0.5)
    rec_conv_w = nrm(ks[9], (N_REC, LRU_CONV, LRU_WIDTH), LRU_CONV ** -0.5)
    rec_conv_b = nrm(ks[10], (N_REC, LRU_WIDTH), 0.02)
    rec_w_a = nrm(ks[11], (N_REC, LRU_BLOCKS, bw, bw), bw ** -0.5)
    rec_b_a = nrm(ks[12], (N_REC, LRU_WIDTH), 0.02)
    rec_w_x = nrm(ks[13], (N_REC, LRU_BLOCKS, bw, bw), bw ** -0.5)
    rec_b_x = nrm(ks[14], (N_REC, LRU_WIDTH), 0.02)
    u = jax.random.uniform(ks[15], (N_REC, LRU_WIDTH), f32, 0.9, 0.999)
    a0 = u ** (1.0 / LRU_C)
    rec_lambda = jnp.log(a0) - jnp.log1p(-a0)
    rec_w_out = nrm(ks[16], (N_REC, LRU_WIDTH, D_MODEL), DN_BETA * LRU_WIDTH ** -0.5)
    ln1_g = 1.0 + nrm(ks[17], (DEPTH, D_MODEL), 0.02)
    ln1_b = nrm(ks[18], (DEPTH, D_MODEL), 0.02)
    mlp_w1 = nrm(ks[19], (DEPTH, D_MODEL, D_FF), D_MODEL ** -0.5)
    mlp_w2 = nrm(ks[20], (DEPTH, D_FF, D_MODEL), DN_BETA * D_FF ** -0.5)
    ln2_g = 1.0 + nrm(ks[21], (DEPTH, D_MODEL), 0.02)
    ln2_b = nrm(ks[22], (DEPTH, D_MODEL), 0.02)
    return {'x': x, 'hyb_w_in': hyb_w_in, 'hyb_sinks': hyb_sinks, 'hyb_conv_w': hyb_conv_w,
            'hyb_a_log': hyb_a_log, 'hyb_dt_bias': hyb_dt_bias, 'hyb_norm_w': hyb_norm_w,
            'hyb_w_out': hyb_w_out, 'rec_w_in': rec_w_in, 'rec_conv_w': rec_conv_w,
            'rec_conv_b': rec_conv_b, 'rec_w_a': rec_w_a, 'rec_b_a': rec_b_a, 'rec_w_x': rec_w_x,
            'rec_b_x': rec_b_x, 'rec_lambda': rec_lambda, 'rec_w_out': rec_w_out,
            'ln1_g': ln1_g, 'ln1_b': ln1_b, 'mlp_w1': mlp_w1, 'mlp_w2': mlp_w2,
            'ln2_g': ln2_g, 'ln2_b': ln2_b}

def first_block(x, hyb_w_in, hyb_sinks, hyb_conv_w, hyb_a_log, hyb_dt_bias, hyb_norm_w, hyb_w_out,
              rec_w_in, rec_conv_w, rec_conv_b, rec_w_a, rec_b_a, rec_w_x, rec_b_x, rec_lambda,
              rec_w_out, ln1_g, ln1_b, mlp_w1, mlp_w2, ln2_g, ln2_b):
    for layer in range(DEPTH):
        j = layer // 2
        if layer % 2 == 0:
            mix = hybrid_mixer(x, hyb_w_in[j], hyb_sinks[j], hyb_conv_w[j], hyb_a_log[j],
                               hyb_dt_bias[j], hyb_norm_w[j], hyb_w_out[j])
        else:
            mix = recurrent_mixer(x, rec_w_in[j], rec_conv_w[j], rec_conv_b[j], rec_w_a[j],
                                  rec_b_a[j], rec_w_x[j], rec_b_x[j], rec_lambda[j], rec_w_out[j])
        x = layer_norm(DN_ALPHA * x + mix, ln1_g[layer], ln1_b[layer])
        x = layer_norm(DN_ALPHA * x + sqrelu_mlp(x, mlp_w1[layer], mlp_w2[layer]), ln2_g[layer], ln2_b[layer])
    return x


GRID_W = 64
CTX_LEN = 256
D_FF_2 = 4 * D_MODEL
N_MOD = 6

MLA_HEADS = 8
QK_NOPE = 64
QK_ROPE = 32
QK_DIM = QK_NOPE + QK_ROPE
V_DIM = 64
MLA_WIDTH = MLA_HEADS * V_DIM
Q_LORA = 256
KV_LORA = 128
AXIS_DIM = QK_ROPE // 2
Q_BLOCK = 128
SM_SCALE = 1.0 / math.sqrt(QK_DIM)

CONF_WIDTH = 256
CONF_K = 31
SC_WIDTH = 256
SC_K = 3

MIX_WIDTH = MLA_WIDTH + CONF_WIDTH + SC_WIDTH

Q_END = Q_LORA
KV_START = Q_END
KV_END = KV_START + KV_LORA
ROPE_END = KV_END + QK_ROPE
CONF_END = ROPE_END + 2 * CONF_WIDTH
IN_WIDTH = CONF_END + 3 * SC_WIDTH

EPS = 1e-6


def rmsnorm(u, g):
    uf = u.astype(jnp.float32)
    y = uf * lax.rsqrt(jnp.mean(uf * uf, axis=-1, keepdims=True) + EPS)
    return (y * g.astype(jnp.float32)).astype(u.dtype)

def layernorm(u, g, b):
    uf = u.astype(jnp.float32)
    mu = jnp.mean(uf, axis=-1, keepdims=True)
    d = uf - mu
    y = d * lax.rsqrt(jnp.mean(d * d, axis=-1, keepdims=True) + EPS)
    return (y * g.astype(jnp.float32) + b.astype(jnp.float32)).astype(u.dtype)

def modulation(cvec, w_mod, b_mod):
    m = jax.nn.silu(cvec) @ w_mod + b_mod
    return jnp.split(m[:, None, :], N_MOD, axis=-1)

def modulate(h, shift, scale):
    return h * (1.0 + scale) + shift

def axial_rope_tables(rows):
    row = jnp.broadcast_to(jnp.arange(rows)[:, None], (rows, GRID_W)).reshape(-1).astype(jnp.float32)
    col = jnp.broadcast_to(jnp.arange(GRID_W)[None, :], (rows, GRID_W)).reshape(-1).astype(jnp.float32)
    inv = 1.0 / (ROPE_THETA ** (jnp.arange(0, AXIS_DIM, 2, dtype=jnp.float32) / AXIS_DIM))
    ar = row[:, None] * inv
    ac = col[:, None] * inv
    ang = jnp.concatenate([ar, ar, ac, ac], axis=-1)
    return jnp.cos(ang), jnp.sin(ang)

def apply_axial_rope(u, cos, sin):
    def rot(p):
        h = p.shape[-1] // 2
        return jnp.concatenate([-p[..., h:], p[..., :h]], axis=-1)
    rotated = jnp.concatenate([rot(u[..., :AXIS_DIM]), rot(u[..., AXIS_DIM:])], axis=-1)
    return (u.astype(jnp.float32) * cos + rotated.astype(jnp.float32) * sin).astype(u.dtype)

def mla_queries(zq, g_q, w_q_b, rope):
    b, s, _ = zq.shape
    q = (rmsnorm(zq, g_q) @ w_q_b).reshape(b, s, MLA_HEADS, QK_DIM)
    if rope is None:
        return q
    cos, sin = rope
    q_rope = apply_axial_rope(q[..., QK_NOPE:], cos[:, None, :], sin[:, None, :])
    return jnp.concatenate([q[..., :QK_NOPE], q_rope], axis=-1)

def mla_keys_values(zkv, g_kv, w_kv_b, rope):
    b, s, _ = zkv.shape
    ckv, k_rope = zkv[..., :KV_LORA], zkv[..., KV_LORA:]
    kv = (rmsnorm(ckv, g_kv) @ w_kv_b).reshape(b, s, MLA_HEADS, QK_NOPE + V_DIM)
    k_nope, v = kv[..., :QK_NOPE], kv[..., QK_NOPE:]
    if rope is not None:
        cos, sin = rope
        k_rope = apply_axial_rope(k_rope, cos, sin)
    k_rope = jnp.broadcast_to(k_rope[:, :, None, :], (b, s, MLA_HEADS, QK_ROPE))
    return jnp.concatenate([k_nope, k_rope], axis=-1), v

def block_attention(q, k, v):
    b, s, h, dq = q.shape
    dv = v.shape[-1]
    nb = s // Q_BLOCK
    qb = jnp.moveaxis(q.reshape(b, nb, Q_BLOCK, h, dq), 1, 0)

    def attend(qblk):
        logits = jnp.einsum('bqhd,bkhd->bhqk', qblk, k).astype(jnp.float32) * SM_SCALE
        p = jax.nn.softmax(logits, axis=-1).astype(v.dtype)
        return jnp.einsum('bhqk,bkhd->bqhd', p, v)

    o = lax.map(attend, qb)
    return jnp.moveaxis(o, 0, 1).reshape(b, s, h * dv)

def depthwise_conv(u, w):
    k, ch = w.shape
    return lax.conv_general_dilated(
        u, w[:, None, :].astype(u.dtype), window_strides=(1,),
        padding=[(k // 2, k // 2)], dimension_numbers=('NWC', 'WIO', 'NWC'),
        feature_group_count=ch)

def conformer_branch(z, dw_w, dw_b, ln_g, ln_b):
    a, g = jnp.split(z, 2, axis=-1)
    u = a * jax.nn.sigmoid(g)
    u = depthwise_conv(u, dw_w) + dw_b
    u = layernorm(u, ln_g, ln_b)
    return jax.nn.silu(u)

def shortconv_branch(z, w):
    b_gate, c_gate, h = jnp.split(z, 3, axis=-1)
    return b_gate * depthwise_conv(c_gate * h, w)

def mix_stream(z, k, v, rope, g_q, w_q_b, conf_dw_w, conf_dw_b, conf_ln_g, conf_ln_b,
               sc_dw_w, g_branch, w_o):
    q = mla_queries(z[..., :Q_END], g_q, w_q_b, rope)
    attn = block_attention(q, k, v)
    conf = conformer_branch(z[..., ROPE_END:CONF_END], conf_dw_w, conf_dw_b, conf_ln_g, conf_ln_b)
    sc = shortconv_branch(z[..., CONF_END:], sc_dw_w)
    merged = jnp.concatenate([
        rmsnorm(attn, g_branch[:MLA_WIDTH]),
        rmsnorm(conf, g_branch[MLA_WIDTH:MLA_WIDTH + CONF_WIDTH]),
        rmsnorm(sc, g_branch[MLA_WIDTH + CONF_WIDTH:])], axis=-1)
    return merged @ w_o

def sqrelu_mlp_2(h, w1, w2):
    a = jax.nn.relu(h @ w1)
    return (a * a) @ w2

def second_inputs(seed: int = 0) -> dict:
    key = jax.random.key(seed)
    ks = jax.random.split(key, 32)
    f32 = jnp.float32

    def nrm(k, shape, scale):
        return jax.random.normal(k, shape, f32) * scale

    def gain(k, shape):
        return 1.0 + 0.05 * jax.random.normal(k, shape, f32)

    L, D = DEPTH, D_MODEL
    return {
        "x": nrm(ks[0], (BATCH, SEQ, D), 1.0),
        "c": nrm(ks[1], (BATCH, D), 1.0),
        "ctx": nrm(ks[2], (BATCH, CTX_LEN, D), 1.0),
        "c_ctx": nrm(ks[3], (D,), 1.0),
        "w_mod": nrm(ks[4], (L, D, N_MOD * D), 0.5 * D ** -0.5),
        "b_mod": nrm(ks[5], (L, N_MOD * D), 0.02),
        "g_pre_mix": gain(ks[6], (L, D)),
        "g_post_mix": gain(ks[7], (L, D)),
        "g_pre_mlp": gain(ks[8], (L, D)),
        "g_post_mlp": gain(ks[9], (L, D)),
        "w_in": nrm(ks[10], (L, D, IN_WIDTH), D ** -0.5),
        "g_q": gain(ks[11], (L, Q_LORA)),
        "w_q_b": nrm(ks[12], (L, Q_LORA, MLA_HEADS * QK_DIM), Q_LORA ** -0.5),
        "g_kv": gain(ks[13], (L, KV_LORA)),
        "w_kv_b": nrm(ks[14], (L, KV_LORA, MLA_HEADS * (QK_NOPE + V_DIM)), KV_LORA ** -0.5),
        "conf_dw_w": nrm(ks[15], (L, CONF_K, CONF_WIDTH), CONF_K ** -0.5),
        "conf_dw_b": nrm(ks[16], (L, CONF_WIDTH), 0.02),
        "conf_ln_g": gain(ks[17], (L, CONF_WIDTH)),
        "conf_ln_b": nrm(ks[18], (L, CONF_WIDTH), 0.02),
        "sc_dw_w": nrm(ks[19], (L, SC_K, SC_WIDTH), SC_K ** -0.5),
        "g_branch": gain(ks[20], (L, MIX_WIDTH)),
        "w_o": nrm(ks[21], (L, MIX_WIDTH, D), MIX_WIDTH ** -0.5),
        "w_mlp_in": nrm(ks[22], (L, D, D_FF_2), D ** -0.5),
        "w_mlp_out": nrm(ks[23], (L, D_FF_2, D), D_FF_2 ** -0.5),
    }

def second_block(x, c, ctx, c_ctx, w_mod, b_mod, g_pre_mix, g_post_mix, g_pre_mlp, g_post_mlp,
              w_in, g_q, w_q_b, g_kv, w_kv_b, conf_dw_w, conf_dw_b, conf_ln_g, conf_ln_b,
              sc_dw_w, g_branch, w_o, w_mlp_in, w_mlp_out):
    n_lat = x.shape[1]
    rows = n_lat // GRID_W
    rope = axial_rope_tables(rows)
    xl, xc = x, ctx
    for i in range(DEPTH):
        last = i == DEPTH - 1
        ml = modulation(c, w_mod[i], b_mod[i])
        mc = modulation(c_ctx[None, :], w_mod[i], b_mod[i])

        hl = modulate(rmsnorm(xl, g_pre_mix[i]), ml[0], ml[1])
        hc = modulate(rmsnorm(xc, g_pre_mix[i]), mc[0], mc[1])
        zl = hl @ w_in[i]
        if last:
            zc_kv = hc @ w_in[i][:, KV_START:ROPE_END]
        else:
            zc = hc @ w_in[i]
            zc_kv = zc[..., KV_START:ROPE_END]

        k_c, v_c = mla_keys_values(zc_kv, g_kv[i], w_kv_b[i], None)
        k_l, v_l = mla_keys_values(zl[..., KV_START:ROPE_END], g_kv[i], w_kv_b[i], rope)
        y_l = mix_stream(zl, jnp.concatenate([k_c, k_l], axis=1), jnp.concatenate([v_c, v_l], axis=1),
                         rope, g_q[i], w_q_b[i], conf_dw_w[i], conf_dw_b[i], conf_ln_g[i],
                         conf_ln_b[i], sc_dw_w[i], g_branch[i], w_o[i])
        xl_new = xl + ml[2] * rmsnorm(y_l, g_post_mix[i])

        h2 = modulate(rmsnorm(xl_new, g_pre_mlp[i]), ml[3], ml[4])
        xl_new = xl_new + ml[5] * rmsnorm(sqrelu_mlp_2(h2, w_mlp_in[i], w_mlp_out[i]), g_post_mlp[i])

        if not last:
            y_c = mix_stream(zc, k_c, v_c, None, g_q[i], w_q_b[i], conf_dw_w[i], conf_dw_b[i],
                             conf_ln_g[i], conf_ln_b[i], sc_dw_w[i], g_branch[i], w_o[i])
            xc_new = xc + mc[2] * rmsnorm(y_c, g_post_mix[i])
            h2c = modulate(rmsnorm(xc_new, g_pre_mlp[i]), mc[3], mc[4])
            xc = xc_new + mc[5] * rmsnorm(sqrelu_mlp_2(h2c, w_mlp_in[i], w_mlp_out[i]), g_post_mlp[i])
        xl = xl_new
    return xl


def setup_inputs(seed=0):
    out = dict(first_inputs(seed))
    for name, value in second_inputs(seed + 1).items():
        if name != "x":
            out[name + "_2"] = value
    return out


def reference(
    x, hyb_w_in, hyb_sinks, hyb_conv_w, hyb_a_log, hyb_dt_bias, hyb_norm_w, hyb_w_out, rec_w_in,
    rec_conv_w, rec_conv_b, rec_w_a, rec_b_a, rec_w_x, rec_b_x, rec_lambda, rec_w_out, ln1_g,
    ln1_b, mlp_w1, mlp_w2, ln2_g, ln2_b, c_2, ctx_2, c_ctx_2, w_mod_2, b_mod_2, g_pre_mix_2,
    g_post_mix_2, g_pre_mlp_2, g_post_mlp_2, w_in_2, g_q_2, w_q_b_2, g_kv_2, w_kv_b_2,
    conf_dw_w_2, conf_dw_b_2, conf_ln_g_2, conf_ln_b_2, sc_dw_w_2, g_branch_2, w_o_2,
    w_mlp_in_2, w_mlp_out_2,
):
    x = first_block(
        x, hyb_w_in, hyb_sinks, hyb_conv_w, hyb_a_log, hyb_dt_bias, hyb_norm_w, hyb_w_out,
        rec_w_in, rec_conv_w, rec_conv_b, rec_w_a, rec_b_a, rec_w_x, rec_b_x, rec_lambda,
        rec_w_out, ln1_g, ln1_b, mlp_w1, mlp_w2, ln2_g, ln2_b,
    )
    return second_block(
        x, c_2, ctx_2, c_ctx_2, w_mod_2, b_mod_2, g_pre_mix_2, g_post_mix_2, g_pre_mlp_2,
        g_post_mlp_2, w_in_2, g_q_2, w_q_b_2, g_kv_2, w_kv_b_2, conf_dw_w_2, conf_dw_b_2,
        conf_ln_g_2, conf_ln_b_2, sc_dw_w_2, g_branch_2, w_o_2, w_mlp_in_2, w_mlp_out_2,
    )


_drawn_inputs = setup_inputs


def setup_inputs(seed=0):
    import zlib

    import numpy as np

    out = dict(_drawn_inputs(seed))
    spreads = {}
    factors = {'hyb_sinks': 8.0,
     'hyb_a_log': 3.805,
     'hyb_norm_w': 8.0,
     'rec_conv_b': 3.165,
     'rec_b_a': 8.0,
     'rec_b_x': 8.0,
     'g_post_mix_2': 2.843,
     'g_post_mlp_2': 2.924,
     'g_q_2': 8.0,
     'g_kv_2': 3.548,
     'conf_dw_b_2': 7.486,
     'conf_ln_g_2': 4.164,
     'conf_ln_b_2': 8.0,
     'g_branch_2': 2.721}
    for name, (base, spread) in spreads.items():
        noise = np.random.default_rng([zlib.crc32(name.encode()), seed]).standard_normal(out[name].shape)
        drawn = base * np.exp(spread * noise) if base else spread * noise
        out[name] = __import__('jax').numpy.asarray(drawn.astype(out[name].dtype))
    for name, factor in factors.items():
        out[name] = (out[name] * factor).astype(out[name].dtype)
    return out
```

```python
import math

import numpy as np

import concourse.bass as bass
from concourse import mybir

F32 = mybir.dt.float32
F32R = mybir.dt.float32r
ALU = mybir.AluOpType
ACT = mybir.ActivationFunctionType
AX = mybir.AxisListType

P = 128
D = 1024
KT = D // P
SEQ = 256
CTX = 256
TB = SEQ + CTX
D_FF = 4096
DEPTH = 2
QUARTERS = D_FF // D
ALPHA = (2 * DEPTH) ** 0.25
LN_EPS = 1e-5
EPS = 1e-6

A_DH = 64
A_HEADS = 8
B_HEADS = 4
B_TAPS = 4
PAIRS = 2 * B_HEADS
DN_BLOCKS = [1, 2, 4, 8, 16, 32, 64]

HEADS = 8
QK = 96
NOPE = 64
DV = 64
SM_SCALE = 1.0 / math.sqrt(QK)
CONF_K = 31
SC_K = 3
N_MOD = 6

RAW_SLOTS = 8
SPLIT_SLOTS = 4
LEAD = SPLIT_SLOTS - 1
BANKS = 4
HYB_IN = 22
GATES = 4
L2_IN = 14
MLP_UNITS = 2 * KT * QUARTERS
U_HYB = 0
U_HOUT = U_HYB + HYB_IN
U_MLP1 = U_HOUT + KT
U_REC = U_MLP1 + MLP_UNITS
U_GATES = U_REC + KT
U_RGELU = U_GATES + GATES
U_ROUT = U_RGELU + KT
U_MLP2 = U_ROUT + KT
U_L2 = U_MLP2 + MLP_UNITS
L2_UNITS = L2_IN + 3 + KT + MLP_UNITS
UNITS = U_L2 + DEPTH * L2_UNITS
MOD_UNITS = DEPTH * N_MOD * KT
MOD_SLOTS = 2

_PARAM_WIDTHS = [
    ("hyb_conv", 12 * B_TAPS), ("norm_w", 1), ("sinks", A_HEADS), ("a_log", B_HEADS), ("dt_bias", B_HEADS),
    ("rec_conv", KT * B_TAPS), ("rec_conv_b", KT), ("b_a", KT), ("b_x", KT), ("lam", KT),
    ("ln1_g", 2 * KT), ("ln1_b", 2 * KT), ("ln2_g", 2 * KT), ("ln2_b", 2 * KT),
    ("cond", 2 * KT), ("b_mod", DEPTH * N_MOD * KT),
    ("g_pre_mix", 2 * KT), ("g_post_mix", 2 * KT), ("g_pre_mlp", 2 * KT), ("g_post_mlp", 2 * KT),
    ("g_q", 4), ("g_kv", 2), ("conf_w", DEPTH * 2 * CONF_K), ("conf_b", 4), ("conf_g", 4), ("conf_beta", 4),
    ("sc_w", DEPTH * 2 * SC_K), ("g_branch", 2 * KT), ("tail", KT * 8),
]
PCOL, _at = {}, 0
for _name, _width in _PARAM_WIDTHS:
    PCOL[_name] = _at
    _at += _width
N_PARAMS = _at

_SHARED = [("ident", P), ("rot2", P), ("cos2", SEQ), ("sin2", SEQ)]
_HYB = [("rot1", P), ("tri", P), ("incl", P), ("low1", P), ("up", 7 * P), ("cos1", SEQ), ("sin1", SEQ), ("window", 2 * P)]


def _columns(widths):
    at, out = 0, {}
    for name, width in widths:
        out[name] = at
        at += width
    return out, at


SCOL, N_SHARED = _columns(_SHARED)
HCOL, N_HYB = _columns(_HYB)


def program(nc, xT_in, ctxT_in, weights, mod_weights, params_in, shared_in, hyb_in, out):
    psum = nc.alloc_psum_tensor("psum", [P, 8, 512], F32)
    MODBANK = 7

    raw_ring = nc.alloc_sbuf_tensor("raw_ring", [P, RAW_SLOTS, D], F32)
    hi_ring = nc.alloc_sbuf_tensor("hi_ring", [P, SPLIT_SLOTS, D], F32R)
    lo_ring = nc.alloc_sbuf_tensor("lo_ring", [P, SPLIT_SLOTS, D], F32R)
    mod_ring = nc.alloc_sbuf_tensor("mod_ring", [P, MOD_SLOTS, D], F32)
    x = nc.alloc_sbuf_tensor("x", [P, KT, TB], F32)
    X_AT = (nc.sbuf_base + 31) // 32 * 32
    x_hi = nc.alloc_sbuf_tensor("x_hi", [P, KT, TB], F32R)
    x_lo = nc.alloc_sbuf_tensor("x_lo", [P, KT, TB], F32R)
    par = nc.alloc_sbuf_tensor("par", [P, N_PARAMS], F32)
    shared = nc.alloc_sbuf_tensor("shared", [P, N_SHARED], F32)
    ones = nc.alloc_sbuf_tensor("ones", [P, P], F32)
    eps = nc.alloc_sbuf_tensor("eps", [P, 2], F32)
    stat = nc.alloc_sbuf_tensor("stat", [P, TB], F32)
    rstd = nc.alloc_sbuf_tensor("rstd", [P, TB], F32)
    normed = nc.alloc_sbuf_tensor("normed", [P, 2, TB], F32)
    coef = nc.alloc_sbuf_tensor("coef", [P, DEPTH, N_MOD, KT, 2], F32)
    silu_c = nc.alloc_sbuf_tensor("silu_c", [P, KT, 2], F32)
    LAM_AT = (nc.sbuf_base + 31) // 32 * 32
    nc.alloc_sbuf_tensor("lam_place", [P, 6, KT], F32)
    SOFT_AT = (nc.sbuf_base + 31) // 32 * 32
    nc.alloc_sbuf_tensor("soft_place", [P, 4, 32], F32)
    Y0 = (nc.sbuf_base + 63) // 64 * 64
    Y_BYTES = KT * TB * 4
    M0 = Y0 + Y_BYTES
    END = nc.sbuf_usable_end

    class Region:

        def __init__(self, start, end):
            self.at, self.end = start, end

        def __call__(self, name, shape, dtype=F32):
            n = 4 * int(np.prod(shape[1:]))
            t = nc.alloc_sbuf_tensor_at(name, shape, dtype, offset=self.at)
            self.at += (n + 31) // 32 * 32
            assert self.at <= self.end, (name, self.at, self.end)
            return t

    y = Region(Y0, M0)("y", [P, KT, TB])
    r = Region(M0, END)
    hid_hi = r("hid_hi", [P, KT, TB], F32R)
    hid_lo = r("hid_lo", [P, KT, TB], F32R)
    relu = r("relu", [P, 2, TB])
    relu2 = r("relu2", [P, 2, TB])
    sq = r("sq", [P, KT, TB])

    h_conv = Region(Y0, M0)("h_conv", [P, 12, SEQ])
    r = Region(M0, END)
    h_const = r("h_const", [P, N_HYB])
    h_pad_at = r.at
    h_pad = r("h_pad", [P, 12, SEQ + B_TAPS - 1])
    h_pad_end = r.at
    h_qk = r("h_qk", [P, 5, SEQ])
    h_vT = r("h_vT", [P, SEQ])
    h_v = r("h_v", [P, 2, P])
    h_z = r("h_z", [P, B_HEADS, SEQ])
    h_lg = r("h_lg", [P, 2, 8])
    h_small = r("h_small", [P, 16, PAIRS])
    h_decay = r("h_decay", [P, PAIRS, P])
    h_expg = r("h_expg", [P, B_HEADS, P])
    h_gb = r("h_gb", [P, PAIRS, P])
    h_late = r.at
    h_vb = r("h_vb", [P, PAIRS, P])
    h_kbe_at = r.at
    h_kbe = r("h_kbe", [P, B_HEADS, P])
    h_ktail = r("h_ktail", [P, B_HEADS, P])
    h_wT = r("h_wT", [P, B_HEADS, P])
    h_S = r("h_S", [P, B_HEADS, P])
    h_qg = r("h_qg", [P, B_HEADS, P])
    h_soft = r("h_soft", [P, 5, 2 * 4])
    h_vn = Region(h_kbe_at, END)("h_vn", [P, B_HEADS, P])
    r = Region(h_late, END)
    h_sq = r("h_sq", [P, 4, SEQ])
    h_rs = r("h_rs", [P, 4, SEQ])
    h_o = h_gb[:, :, :].rearrange("p a b -> p (a b)").rearrange("p (h t) -> p h t", h=B_HEADS)
    r = Region(h_pad_at, h_pad_end)
    h_rot = r("h_rot", [P, 5, SEQ])
    r = Region(h_pad_at, h_pad_end)
    h_p = r("h_p", [P, 4, 3 * P])
    h_pT = r("h_pT", [P, 4, 3 * P])
    X0 = X_AT
    r = Region(X0, X0 + 2 * KT * TB * 4)
    h_A = r("h_A", [P, PAIRS, P])
    h_AT = r("h_AT", [P, PAIRS, P])
    h_T = r("h_T", [P, PAIRS, P])
    h_TT = r("h_TT", [P, PAIRS, P])
    h_M = r("h_M", [P, PAIRS, P])
    h_Q = r("h_Q", [P, PAIRS, P])
    h_qkT = r("h_qkT", [P, PAIRS, P])
    h_u = r("h_u", [P, PAIRS, P])

    def pcol(name, i=0, n=1):
        return par[:, PCOL[name] + i:PCOL[name] + i + n]

    def hc(name, n=P, i=0):
        return h_const[:, HCOL[name] + i:HCOL[name] + i + n]

    def sc(name, n=P):
        return shared[:, SCOL[name]:SCOL[name] + n]

    ident = sc("ident")

    def bc(ap, n):
        return ap.unsqueeze(1).broadcast_to([P, n, ap.shape[1]])

    def bank(b, n=512):
        return psum[:, b, 0:n]

    def cells(b, n, w):
        return psum[:, b:b + (n * w + 511) // 512, :].rearrange("p b c -> p (b c)")[:, 0:n * w].rearrange("p (n w) -> p n w", w=w)

    def sem(name):
        return nc.alloc_semaphore(name)

    raw_loaded = [sem(f"raw_loaded{s}") for s in range(RAW_SLOTS)]
    rounding = sem("rounding")
    hi_ready, lo_ready, unit_done = sem("hi_ready"), sem("lo_ready"), sem("unit_done")
    drained = [sem(f"drained{b}") for b in range(BANKS)]
    mod_loaded = [sem(f"mod_loaded{s}") for s in range(MOD_SLOTS)]
    mod_used = sem("mod_used")
    x_loaded, par_loaded, hyb_loaded, ctx_loaded = sem("x_loaded"), sem("par_loaded"), sem("hyb_loaded"), sem("ctx_loaded")
    consts_set, split_hi, x_ready = sem("consts_set"), sem("split_hi"), sem("x_ready")
    pe_step, act_step, dve_step = sem("pe_step"), sem("act_step"), sem("dve_step")
    flags = {}

    def flag(name):
        if name not in flags:
            flags[name] = sem(name)
        return flags[name]

    class Link:

        def __init__(self, engine, step):
            self.engine, self.step, self.count = engine, step, 0

        def __call__(self, instruction):
            instruction.then_inc(self.step, 1)
            self.count += 1
            self.engine.wait_ge(self.step, self.count)

    HYB_TILES = 12


    def lo_split(dve, u, n=None):
        n = u if n is None else n
        dve.wait_ge(hi_ready, n + 1)
        nc.vector.tensor_tensor(lo_ring[:, u % SPLIT_SLOTS, :], raw_ring[:, u % RAW_SLOTS, :],
                                hi_ring[:, u % SPLIT_SLOTS, :].bitcast(F32), ALU.subtract).then_inc(lo_ready, 1)

    def next_lo(dve, u):
        if u + LEAD < UNITS:
            lo_split(dve, u + LEAD)

    def unit(pe, u, hi, lo, T, first=None, n=None, turn=None):
        n = u if n is None else n
        turn = u // BANKS if turn is None else turn
        pe.wait_ge(lo_ready, n + 1)
        if u >= BANKS:
            pe.wait_ge(drained[u % BANKS], turn)
        s = u % SPLIT_SLOTS
        for k in range(KT):
            if first:
                first(k)
            w_hi, w_lo = hi_ring[:, s, k * P:(k + 1) * P], lo_ring[:, s, k * P:(k + 1) * P]
            nc.tensor.matmul(bank(u % BANKS, T), w_hi, hi[:, k, 0:T], start=(k == 0), stop=False)
            nc.tensor.matmul(bank(u % BANKS, T), w_hi, lo[:, k, 0:T], start=False, stop=False)
            last = nc.tensor.matmul(bank(u % BANKS, T), w_lo, hi[:, k, 0:T], start=False, stop=(k == KT - 1))
        last.then_inc(unit_done, 1)

    def wait_unit(engine, u, n=None):
        engine.wait_ge(unit_done, (u if n is None else n) + 1)

    def wait_drained(engine, u, turn=None):
        engine.wait_ge(drained[u % BANKS], (u // BANKS if turn is None else turn) + 1)

    def mod_units(pe, first, count):
        for m in range(first, first + count):
            pe.wait_ge(mod_loaded[m % MOD_SLOTS], 16 * (m // MOD_SLOTS + 1))
            for k in range(KT):
                last = nc.tensor.matmul(psum[:, MODBANK, 2 * m:2 * m + 2], mod_ring[:, m % MOD_SLOTS, k * P:(k + 1) * P],
                                        silu_c[:, k, :], start=(k == 0), stop=(k == KT - 1))
            last.then_inc(mod_used, 1)

    BETA, ABS, EXP_ABS, NEG, S1, S2, POLY, RELU_A, G_STEP, EXP_A, G, EXP_G, TAIL, BETA_G, TMP, A_IN = range(16)

    def row(i, a=0, b=PAIRS):
        return h_small[:, i, a:b]

    def row2(i):
        return h_small[:, i, :].rearrange("p (t h) -> p t h", t=2)

    q_h, k_h, v_h = h_conv[:, 4:8, :], h_conv[:, 0:4, :], h_conv[:, 8:12, :]

    def pair_cols(tiles, p):
        t, h = divmod(p, B_HEADS)
        return tiles[:, h, t * P:(t + 1) * P]

    def hyb_pe(pe):
        pe.wait_ge(x_loaded, 16)
        pe.wait_ge(par_loaded, 16)
        for t in range(2):
            for k in range(KT):
                last = nc.tensor.matmul(psum[:, 4, 8 * t:8 * t + 8], x[:, k, t * P:(t + 1) * P], pcol("tail", 8 * k, 8),
                                        start=(k == 0), stop=(k == KT - 1))
        last.then_inc(flag("logits"), 1)
        for u in range(HYB_IN):
            unit(pe, u, x_hi, x_lo, SEQ, first=(lambda k: pe.wait_ge(x_ready, k + 1)) if u == 0 else None)
            if u == 3:
                pe.wait_ge(hyb_loaded, 16)
                pe.wait_ge(flag("g_ready"), 1)
                nc.tensor.matmul(psum[:, 4, 16:24], hc("tri"), row(G_STEP), start=True, stop=True).then_inc(flag("cumsum"), 1)
            if u == 8:
                pe.wait_ge(flag("gb_ready"), 1)
                pe.wait_ge(par_loaded, 32)
                for p in range(PAIRS):
                    last = nc.tensor.transpose(cells(5, PAIRS, P)[:, p, :], h_gb[:, p, :], ident)
                last.then_inc(flag("g_rows"), 1)
            if u in (12, 16):
                n = 1 if u == 12 else 2
                pe.wait_ge(flag("conv_squares"), 4 * n)
                pe.wait_ge(flag("banks56_read"), n)
                for i in range(4):
                    last = nc.tensor.matmul(cells(5, 4, SEQ)[:, i, :], ones[:, :], h_sq[:, i, :], start=True, stop=True)
                last.then_inc(flag("conv_sums"), 1)
            if u == 17:
                pe.wait_ge(flag("banks56_read"), 3)
                for i in range(5):
                    wait_drained(pe, 12 + i)
                    last = nc.tensor.matmul(cells(4, 5, SEQ)[:, i, :], hc("rot1"), h_qk[:, i, :], start=True, stop=True)
                last.then_inc(flag("rotated_halves"), 1)
        for u in range(HYB_IN - BANKS, HYB_IN):
            wait_drained(pe, u)
        for t in range(2):
            last = nc.tensor.transpose(cells(0, 2, P)[:, t, :], h_vT[:, t * P:(t + 1) * P], ident)
        last.then_inc(flag("v_rows"), 1)
        pe.wait_ge(flag("conv_silu"), 12)
        for p in range(PAIRS):
            last = nc.tensor.transpose(cells(1, PAIRS, P)[:, p, :], pair_cols(v_h, p), ident)
        last.then_inc(flag("v_tok"), 1)
        pe.wait_ge(flag("qk_rotated"), 1)
        pe.wait_ge(flag("conv_normed"), 1)
        for p in range(PAIRS):
            last = nc.tensor.transpose(cells(3, PAIRS, P)[:, p, :], pair_cols(k_h, p), ident)
        last.then_inc(flag("k_tok"), 1)
        for p in range(PAIRS):
            last = nc.tensor.matmul(cells(5, PAIRS, P)[:, p, :], pair_cols(k_h, p), pair_cols(k_h, p), start=True, stop=True)
        last.then_inc(flag("gram"), 1)
        pe.wait_ge(flag("vb_ready"), 1)
        pe.wait_ge(flag("conv_normed"), 2)
        for p in range(PAIRS):
            last = nc.tensor.matmul(cells(1, PAIRS, P)[:, p, :], pair_cols(q_h, p), pair_cols(k_h, p), start=True, stop=True)
        last.then_inc(flag("qk"), 1)
        pe.wait_ge(flag("A_ready"), 1)
        for p in range(PAIRS):
            last = nc.tensor.transpose(cells(5, PAIRS, P)[:, p, :], h_A[:, p, :], ident)
        last.then_inc(flag("AT_ps"), 1)
        pe.wait_ge(flag("qk_decayed"), 1)
        for p in range(PAIRS):
            last = nc.tensor.transpose(cells(3, PAIRS, P)[:, p, :], h_Q[:, p, :], ident)
        last.then_inc(flag("qkT_ps"), 1)
        pe.wait_ge(flag("qkT_ready"), 1)
        for level in range(1, len(DN_BLOCKS)):
            pe.wait_ge(flag("M_ready"), level)
            pe.wait_ge(flag("T_ready"), level)
            for p in range(PAIRS):
                last = nc.tensor.matmul(cells(0, PAIRS, P)[:, p, :], h_M[:, p, :], h_T[:, p, :], start=True, stop=True)
            last.then_inc(flag("MT_ps"), 1)
            pe.wait_ge(flag("MT_ready"), level)
            for p in range(PAIRS):
                nc.tensor.matmul(cells(2, PAIRS, P)[:, p, :], h_TT[:, p, :], h_Q[:, p, :], start=True, stop=True)
            for p in range(PAIRS):
                last = nc.tensor.matmul(cells(5, PAIRS, P)[:, p, :], h_Q[:, p, :], h_TT[:, p, :], start=True, stop=True)
            last.then_inc(flag("TMT_ps"), 1)
        pe.wait_ge(flag("T_ready"), len(DN_BLOCKS))
        for p in range(PAIRS):
            last = nc.tensor.matmul(cells(0, PAIRS, P)[:, p, :], h_TT[:, p, :], h_vb[:, p, :], start=True, stop=True)
        last.then_inc(flag("u_ps"), 1)
        for h in range(B_HEADS):
            last = nc.tensor.matmul(bank(2)[:, h * P:(h + 1) * P], h_kbe[:, h, :], h_TT[:, B_HEADS + h, :], start=True, stop=True)
        last.then_inc(flag("wT_ps"), 1)
        pe.wait_ge(flag("u_ready"), 1)
        for h in range(B_HEADS):
            last = nc.tensor.matmul(bank(3)[:, h * P:(h + 1) * P], h_ktail[:, h, :], h_u[:, h, :], start=True, stop=True)
        last.then_inc(flag("S_ps"), 1)
        pe.wait_ge(flag("wT_ready"), 1)
        pe.wait_ge(flag("S_ready"), 1)
        for h in range(B_HEADS):
            last = nc.tensor.matmul(bank(4)[:, h * P:(h + 1) * P], h_wT[:, h, :], h_S[:, h, :], start=True, stop=True)
        last.then_inc(flag("wS_ps"), 1)
        pe.wait_ge(flag("vn_ready"), 1)
        pe.wait_ge(flag("qg_ready"), 1)
        for h in range(B_HEADS):
            o = cells(5, B_HEADS, SEQ)[:, h, :]
            nc.tensor.matmul(o[:, 0:P], h_u[:, h, :], h_qkT[:, h, :], start=True, stop=True)
            nc.tensor.matmul(o[:, P:SEQ], h_S[:, h, :], h_qg[:, h, :], start=True, stop=False)
            last = nc.tensor.matmul(o[:, P:SEQ], h_vn[:, h, :], h_qkT[:, B_HEADS + h, :], start=False, stop=True)
        last.then_inc(flag("o_ps"), 1)
        pe.wait_ge(flag("o_squares"), 1)
        for h in range(B_HEADS):
            last = nc.tensor.matmul(cells(0, B_HEADS, SEQ)[:, h, :], ones[:, :], h_sq[:, h, :], start=True, stop=True)
        last.then_inc(flag("o_sums"), 1)
        pe.wait_ge(flag("silu_c"), 1)
        mod_units(pe, *MOD_AT["hyb"])
        for f in range(2):
            a = f * A_DH
            if f:
                pe.wait_ge(flag("a_pT_ready"), f)
            for t in range(4):
                nc.tensor.matmul(bank(2)[:, t * P:(t + 1) * P], h_qk[a:a + A_DH, t, 0:P], h_qk[a:a + A_DH, 4, 0:P],
                                 start=True, stop=True)
            for t in range(4):
                last = nc.tensor.matmul(cells(3, 4, SEQ)[:, t, :], h_qk[a:a + A_DH, t, P:SEQ], h_qk[a:a + A_DH, 4, :],
                                        start=True, stop=True)
            last.then_inc(flag("a_scores"), 1)
            pe.wait_ge(flag("a_probs"), f + 1)
            for j in range(12):
                last = nc.tensor.transpose(cells(2, 12, P)[:, j, :], h_p[:, j // 3, (j % 3) * P:(j % 3 + 1) * P], ident)
            last.then_inc(flag("a_pT_ps"), 1)
            pe.wait_ge(flag("a_pT_ready"), f + 1)
            pe.wait_ge(flag("v_rows_read"), 1)
            pe.wait_ge(flag("o_read"), 1)
            for t in range(4):
                h = f * 4 + t
                b = (h % 2) * A_DH
                o = psum[b:b + A_DH, 5 + h // 4, :].rearrange("p (n w) -> p n w", n=2)[:, (h // 2) % 2, :]
                v = [h_v[:, j, a:a + A_DH] for j in range(2)]
                nc.tensor.matmul(o[:, 0:P], v[0], h_pT[:, t, 0:P], start=True, stop=True)
                nc.tensor.matmul(o[:, P:SEQ], v[0], h_pT[:, t, P:2 * P], start=True, stop=False)
                last = nc.tensor.matmul(o[:, P:SEQ], v[1], h_pT[:, t, 2 * P:3 * P], start=False, stop=True)
            last.then_inc(flag("a_out_ps"), 1)
        for u in range(U_HOUT, U_HOUT + KT):
            unit(pe, u, x_hi, x_lo, SEQ, first=(lambda k: pe.wait_ge(flag("merged"), 2)) if u == U_HOUT else None)

    def hyb_act(act, link):
        act.wait_ge(consts_set, 1)
        act.wait_ge(par_loaded, 16)
        nc.scalar.activation(silu_c[:, :, :].rearrange("p k s -> p (k s)"), pcol("cond", 0, 2 * KT), ACT.Silu).then_inc(flag("silu_c"), 1)
        act.wait_ge(x_loaded, 16)
        for k in range(KT):
            nc.scalar.activation(x_hi[:, k, 0:SEQ], x[:, k, 0:SEQ], ACT.Copy).then_inc(split_hi, 1)
        nc.scalar.activation(row(EXP_A, 0, 4), pcol("a_log", 0, 4), ACT.Exp).then_inc(flag("exp_abs"), 1)

        def silu(i):
            act.wait_ge(flag("conv_done"), i + 1)
            nc.scalar.activation(h_conv[:, i, :], h_conv[:, i, :], ACT.Silu).then_inc(flag("conv_silu"), 1)
            if i < 8:
                act.wait_ge(flag("conv_silu"), i + 1)
                if i >= 4:
                    act.wait_ge(flag("conv_sums"), 1)
                nc.scalar.activation(h_sq[:, i % 4, :], h_conv[:, i, :], ACT.Square).then_inc(flag("conv_squares"), 1)

        def conv_rstd(n):
            act.wait_ge(flag("conv_sums"), n + 1)
            if n:
                act.wait_ge(flag("conv_normed"), n)
            link(nc.scalar.activation(h_rs[:, :, :].rearrange("p a b -> p (a b)"), psum[:, 5:7, :].rearrange("p a b -> p (a b)"),
                                      ACT.Ln, bias=eps[:, 1:2]))
            nc.scalar.activation(h_rs[:, :, :], h_rs[:, :, :], ACT.Exp, scale=-0.5).then_inc(flag("banks56_read"), 1)

        pending = []
        for u in range(HYB_IN):
            wait_unit(act, u)
            if u < HYB_TILES:
                nc.scalar.activation(h_pad[:, u, B_TAPS - 1:], bank(u % BANKS, SEQ), ACT.Copy).then_inc(drained[u % BANKS], 1)
                if 1 <= u <= 4:
                    silu(u - 1)
            elif u < 17:
                nc.scalar.activation(h_qk[:, u - 12, :], bank(u % BANKS, SEQ), ACT.Copy).then_inc(drained[u % BANKS], 1)
            elif u == 17:
                nc.scalar.activation(h_vT[:, :], bank(u % BANKS, SEQ), ACT.Copy).then_inc(drained[u % BANKS], 1)
            else:
                nc.scalar.activation(h_z[:, u - 18, :], bank(u % BANKS, SEQ), ACT.Silu).then_inc(drained[u % BANKS], 1)
            if u == 1:
                act.wait_ge(flag("abs_a"), 1)
                nc.scalar.activation(row(EXP_ABS), row(ABS), ACT.Exp).then_inc(flag("exp_abs"), 1)
                nc.scalar.activation(row2(BETA), h_lg[:, :, 0:4], ACT.Exp, scale=-1.0).then_inc(flag("exp_abs"), 1)
            if u == 6:
                act.wait_ge(flag("gb_ready"), 1)
                nc.scalar.activation(row(EXP_G), row(G), ACT.Exp).then_inc(flag("exp_g"), 1)
            if u == 10:
                act.wait_ge(flag("decay_in"), 1)
                nc.scalar.activation(h_decay[:, :, :], h_decay[:, :, :], ACT.Exp, scale=-1.0).then_inc(flag("exp_g"), 1)
                nc.scalar.activation(row(TAIL, 0, 4), row(TAIL, 0, 4), ACT.Exp).then_inc(flag("exp_g"), 1)
                nc.scalar.activation(h_expg[:, :, :], cells(5, PAIRS, P)[:, 4:8, :], ACT.Exp).then_inc(flag("banks56_read"), 1)
            if u == 13:
                conv_rstd(0)
                for i in range(4, 8):
                    silu(i)
            if u == 15:
                for i in range(8, 12):
                    silu(i)
            if u == 17:
                conv_rstd(1)
        act.wait_ge(flag("v_rows"), 1)
        nc.scalar.activation(h_v[:, :, :], cells(0, 2, P), ACT.Copy).then_inc(flag("v_rows_read"), 1)
        act.wait_ge(flag("AT_ps"), 1)
        nc.scalar.activation(h_AT[:, :, :], cells(5, PAIRS, P), ACT.Copy).then_inc(flag("AT_ready"), 1)
        act.wait_ge(flag("qkT_ps"), 1)
        nc.scalar.activation(h_qkT[:, :, :], cells(3, PAIRS, P), ACT.Copy).then_inc(flag("qkT_ready"), 1)
        for level in range(1, len(DN_BLOCKS)):
            act.wait_ge(flag("MT_ps"), level)
            nc.scalar.activation(h_Q[:, :, :], cells(0, PAIRS, P), ACT.Copy).then_inc(flag("MT_ready"), 1)
        act.wait_ge(flag("u_ps"), 1)
        nc.scalar.activation(h_u[:, :, :], cells(0, PAIRS, P), ACT.Copy).then_inc(flag("u_ready"), 1)
        act.wait_ge(flag("S_ps"), 1)
        nc.scalar.activation(h_S[:, :, :], cells(3, 4, P), ACT.Copy).then_inc(flag("S_ready"), 1)
        act.wait_ge(flag("o_ps"), 1)
        nc.scalar.activation(h_sq[:, :, :], cells(5, 4, SEQ), ACT.Square).then_inc(flag("o_squares"), 1)
        act.wait_ge(flag("o_sums"), 1)
        link(nc.scalar.activation(h_rs[:, :, :], cells(0, 4, SEQ), ACT.Ln, bias=eps[:, 1:2], scale=1.0 / P))
        nc.scalar.activation(h_rs[:, :, :], h_rs[:, :, :], ACT.Exp, scale=-0.5).then_inc(flag("o_rstd"), 1)
        for f in range(2):
            act.wait_ge(flag("a_max"), f + 1)
            for i in range(8):
                t, b = i % 4, i // 4
                part = h_p[:, t, 0:P] if b == 0 else h_p[:, t, P:3 * P]
                nc.scalar.activation(part, part, ACT.Exp, bias=h_soft[:, 1, i:i + 1],
                                     accum_out=h_soft[:, 2, i:i + 1]).then_inc(flag("a_exp"), 1)
            nc.scalar.activation(h_soft[:, 3, :], h_soft[:, 3, :], ACT.Exp).then_inc(flag("a_exp"), 1)
            act.wait_ge(flag("a_pT_ps"), f + 1)
            nc.scalar.activation(h_pT[:, :, :].rearrange("p t c -> p (t c)").rearrange("p (j c) -> p j c", c=P), cells(2, 12, P),
                                 ACT.Copy).then_inc(flag("a_pT_ready"), 1)
        act.wait_ge(flag("o_gated"), 1)
        nc.scalar.activation(x_hi[:, 4:8, 0:SEQ], h_o, ACT.Copy).then_inc(flag("merged_hi"), 1)
        act.wait_ge(flag("a_out_ps"), 2)
        nc.scalar.activation(x_hi[:, 0:4, 0:SEQ], cells(5, 4, SEQ), ACT.Copy).then_inc(flag("merged_hi"), 1)

    def hyb_dve(dve, link):
        link(nc.vector.memset(ones[:, :], 1.0))
        link(nc.vector.memset(eps[:, 0:1], LN_EPS))
        nc.vector.memset(eps[:, 1:2], EPS).then_inc(consts_set, 1)
        link(nc.vector.memset(h_pad[:, :, 0:B_TAPS - 1], 0.0))
        dve.wait_ge(x_loaded, 16)
        for u in range(LEAD):
            lo_split(dve, u)
        for k in range(KT):
            dve.wait_ge(split_hi, k + 1)
            nc.vector.tensor_tensor(x_lo[:, k, 0:SEQ], x[:, k, 0:SEQ], x_hi[:, k, 0:SEQ].bitcast(F32), ALU.subtract).then_inc(x_ready, 1)
        dve.wait_ge(par_loaded, 16)
        dve.wait_ge(flag("logits"), 1)
        link(nc.vector.tensor_copy(h_lg[:, :, :].rearrange("p t c -> p (t c)"), psum[:, 4, 0:16]))
        link(nc.vector.tensor_tensor(row2(A_IN), h_lg[:, :, 4:8], bc(pcol("dt_bias", 0, 4), 2), ALU.add))
        nc.vector.scalar_tensor_tensor(row(ABS), row(A_IN), -1.0, row(A_IN), ALU.mult, ALU.min).then_inc(flag("abs_a"), 1)

        def conv(i):
            wait_drained(dve, i)
            tap = lambda j: pcol("hyb_conv", i * B_TAPS + j)
            link(nc.vector.tensor_scalar(h_conv[:, i, :], h_pad[:, i, 0:SEQ], tap(0), None, ALU.mult))
            for j in range(1, B_TAPS):
                last = nc.vector.scalar_tensor_tensor(h_conv[:, i, :], h_pad[:, i, j:j + SEQ], tap(j), h_conv[:, i, :],
                                                      ALU.mult, ALU.add)
                if j < B_TAPS - 1:
                    link(last)
            last.then_inc(flag("conv_done"), 1)

        def log_decay():
            dve.wait_ge(flag("exp_abs"), 3)
            link(nc.vector.tensor_scalar(row(TMP), row(BETA), 1.0, None, ALU.add))
            link(nc.vector.reciprocal(row(BETA), row(TMP)))
            log1p_series(link, row(EXP_ABS), row(S1), row(S2), row(POLY))
            link(nc.vector.tensor_scalar(row(RELU_A), row(A_IN), 0.0, None, ALU.max))
            link(nc.vector.scalar_tensor_tensor(row(TMP), row(POLY), 2.0, row(RELU_A), ALU.mult, ALU.add))
            nc.vector.scalar_tensor_tensor(row2(G_STEP), row2(TMP), -1.0, bc(row(EXP_A, 0, 4), 2), ALU.mult,
                                           ALU.mult).then_inc(flag("g_ready"), 1)

        def normalise(n):
            dve.wait_ge(flag("banks56_read"), n + 2)
            part = q_h if n else k_h
            nc.vector.scalar_tensor_tensor(part, part, float(P) ** -0.5 if n else 1.0, h_rs[:, :, :], ALU.mult,
                                           ALU.mult).then_inc(flag("conv_normed"), 1)

        for u in range(HYB_IN):
            if u < HYB_TILES:
                conv(u)
            else:
                wait_unit(dve, u - 1)
            next_lo(dve, u)
            if u == 2:
                log_decay()
            if u == 4:
                dve.wait_ge(flag("cumsum"), 1)
                link(nc.vector.tensor_copy(row(G), psum[:, 4, 16:24]))
                for p in range(PAIRS):
                    last = nc.vector.tensor_scalar(h_gb[:, p, :], ones[:, :], row(G, p, p + 1), None, ALU.mult)
                last.then_inc(flag("gb_ready"), 1)
            if u == 9:
                dve.wait_ge(flag("g_rows"), 1)
                rows = cells(5, PAIRS, P)
                for p in range(PAIRS):
                    nc.vector.tensor_scalar(h_decay[:, p, :], rows[:, p, :], row(G, p, p + 1), 0.0, ALU.subtract, ALU.max)
                nc.vector.tensor_tensor(row(TAIL, 0, 4), rows[:, 0:4, P - 1], row(G, 0, 4), ALU.subtract).then_inc(flag("decay_in"), 1)
            if u == 11:
                dve.wait_ge(flag("exp_g"), 3)
                dve.wait_ge(hyb_loaded, 16)
                nc.vector.tensor_tensor(row(BETA_G), row(BETA), row(EXP_G), ALU.mult)
                link(nc.vector.tensor_tensor(h_decay[:, :, :], h_decay[:, :, :], bc(hc("incl"), PAIRS), ALU.mult))
            if u == 15:
                normalise(0)
            if u == 18:
                dve.wait_ge(flag("rotated_halves"), 1)
                normalise(1)
                link(nc.vector.tensor_tensor(h_rot[:, :, :], cells(4, 5, SEQ), bc(hc("sin1", SEQ), 5), ALU.mult))
                link(nc.vector.tensor_tensor(h_qk[:, :, :], h_qk[:, :, :], bc(hc("cos1", SEQ), 5), ALU.mult))
                nc.vector.tensor_tensor(h_qk[:, :, :], h_qk[:, :, :], h_rot[:, :, :], ALU.add).then_inc(flag("qk_rotated"), 1)
        dve.wait_ge(flag("v_tok"), 1)
        for p in range(PAIRS):
            last = nc.vector.tensor_scalar(h_vb[:, p, :], cells(1, PAIRS, P)[:, p, :], row(BETA, p, p + 1), None, ALU.mult)
        last.then_inc(flag("vb_ready"), 1)
        dve.wait_ge(flag("k_tok"), 1)
        for p in range(PAIRS):
            h = p % B_HEADS
            dst, by = (h_ktail[:, h, :], row(TAIL, h, h + 1)) if p < B_HEADS else (h_kbe[:, h, :], row(BETA_G, p, p + 1))
            nc.vector.tensor_scalar(dst, cells(3, PAIRS, P)[:, p, :], by, None, ALU.mult)
        dve.wait_ge(flag("gram"), 1)
        for p in range(PAIRS):
            last = nc.vector.scalar_tensor_tensor(h_A[:, p, :], cells(5, PAIRS, P)[:, p, :], row(BETA, p, p + 1),
                                                  h_decay[:, p, :], ALU.mult, ALU.mult)
        last.then_inc(flag("A_ready"), 1)
        dve.wait_ge(flag("qk"), 1)
        nc.vector.tensor_tensor(h_Q[:, :, :], cells(1, PAIRS, P), h_decay[:, :, :], ALU.mult).then_inc(flag("qk_decayed"), 1)
        nc.vector.tensor_tensor(h_qg[:, :, :], q_h[:, :, P:SEQ], h_expg[:, :, :], ALU.mult).then_inc(flag("qg_ready"), 1)
        dve.wait_ge(flag("A_ready"), 1)
        link(nc.vector.tensor_tensor(h_T[:, :, :], h_A[:, :, :], bc(hc("low1"), PAIRS), ALU.mult))
        link(nc.vector.tensor_tensor(h_T[:, :, :], bc(ident, PAIRS), h_T[:, :, :], ALU.subtract))
        dve.wait_ge(flag("AT_ready"), 1)
        link(nc.vector.tensor_tensor(h_TT[:, :, :], h_AT[:, :, :], bc(hc("up"), PAIRS), ALU.mult))
        nc.vector.tensor_tensor(h_TT[:, :, :], bc(ident, PAIRS), h_TT[:, :, :], ALU.subtract).then_inc(flag("T_ready"), 1)
        for level in range(1, len(DN_BLOCKS)):
            if level > 1:
                dve.wait_ge(flag("TMT_ps"), level - 1)
            nc.vector.tensor_tensor(h_M[:, :, :], h_AT[:, :, :], bc(hc("up", P, level * P), PAIRS), ALU.mult).then_inc(flag("M_ready"), 1)
            if level > 1:
                nc.vector.tensor_tensor(h_T[:, :, :], h_T[:, :, :], cells(2, PAIRS, P), ALU.subtract)
                nc.vector.tensor_tensor(h_TT[:, :, :], h_TT[:, :, :], cells(5, PAIRS, P), ALU.subtract).then_inc(flag("T_ready"), 1)
        dve.wait_ge(flag("TMT_ps"), len(DN_BLOCKS) - 1)
        nc.vector.tensor_tensor(h_TT[:, :, :], h_TT[:, :, :], cells(5, PAIRS, P), ALU.subtract).then_inc(flag("T_ready"), 1)
        dve.wait_ge(flag("wT_ps"), 1)
        nc.vector.tensor_copy(h_wT[:, :, :], cells(2, 4, P)).then_inc(flag("wT_ready"), 1)
        dve.wait_ge(flag("u_ready"), 1)
        dve.wait_ge(flag("wS_ps"), 1)
        nc.vector.tensor_tensor(h_vn[:, :, :], h_u[:, B_HEADS:, :], cells(4, 4, P), ALU.subtract).then_inc(flag("vn_ready"), 1)
        dve.wait_ge(flag("o_rstd"), 1)
        nc.vector.tensor_tensor(h_o, cells(5, 4, SEQ), h_rs[:, :, :], ALU.mult).then_inc(flag("o_read"), 1)
        dve.wait_ge(flag("o_read"), 1)
        wait_drained(dve, HYB_IN - 1)
        nc.vector.scalar_tensor_tensor(h_o, h_o, pcol("norm_w"), h_z[:, :, :], ALU.mult, ALU.mult).then_inc(flag("o_gated"), 1)
        for f in range(2):
            dve.wait_ge(flag("a_scores"), f + 1)
            sinks = pcol("sinks", 4 * f, 4)
            mask = hc("window", 2 * P)
            nc.vector.scalar_tensor_tensor(h_p[:, :, 0:P], cells(2, 4, P), A_DH ** -0.5, bc(mask[:, P:2 * P], 4), ALU.mult, ALU.add)
            link(nc.vector.scalar_tensor_tensor(h_p[:, :, P:3 * P], cells(3, 4, SEQ), A_DH ** -0.5, bc(mask, 4), ALU.mult, ALU.add))
            nc.vector.tensor_reduce(h_soft[:, 0, 0:4], h_p[:, :, 0:P], AX.X, ALU.max)
            link(nc.vector.tensor_reduce(h_soft[:, 0, 4:8], h_p[:, :, P:3 * P], AX.X, ALU.max))
            two = lambda i: h_soft[:, i, :].rearrange("p (b t) -> p b t", b=2)
            link(nc.vector.tensor_tensor(two(0), two(0), bc(sinks, 2), ALU.max))
            nc.vector.tensor_tensor(two(3), bc(sinks, 2), two(0), ALU.subtract)
            nc.vector.tensor_scalar(h_soft[:, 1, :], h_soft[:, 0, :], -1.0, None, ALU.mult).then_inc(flag("a_max"), 1)
            dve.wait_ge(flag("a_exp"), 9 * (f + 1))
            link(nc.vector.tensor_tensor(h_soft[:, 4, :], h_soft[:, 2, :], h_soft[:, 3, :], ALU.add))
            link(nc.vector.reciprocal(h_soft[:, 0, :], h_soft[:, 4, :]))
            for b, part in enumerate((h_p[:, :, 0:P], h_p[:, :, P:3 * P])):
                by = h_soft[:, 0, 4 * b:4 * b + 4].unsqueeze(2).broadcast_to([P, 4, part.shape[2]])
                last = nc.vector.tensor_tensor(part, part, by, ALU.mult)
            last.then_inc(flag("a_probs"), 1)
        dve.wait_ge(flag("merged_hi"), 1)
        nc.vector.tensor_tensor(x_lo[:, 4:8, 0:SEQ], h_o, x_hi[:, 4:8, 0:SEQ].bitcast(F32), ALU.subtract).then_inc(flag("merged"), 1)
        dve.wait_ge(flag("merged_hi"), 2)
        nc.vector.tensor_tensor(x_lo[:, 0:4, 0:SEQ], cells(5, 4, SEQ), x_hi[:, 0:4, 0:SEQ].bitcast(F32),
                                ALU.subtract).then_inc(flag("merged"), 1)
        for u in range(U_HOUT, U_HOUT + KT):
            k = u - U_HOUT
            wait_unit(dve, u)
            nc.vector.scalar_tensor_tensor(y[:, k, 0:SEQ], x[:, k, 0:SEQ], ALPHA, bank(u % BANKS, SEQ), ALU.mult,
                                           ALU.add).then_inc(drained[u % BANKS], 1)
            next_lo(dve, u)

    def log1p_series(link, e, s, s2, poly):
        link(nc.vector.tensor_scalar(s2, e, 2.0, None, ALU.add))
        link(nc.vector.reciprocal(s, s2))
        link(nc.vector.tensor_tensor(s, s, e, ALU.mult))
        link(nc.vector.tensor_tensor(s2, s, s, ALU.mult))
        link(nc.vector.tensor_scalar(poly, s2, 1.0 / 17, None, ALU.mult))
        for c in (15, 13, 11, 9, 7, 5, 3):
            link(nc.vector.scalar_tensor_tensor(poly, poly, 1.0 / c, s2, ALU.add, ALU.mult))
        link(nc.vector.scalar_tensor_tensor(poly, poly, 1.0, s, ALU.add, ALU.mult))

    def norm_pe(pe, n, T, mean=None):
        if mean:
            for k in range(KT):
                wait_drained(pe, mean[1] + k)
                last = nc.tensor.matmul(bank(4, T), ones[:, :], y[:, k, 0:T], start=(k == 0), stop=(k == KT - 1))
            last.then_inc(flag("mean_ps"), 1)
        for k in range(KT):
            pe.wait_ge(flag("norm_sq"), KT * n + k + 1)
            last = nc.tensor.matmul(bank(5, T), ones[:, :], sq[:, k, 0:T], start=(k == 0), stop=(k == KT - 1))
        last.then_inc(flag("norm_sum"), 1)

    def norm_rstd_act(act, link, n, T, e):
        act.wait_ge(flag("norm_sum"), n + 1)
        link(nc.scalar.activation(stat[:, 0:T], bank(5, T), ACT.Ln, bias=eps[:, e:e + 1], scale=1.0 / D))
        nc.scalar.activation(rstd[:, 0:T], stat[:, 0:T], ACT.Exp, scale=-0.5).then_inc(flag("norm_rstd"), 1)

    def squares_act(act, n, T, src, name, at):
        for k in range(KT):
            act.wait_ge(flag(name), at + k + 1)
            nc.scalar.activation(sq[:, k, 0:T], src[:, k, 0:T], ACT.Square).then_inc(flag("norm_sq"), 1)

    def split_act(act, s, T, src):
        for k in range(KT):
            act.wait_ge(flag("normed_f32"), KT * s + k + 1)
            nc.scalar.activation(x_hi[:, k, 0:T], src[:, k, 0:T], ACT.Copy).then_inc(split_hi, 1)

    def split_dve(dve, s, k, T, src):
        dve.wait_ge(split_hi, KT * (s + 1) + k + 1)
        nc.vector.tensor_tensor(x_lo[:, k, 0:T], src[:, k, 0:T], x_hi[:, k, 0:T].bitcast(F32), ALU.subtract).then_inc(x_ready, 1)

    def layer_norm_dve(dve, link, n, ln, g, b, s):
        T = SEQ
        dve.wait_ge(flag("mean_ps"), ln + 1)
        for k in range(KT):
            nc.vector.scalar_tensor_tensor(y[:, k, 0:T], bank(4, T), -1.0 / D, y[:, k, 0:T], ALU.mult, ALU.add).then_inc(flag("centered"), 1)
        dve.wait_ge(flag("norm_rstd"), n + 1)
        for k in range(KT):
            link(nc.vector.tensor_tensor(normed[:, k % 2, 0:T], y[:, k, 0:T], rstd[:, 0:T], ALU.mult))
            last = nc.vector.tensor_scalar(x[:, k, 0:T], normed[:, k % 2, 0:T], pcol(g, ln // 2 * KT + k), pcol(b, ln // 2 * KT + k),
                                           ALU.mult, ALU.add)
            if s is None:
                last.then_inc(flag("x_updated"), 1)
            else:
                last.then_inc(flag("normed_f32"), 1)
                if k:
                    split_dve(dve, s, k - 1, T, x)
        if s is not None:
            split_dve(dve, s, KT - 1, T, x)

    def streams(T):
        return [(i, slice(i * SEQ, (i + 1) * SEQ)) for i in range(T // SEQ)]

    def modulated_dve(dve, link, n, T, l, part, s):
        dve.wait_ge(flag("norm_rstd"), n + 1)
        for k in range(KT):
            link(nc.vector.tensor_tensor(normed[:, k % 2, 0:T], x[:, k, 0:T], rstd[:, 0:T], ALU.mult))
            for i, c in streams(T):
                last = nc.vector.tensor_scalar(y[:, k, c], normed[:, k % 2, c], coef[:, l, part + 1, k, i:i + 1],
                                               coef[:, l, part, k, i:i + 1], ALU.mult, ALU.add)
            last.then_inc(flag("normed_f32"), 1)
            if k:
                split_dve(dve, s, k - 1, T, y)
        split_dve(dve, s, KT - 1, T, y)

    def gated_dve(dve, link, n, T, l, part):
        dve.wait_ge(flag("norm_rstd"), n + 1)
        for k in range(KT):
            link(nc.vector.tensor_tensor(normed[:, k % 2, 0:T], y[:, k, 0:T], rstd[:, 0:T], ALU.mult))
            for i, c in streams(T):
                last = nc.vector.scalar_tensor_tensor(x[:, k, c], normed[:, k % 2, c], coef[:, l, part, k, i:i + 1], x[:, k, c],
                                                      ALU.mult, ALU.add)
            last.then_inc(flag("x_updated"), 1)

    def mlp_pe(pe, m, base, T, s):
        with pe.Fori(0, QUARTERS) as i:
            for j in range(KT):
                unit(pe, base + j, x_hi, x_lo, T, first=(lambda k: pe.wait_ge(x_ready, KT * (s + 1) + k + 1)) if j == 0 else None,
                     n=i * 16 + (base + j), turn=i * 4 + (base + j) // BANKS)
            for j in range(KT):
                u = base + KT + j
                unit(pe, u, hid_hi, hid_lo, T,
                     first=(lambda k: pe.wait_ge(flag("hidden_ready"), i * KT + (KT * QUARTERS * m + k + 1))) if j == 0 else None,
                     n=i * 16 + u, turn=i * 4 + u // BANKS)

    def mlp_act(act, m, base, T):
        with act.Fori(0, QUARTERS) as i:
            for j in range(KT):
                u = base + j
                turn = i * 4 + u // BANKS
                wait_unit(act, u, i * 16 + u)
                if j >= 2:
                    act.wait_ge(flag("hidden_ready"), i * KT + (KT * QUARTERS * m + j - 1))
                nc.scalar.activation(relu[:, j % 2, 0:T], bank(u % BANKS, T), ACT.Relu).then_inc(drained[u % BANKS], 1)
                wait_drained(act, u, turn)
                nc.scalar.activation(hid_hi[:, j, 0:T], relu[:, j % 2, 0:T], ACT.Square).then_inc(flag("hidden_hi"), 1)

    def mlp_dve(dve, m, base, T):
        with dve.Fori(0, QUARTERS) as i:
            for j in range(KT):
                u = base + j
                dve.wait_ge(flag("hidden_hi"), i * KT + (KT * QUARTERS * m + j + 1))
                nc.vector.tensor_tensor(relu2[:, j % 2, 0:T], relu[:, j % 2, 0:T], relu[:, j % 2, 0:T], ALU.mult).then_inc(flag("hidden_sq"), 1)
                dve.wait_ge(flag("hidden_sq"), i * KT + (KT * QUARTERS * m + j + 1))
                nc.vector.tensor_tensor(hid_lo[:, j, 0:T], relu2[:, j % 2, 0:T], hid_hi[:, j, 0:T].bitcast(F32),
                                        ALU.subtract).then_inc(flag("hidden_ready"), 1)
                lo_split(dve, u + LEAD, i * 16 + (u + LEAD))
            for j in range(KT):
                u = base + KT + j
                wait_unit(dve, u, i * 16 + u)
                nc.vector.tensor_tensor(y[:, j, 0:T], bank(u % BANKS, T), y[:, j, 0:T], ALU.add).then_inc(drained[u % BANKS], 1)
                lo_split(dve, u + LEAD, i * 16 + (u + LEAD))

    r = Region(M0, END)
    r_pad = r("r_pad", [P, KT, SEQ + B_TAPS - 1])
    r_x = r("r_x", [P, KT, SEQ])
    r_hi = r("r_hi", [P, KT, SEQ], F32R)
    r_lo = r("r_lo", [P, KT, SEQ], F32R)
    r_t = r("r_t", [P, KT, SEQ])
    r_i = r("r_i", [P, KT, SEQ])
    r_gate = r("r_gate", [P, KT, SEQ])
    r = Region(Y0, M0)
    r_s = r("r_s", [P, KT, SEQ])
    r_q = r("r_q", [P, KT, SEQ])
    r_lam = nc.alloc_sbuf_tensor_at("r_lam", [P, 6, KT], F32, offset=LAM_AT)

    def rec_pe(pe, s):
        for u in range(U_REC, U_REC + KT):
            unit(pe, u, x_hi, x_lo, SEQ, first=(lambda k: pe.wait_ge(x_ready, KT * (s + 1) + k + 1)) if u == U_REC else None)
        for b in range(GATES):
            u = U_GATES + b
            pe.wait_ge(lo_ready, u + 1)
            pe.wait_ge(drained[u % BANKS], u // BANKS)
            if b >= 2:
                pe.wait_ge(flag("gate_i_read"), b - 1)
            pe.wait_ge(flag("r_ready"), 2 * b + 2)
            for g, dst in enumerate((bank(u % BANKS), bank(4 + b % 2))):
                for m in range(2):
                    o = dst[:, m * SEQ:(m + 1) * SEQ]
                    for k in range(2):
                        c = (g * 4 + m * 2 + k) * P
                        w_hi, w_lo = hi_ring[:, u % SPLIT_SLOTS, c:c + P], lo_ring[:, u % SPLIT_SLOTS, c:c + P]
                        nc.tensor.matmul(o, w_hi, r_hi[:, 2 * b + k, :], start=(k == 0), stop=False)
                        nc.tensor.matmul(o, w_hi, r_lo[:, 2 * b + k, :], start=False, stop=False)
                        last = nc.tensor.matmul(o, w_lo, r_hi[:, 2 * b + k, :], start=False, stop=(k == 1))
            last.then_inc(unit_done, 1)
        for u in range(U_RGELU, U_RGELU + KT):
            unit(pe, u, x_hi, x_lo, SEQ)
        mod_units(pe, *MOD_AT["rec"])
        for u in range(U_ROUT, U_ROUT + KT):
            unit(pe, u, x_hi, x_lo, SEQ, first=(lambda k: pe.wait_ge(x_ready, KT * (s + 2) + k + 1)) if u == U_ROUT else None)

    def rec_act(act, link, s):
        act.wait_ge(flag("lam_abs"), 1)
        nc.scalar.activation(r_lam[:, 1, :], r_lam[:, 0, :], ACT.Exp).then_inc(flag("lam_exp"), 1)
        act.wait_ge(flag("pads_set"), 1)
        for k in range(KT + 1):
            if k < KT:
                u = U_REC + k
                wait_unit(act, u)
                nc.scalar.activation(r_pad[:, k, B_TAPS - 1:], bank(u % BANKS, SEQ), ACT.Copy).then_inc(drained[u % BANKS], 1)
            if k:
                act.wait_ge(flag("r_conv"), k)
                nc.scalar.activation(r_hi[:, k - 1, :], r_x[:, k - 1, :], ACT.Copy).then_inc(flag("r_hi_ready"), 1)
        for b in range(GATES):
            u = U_GATES + b
            wait_unit(act, u)
            for m in range(2):
                k = 2 * b + m
                last = nc.scalar.activation(r_t[:, k, :], bank(u % BANKS)[:, m * SEQ:(m + 1) * SEQ], ACT.Sigmoid, bias=pcol("b_a", k))
            last.then_inc(drained[u % BANKS], 1)
            for m in range(2):
                k = 2 * b + m
                last = nc.scalar.activation(r_i[:, k, :], bank(4 + b % 2)[:, m * SEQ:(m + 1) * SEQ], ACT.Sigmoid, bias=pcol("b_x", k))
            last.then_inc(flag("gate_i_read"), 1)
            act.wait_ge(flag("gate_i_read"), b + 1)
            act.wait_ge(flag("lam_ready"), 1)
            for m in range(2):
                k = 2 * b + m
                nc.scalar.activation(r_t[:, k, :], r_t[:, k, :], ACT.Tanh, scale=r_lam[:, 5, k:k + 1]).then_inc(flag("r_tanh"), 1)
        act.wait_ge(flag("r_tanh"), KT)
        for h in range(2):
            c = slice(4 * h, 4 * h + 4)
            nc.scalar.activation(r_s[:, c, :], r_t[:, c, :], ACT.Sqrt, scale=-1.0).then_inc(flag("r_sqrt"), 1)
        for k in range(KT):
            u = U_RGELU + k
            wait_unit(act, u)
            nc.scalar.activation(r_gate[:, k, :], bank(u % BANKS, SEQ), ACT.Gelu_apprx_tanh).then_inc(drained[u % BANKS], 1)
        split_act(act, s + 1, SEQ, r_q)

    def rec_dve(dve, link, s):
        nc.vector.memset(r_pad[:, :, 0:B_TAPS - 1], 0.0).then_inc(flag("pads_set"), 1)
        dve.wait_ge(flag("pads_set"), 1)
        lam = pcol("lam", 0, KT)
        nc.vector.scalar_tensor_tensor(r_lam[:, 0, :], lam, -1.0, lam, ALU.mult, ALU.min).then_inc(flag("lam_abs"), 1)
        dve.wait_ge(flag("lam_exp"), 1)
        log1p_series(link, r_lam[:, 1, :], r_lam[:, 2, :], r_lam[:, 3, :], r_lam[:, 4, :])
        link(nc.vector.tensor_scalar(r_lam[:, 0, :], lam, -1.0, 0.0, ALU.mult, ALU.max))
        link(nc.vector.scalar_tensor_tensor(r_lam[:, 2, :], r_lam[:, 4, :], 2.0, r_lam[:, 0, :], ALU.mult, ALU.add))
        nc.vector.tensor_scalar(r_lam[:, 5, :], r_lam[:, 2, :], -4.0, None, ALU.mult).then_inc(flag("lam_ready"), 1)

        def lo(k):
            dve.wait_ge(flag("r_hi_ready"), k + 1)
            nc.vector.tensor_tensor(r_lo[:, k, :], r_x[:, k, :], r_hi[:, k, :].bitcast(F32), ALU.subtract).then_inc(flag("r_ready"), 1)

        for k in range(KT):
            u = U_REC + k
            wait_drained(dve, u)
            tap = lambda j: pcol("rec_conv", k * B_TAPS + j)
            link(nc.vector.tensor_scalar(r_x[:, k, :], r_pad[:, k, 0:SEQ], tap(0), pcol("rec_conv_b", k), ALU.mult, ALU.add))
            for j in range(1, B_TAPS):
                last = nc.vector.scalar_tensor_tensor(r_x[:, k, :], r_pad[:, k, j:j + SEQ], tap(j), r_x[:, k, :], ALU.mult, ALU.add)
                if j < B_TAPS - 1:
                    link(last)
            last.then_inc(flag("r_conv"), 1)
            if k:
                lo(k - 1)
            next_lo(dve, u)
        lo(KT - 1)
        for b in range(GATES):
            next_lo(dve, U_GATES + b)
        for k in range(KT):
            dve.wait_ge(flag("r_tanh"), k + 1)
            link(nc.vector.tensor_scalar(r_q[:, k, :], r_t[:, k, :], -1.0, 1.0, ALU.mult, ALU.add))
            link(nc.vector.reciprocal(r_q[:, k, :], r_q[:, k, :]))
            link(nc.vector.tensor_tensor(r_i[:, k, :], r_i[:, k, :], r_x[:, k, :], ALU.mult))
            dve.wait_ge(flag("r_sqrt"), k // 4 + 1)
            link(nc.vector.scalar_tensor_tensor(r_s[:, k, :], r_s[:, k, :], 2.0, r_q[:, k, :], ALU.mult, ALU.mult))
            link(nc.vector.scalar_tensor_tensor(r_t[:, k, :], r_t[:, k, :], 1.0, r_q[:, k, :], ALU.add, ALU.mult))
            link(nc.vector.tensor_tensor(r_s[:, k, :], r_s[:, k, :], r_i[:, k, :], ALU.mult))
            link(nc.vector.tensor_tensor_scan(r_q[:, k, :], r_t[:, k, :], r_s[:, k, :], 0.0, ALU.mult, ALU.add))
            next_lo(dve, U_RGELU + k)
        for k in range(KT):
            wait_drained(dve, U_RGELU + k)
            nc.vector.tensor_tensor(r_q[:, k, :], r_q[:, k, :], r_gate[:, k, :], ALU.mult).then_inc(flag("normed_f32"), 1)
        for k in range(KT):
            if k == 0:
                wait_unit(dve, U_ROUT - 1)
            split_dve(dve, s + 1, k, SEQ, r_q)
        for k in range(KT):
            u = U_ROUT + k
            wait_unit(dve, u)
            nc.vector.scalar_tensor_tensor(y[:, k, 0:SEQ], x[:, k, 0:SEQ], ALPHA, bank(u % BANKS, SEQ), ALU.mult,
                                           ALU.add).then_inc(drained[u % BANKS], 1)
            next_lo(dve, u)

    PAD = CONF_K // 2
    r = Region(M0, END)
    c_conf = r("c_conf", [P, 2, TB])
    c_u_at = r.at
    c_u = r("c_u", [P, 2, 2, SEQ + 2 * PAD])
    c_sc = r("c_sc", [P, 2, TB])
    c_ch = r("c_ch", [P, 2, 2, SEQ + 2])
    c_b = r("c_b", [P, 2, TB])
    c_K = r("c_K", [P, HEADS, TB])
    c_Q_at = r.at
    c_Q = r("c_Q", [P, HEADS, TB])
    c_att_sq = Region(c_Q_at, END)("c_att_sq", [P, 4, TB])
    c_sq = Region(c_u_at, END)("c_sq", [P, 2, TB])
    r = Region(Y0, M0)
    c_kv = r("c_kv", [P, TB])
    c_kr = r("c_kr", [P, TB])
    c_q = r("c_q", [P, 2, TB])
    c_o = r("c_o", [P, 4, TB])
    r = Region(X0, X0 + 2 * KT * TB * 4)
    c_qh = r("c_qh", [P, 2, TB], F32R)
    c_ql = r("c_ql", [P, 2, TB], F32R)
    c_kh = r("c_kh", [P, TB], F32R)
    c_kl = r("c_kl", [P, TB], F32R)
    c_v = r("c_v", [P, 4, TB])
    c_p = r("c_p", [P, 2, TB])
    c_pT = r("c_pT", [P, 2, TB])
    c_stat = r("c_stat", [P, TB])
    c_rstd = r("c_rstd", [P, TB])
    c_soft = nc.alloc_sbuf_tensor_at("c_soft", [P, 4, 32], F32, offset=SOFT_AT)
    c_sq3 = Region(Y0 + 4 * TB * 4, M0)("c_sq3", [P, 3, TB])
    CONF_TAPS = [(i, j) for i in range(2) for j in range(CONF_K)]
    ORDER = ["g0", "g1", "a0", "a1", "c0", "c1", "h0", "h1", "b0", "b1", "kv", "kr", "q0", "q1"]

    class Layer:

        def __init__(self, l):
            self.l = l
            self.base = U_L2 + l * L2_UNITS
            self.T = TB if l == 0 else SEQ
            self.S = self.T // SEQ
            self.split = 4 + 3 * l
            self.norm = 4 + 4 * l
            self.updated = KT + 2 * KT * l
            self.items = [(st, h, b) for st in range(self.S) for h in range(HEADS) for b in range(2)]
            self.at = 0 if l == 0 else 2 * HEADS * 2
            self.pairs_at = 0 if l == 0 else HEADS
            self.jobs = 2 * HEADS + 4

        def width(self, name):
            return TB if name in ("kv", "kr") else self.T

    HOOKS = {2: "conf_mean", 4: "center", 6: "sums", 8: "rstd", 10: "silu", 12: "again", 14: "last"}

    def l2_pe(pe, L):
        l, T, S = L.l, L.T, L.S
        for j, name in enumerate(ORDER):
            unit(pe, L.base + j, x_hi, x_lo, L.width(name),
                 first=(lambda k: pe.wait_ge(x_ready, KT * (L.split + 1) + k + 1)) if j == 0 else None)
        pe.wait_ge(flag("kvq_sq"), 3 * l + 1)
        nc.tensor.matmul(bank(4, TB), ones[:, :], c_sq3[:, 0, :], start=True, stop=True).then_inc(flag("kv_sum"), 1)
        wait_drained(pe, L.base + ORDER.index("kr"))
        nc.tensor.matmul(psum[0:QK, 6, 0:SEQ], sc("rot2")[0:QK, 0:QK], c_kr[0:QK, 0:SEQ], start=True, stop=True).then_inc(flag("kr_rot"), 1)
        pe.wait_ge(flag("kvq_sq"), 3 * l + 3)
        nc.tensor.matmul(bank(5, T), ones[:, :], c_sq3[:, 1, 0:T], start=True, stop=False)
        nc.tensor.matmul(bank(5, T), ones[:, :], c_sq3[:, 2, 0:T], start=False, stop=True).then_inc(flag("q_sum"), 1)
        for u in range(L.base + L2_IN - BANKS, L.base + L2_IN):
            wait_drained(pe, u)
        job = L.jobs * l

        def place(j):
            if j >= job + BANKS:
                pe.wait_ge(flag("job_read"), j - BANKS + 1)
            return psum[:, j % BANKS, :]

        u = L.base + L2_IN
        s = u % SPLIT_SLOTS
        pe.wait_ge(lo_ready, u + 1)
        pe.wait_ge(flag("kv_split"), l + 1)
        for h in range(HEADS):
            o = place(job + h)[0:NOPE, 0:TB]
            w_hi, w_lo = (ring[:, s, h * NOPE:(h + 1) * NOPE] for ring in (hi_ring, lo_ring))
            nc.tensor.matmul(o, w_hi, c_kh[:, :], start=True, stop=False)
            nc.tensor.matmul(o, w_hi, c_kl[:, :], start=False, stop=False)
            nc.tensor.matmul(o, w_lo, c_kh[:, :], start=False, stop=True).then_inc(flag("job_done"), 1)
        for t in range(4):
            o = place(job + HEADS + t)
            c = slice(t * P, (t + 1) * P)
            w_hi, w_lo = (ring[:, s, 512:1024] for ring in (hi_ring, lo_ring))
            nc.tensor.matmul(o, c_kh[:, c], w_hi, start=True, stop=False)
            nc.tensor.matmul(o, c_kh[:, c], w_lo, start=False, stop=False)
            nc.tensor.matmul(o, c_kl[:, c], w_hi, start=False, stop=True).then_inc(unit_done if t == 3 else flag("job_done"), 1)
        for half in range(2):
            u = L.base + L2_IN + 1 + half
            s = u % SPLIT_SLOTS
            pe.wait_ge(lo_ready, u + 1)
            pe.wait_ge(flag("q_split"), 2 * l + 2)
            for h in range(4):
                o = place(job + HEADS + 4 + 4 * half + h)[0:QK, 0:T]
                for k in range(2):
                    c = (2 * h + k) * QK
                    w_hi, w_lo = hi_ring[:, s, c:c + QK], lo_ring[:, s, c:c + QK]
                    nc.tensor.matmul(o, w_hi, c_qh[:, k, 0:T], start=(k == 0), stop=False)
                    nc.tensor.matmul(o, w_hi, c_ql[:, k, 0:T], start=False, stop=False)
                    last = nc.tensor.matmul(o, w_lo, c_qh[:, k, 0:T], start=False, stop=(k == 1))
                last.then_inc(unit_done if h == 3 else flag("job_done"), 1)
        pe.wait_ge(flag("kr_rotated"), l + 1)
        for g in range(2):
            for h in range(4):
                pe.wait_ge(flag("job_read"), L.jobs * (l + 1) - HEADS + 4 * g + h + 1)
                last = nc.tensor.matmul(psum[0:QK, 4 + 2 * g + h // 2, (h % 2) * SEQ:(h % 2 + 1) * SEQ], sc("rot2")[0:QK, 0:QK],
                                        c_Q[0:QK, 4 * g + h, 0:SEQ], start=True, stop=True)
            last.then_inc(flag("q_rot"), 1)
        pe.wait_ge(flag("q_rotated"), 2 * l + 2)
        pe.wait_ge(flag("K_ready"), l + 1)

        def keys(st):
            return (0, 4) if st == 0 else (2, 2)

        def scores(i):
            st, h, b = L.items[i]
            first, n = keys(st)
            if i >= 2:
                pe.wait_ge(flag("p_exp"), L.at + i - 1)
            q = c_Q[0:QK, h, st * SEQ + b * P:st * SEQ + (b + 1) * P]
            nc.tensor.matmul(psum[:, i % 2, 0:n * P], q, c_K[0:QK, h, first * P:(first + n) * P], start=True,
                             stop=True).then_inc(flag("s_ps"), 1)

        def turned(i):
            st, h, b = L.items[i]
            pe.wait_ge(flag("p_ready"), L.at + i + 1)
            if i >= 2:
                pe.wait_ge(flag("pT_ready"), L.at + i - 1)
            for k in range(keys(st)[1]):
                last = nc.tensor.transpose(psum[:, 2 + i % 2, k * P:(k + 1) * P], c_p[:, i % 2, k * P:(k + 1) * P], ident)
            last.then_inc(flag("pT_ps"), 1)

        def out_of(i):
            st, h, b = L.items[i]
            first, n = keys(st)
            pair = i // 4
            if i % 4 == 0 and pair >= 2:
                pe.wait_ge(flag("o_pair_read"), L.pairs_at + pair - 1)
            pe.wait_ge(flag("pT_ready"), L.at + i + 1)
            r0 = (h % 2) * DV
            o = psum[r0:r0 + DV, 4 + pair % 2, b * P:(b + 1) * P]
            for k in range(n):
                last = nc.tensor.matmul(o, c_v[:, first + k, h * DV:(h + 1) * DV], c_pT[:, i % 2, k * P:(k + 1) * P],
                                        start=(k == 0), stop=(k == n - 1))
            last.then_inc(flag("o_item"), 1)

        def branch_pe(step):
            if step == "conf_mean":
                pe.wait_ge(flag("branches_done"), l + 1)
                for i in range(2):
                    last = nc.tensor.matmul(bank(6, T), ones[:, :], c_conf[:, i, 0:T], start=(i == 0), stop=(i == 1))
                last.then_inc(flag("conf_mean_ps"), 1)
            if step in ("sums", "again"):
                n = 3 * l + (1 if step == "sums" else 3)
                pe.wait_ge(flag("branch_sq"), n)
                for i in range(2):
                    last = nc.tensor.matmul(bank(6, T), ones[:, :], c_sq[:, i, 0:T], start=(i == 0), stop=(i == 1))
                last.then_inc(flag("branch_sum"), 1)
            if step == "rstd":
                pe.wait_ge(flag("branch_sq"), 3 * l + 2)
                for i in range(2):
                    last = nc.tensor.matmul(bank(7, T), ones[:, :], c_b[:, i, 0:T], start=(i == 0), stop=(i == 1))
                last.then_inc(flag("sc_sum"), 1)

        scores(0)
        scores(1)
        for i in range(len(L.items)):
            if i in HOOKS:
                branch_pe(HOOKS[i])
            turned(i)
            if i + 2 < len(L.items):
                scores(i + 2)
            if i:
                out_of(i - 1)
        out_of(len(L.items) - 1)
        for i in range(4):
            pe.wait_ge(flag("attn_sq"), 4 * l + i + 1)
            last = nc.tensor.matmul(bank(6, T), ones[:, :], c_att_sq[:, i, 0:T], start=(i == 0), stop=(i == 3))
        last.then_inc(flag("attn_sum"), 1)
        for k in range(KT):
            unit(pe, L.base + L2_IN + 3 + k, x_hi, x_lo, T,
                 first=(lambda q: pe.wait_ge(x_ready, KT * (L.split + 2) + q + 1)) if k == 0 else None)

    def l2_act(act, link, L):
        l, T, S = L.l, L.T, L.S
        for j, name in enumerate(ORDER):
            u = L.base + j
            i = int(name[1]) if name[1] in "01" else 0
            if name[0] in "ah":
                continue
            wait_unit(act, u)
            W = L.width(name)
            dst, f = {"g": (c_conf[:, i, 0:W], ACT.Sigmoid), "c": (c_sc[:, i, 0:W], ACT.Copy), "b": (c_b[:, i, 0:W], ACT.Copy),
                      "q": (c_q[:, i, 0:W], ACT.Copy), "k": ((c_kv if name == "kv" else c_kr)[:, 0:W], ACT.Copy)}[name[0]]
            if name in ("kv", "q0", "q1"):
                n = ("kv", "q0", "q1").index(name)
                nc.scalar.activation(c_sq3[:, n, 0:W], bank(u % BANKS, W), ACT.Square).then_inc(flag("kvq_sq"), 1)
            nc.scalar.activation(dst, bank(u % BANKS, W), f).then_inc(drained[u % BANKS], 1)
        act.wait_ge(flag("kv_sum"), l + 1)
        link(nc.scalar.activation(c_stat[:, 0:TB], bank(4, TB), ACT.Ln, bias=eps[:, 1:2], scale=1.0 / P))
        nc.scalar.activation(c_rstd[:, 0:TB], c_stat[:, 0:TB], ACT.Exp, scale=-0.5).then_inc(flag("kvq_rstd"), 1)
        act.wait_ge(flag("q_sum"), l + 1)
        link(nc.scalar.activation(stat[:, 0:T], bank(5, T), ACT.Ln, bias=eps[:, 1:2], scale=1.0 / (2 * P)))
        nc.scalar.activation(rstd[:, 0:T], stat[:, 0:T], ACT.Exp, scale=-0.5).then_inc(flag("kvq_rstd"), 1)
        act.wait_ge(flag("kvq_normed"), 3 * l + 1)
        nc.scalar.activation(c_kh[:, :], c_kv[:, :], ACT.Copy).then_inc(flag("kvq_hi"), 1)
        for k in range(2):
            act.wait_ge(flag("kvq_normed"), 3 * l + 2 + k)
            nc.scalar.activation(c_qh[:, k, 0:T], c_q[:, k, 0:T], ACT.Copy).then_inc(flag("kvq_hi"), 1)
        for j in range(L.jobs):
            ends = (HEADS + 3, HEADS + 7, HEADS + 11)
            if j in ends:
                wait_unit(act, L.base + L2_IN + ends.index(j))
            else:
                act.wait_ge(flag("job_done"), (L.jobs - 3) * l + j + 1 - sum(j > e for e in ends))
            src = psum[:, j % BANKS, :]
            if j < HEADS:
                args = c_K[0:NOPE, j, :], src[0:NOPE, 0:TB]
            elif j < HEADS + 4:
                args = c_v[:, j - HEADS, :], src
            else:
                args = c_Q[0:QK, j - HEADS - 4, 0:T], src[0:QK, 0:T]
            nc.scalar.activation(*args, ACT.Copy).then_inc(flag("job_read"), 1)
        act.wait_ge(flag("job_read"), L.jobs * (l + 1))
        for i in range(3):
            act.sem_inc(drained[(L.base + L2_IN + i) % BANKS], 1)

        def exp(i):
            st, h, b = L.items[i]
            n = 4 if st == 0 else 2
            act.wait_ge(flag("s_max"), L.at + i + 1)
            if i >= 2:
                act.wait_ge(flag("pT_ps"), L.at + i - 1)
            nc.scalar.activation(c_p[:, i % 2, 0:n * P], psum[:, i % 2, 0:n * P], ACT.Exp, bias=c_soft[:, 1, i:i + 1], scale=SM_SCALE,
                                 accum_out=c_soft[:, 2, i:i + 1]).then_inc(flag("p_exp"), 1)

        def branch_act(step):
            if step == "center":
                for i in range(2):
                    act.wait_ge(flag("conf_centered"), 2 * l + i + 1)
                    last = nc.scalar.activation(c_sq[:, i, 0:T], c_conf[:, i, 0:T], ACT.Square)
                last.then_inc(flag("branch_sq"), 1)
                act.wait_ge(flag("sc_done"), l + 1)
                nc.scalar.activation(c_b[:, :, 0:T], c_sc[:, :, 0:T], ACT.Square).then_inc(flag("branch_sq"), 1)
            if step in ("rstd", "last"):
                act.wait_ge(flag("branch_sum"), 2 * l + (1 if step == "rstd" else 2))
                link(nc.scalar.activation(stat[:, 0:T], bank(6, T), ACT.Ln, bias=eps[:, 1:2], scale=1.0 / (2 * P)))
                nc.scalar.activation(rstd[:, 0:T], stat[:, 0:T], ACT.Exp, scale=-0.5).then_inc(flag("branch_rstd"), 1)
            if step == "rstd":
                act.wait_ge(flag("sc_sum"), l + 1)
                link(nc.scalar.activation(c_stat[:, 0:T], bank(7, T), ACT.Ln, bias=eps[:, 1:2], scale=1.0 / (2 * P)))
                nc.scalar.activation(c_rstd[:, 0:T], c_stat[:, 0:T], ACT.Exp, scale=-0.5).then_inc(flag("sc_rstd"), 1)
            if step == "silu":
                for i in range(2):
                    act.wait_ge(flag("conf_scaled"), 2 * l + i + 1)
                    link(nc.scalar.activation(c_conf[:, i, 0:T], c_conf[:, i, 0:T], ACT.Silu, scale=pcol("conf_g", 2 * l + i),
                                              bias=pcol("conf_beta", 2 * l + i)))
                    last = nc.scalar.activation(c_sq[:, i, 0:T], c_conf[:, i, 0:T], ACT.Square)
                last.then_inc(flag("branch_sq"), 1)

        act.wait_ge(flag("q_rotated"), 2 * l + 2)
        exp(0)
        exp(1)
        for i in range(len(L.items)):
            if i in HOOKS:
                branch_act(HOOKS[i])
            n = 4 if L.items[i][0] == 0 else 2
            act.wait_ge(flag("pT_ps"), L.at + i + 1)
            if i >= 2:
                act.wait_ge(flag("o_item"), L.at + i - 1)
            nc.scalar.activation(c_pT[:, i % 2, 0:n * P], psum[:, 2 + i % 2, 0:n * P], ACT.Copy).then_inc(flag("pT_ready"), 1)
            if i + 2 < len(L.items):
                exp(i + 2)
        for i in range(4):
            act.wait_ge(flag("o_pair_read"), L.pairs_at + len(L.items) // 4)
            nc.scalar.activation(c_att_sq[:, i, 0:T], c_o[:, i, 0:T], ACT.Square).then_inc(flag("attn_sq"), 1)
        act.wait_ge(flag("attn_sum"), l + 1)
        link(nc.scalar.activation(stat[:, 0:T], bank(6, T), ACT.Ln, bias=eps[:, 1:2], scale=1.0 / (4 * P)))
        nc.scalar.activation(rstd[:, 0:T], stat[:, 0:T], ACT.Exp, scale=-0.5).then_inc(flag("attn_rstd"), 1)
        for k in range(KT):
            act.wait_ge(flag("normed_f32"), KT * (L.split + 1) + k + 1)
            nc.scalar.activation(x_hi[:, k, 0:T], merged(k, T), ACT.Copy).then_inc(split_hi, 1)
        for k in range(KT):
            u = L.base + L2_IN + 3 + k
            wait_unit(act, u)
            nc.scalar.activation(y[:, k, 0:T], bank(u % BANKS, T), ACT.Copy).then_inc(flag("y_ready"), 1)
            nc.scalar.activation(sq[:, k, 0:T], bank(u % BANKS, T), ACT.Square).then_inc(flag("norm_sq"), 1)
            act.wait_ge(flag("y_ready"), KT * l + k + 1)
            act.wait_ge(flag("norm_sq"), KT * (L.norm + 1) + k + 1)
            act.sem_inc(drained[u % BANKS], 1)

    def merged(k, T):
        return c_o[:, k, 0:T] if k < 4 else (c_conf[:, k - 4, 0:T] if k < 6 else c_sc[:, k - 6, 0:T])

    def l2_dve(dve, link, L):
        l, T, S = L.l, L.T, L.S
        link(nc.vector.memset(c_u[:, :, :, 0:PAD], 0.0))
        link(nc.vector.memset(c_u[:, :, :, PAD + SEQ:], 0.0))
        link(nc.vector.memset(c_ch[:, :, :, 0:1], 0.0))
        link(nc.vector.memset(c_ch[:, :, :, SEQ + 1:], 0.0))
        if l:
            dve.wait_ge(flag("norm_sum"), L.norm + 1)

        def split(ap):
            return ap.rearrange("p (s t) -> p s t", s=S)

        taps = []

        def conf_tap(i, j):
            acc, src = split(c_conf[:, i, 0:T]), c_u[:, i, 0:S, j:j + SEQ]
            w = pcol("conf_w", (2 * l + i) * CONF_K + j)
            if j == 0:
                return nc.vector.tensor_scalar(acc, src, w, pcol("conf_b", 2 * l + i), ALU.mult, ALU.add)
            return nc.vector.scalar_tensor_tensor(acc, src, w, acc, ALU.mult, ALU.add)

        def sc_tap(i, j):
            acc, src = split(c_sc[:, i, 0:T]), c_ch[:, i, 0:S, j:j + SEQ]
            w = pcol("sc_w", (2 * l + i) * SC_K + j)
            if j == 0:
                return nc.vector.tensor_scalar(acc, src, w, None, ALU.mult)
            return nc.vector.scalar_tensor_tensor(acc, src, w, acc, ALU.mult, ALU.add)

        def do_taps(n):
            for _ in range(min(n, len(taps))):
                f, i, j = taps.pop(0)
                link(f(i, j))

        for j, name in enumerate(ORDER):
            u = L.base + j
            i = int(name[1]) if name[1] in "01" else 0
            if name[0] in "ah":
                wait_drained(dve, u - 2)
                wait_unit(dve, u)
                src = split(bank(u % BANKS, T))
                if name[0] == "a":
                    nc.vector.tensor_tensor(c_u[:, i, 0:S, PAD:PAD + SEQ], src, split(c_conf[:, i, 0:T]),
                                            ALU.mult).then_inc(drained[u % BANKS], 1)
                    wait_drained(dve, u)
                    taps.extend((conf_tap, i, k) for k in range(CONF_K))
                else:
                    nc.vector.tensor_tensor(c_ch[:, i, 0:S, 1:1 + SEQ], src, split(c_sc[:, i, 0:T]),
                                            ALU.mult).then_inc(drained[u % BANKS], 1)
                    wait_drained(dve, u)
                    taps.extend((sc_tap, i, k) for k in range(SC_K))
            next_lo(dve, u)
            if j >= 3:
                do_taps(6)
        dve.wait_ge(flag("kvq_rstd"), 2 * l + 1)
        wait_drained(dve, L.base + ORDER.index("kv"))
        nc.vector.scalar_tensor_tensor(c_kv[:, :], c_kv[:, :], pcol("g_kv", l), c_rstd[:, :], ALU.mult, ALU.mult).then_inc(flag("kvq_normed"), 1)
        dve.wait_ge(flag("kvq_rstd"), 2 * l + 2)
        wait_drained(dve, L.base + ORDER.index("q1"))
        for k in range(2):
            nc.vector.scalar_tensor_tensor(c_q[:, k, 0:T], c_q[:, k, 0:T], pcol("g_q", 2 * l + k), rstd[:, 0:T], ALU.mult,
                                           ALU.mult).then_inc(flag("kvq_normed"), 1)
        dve.wait_ge(flag("kvq_hi"), 3 * l + 1)
        nc.vector.tensor_tensor(c_kl[:, :], c_kv[:, :], c_kh[:, :].bitcast(F32), ALU.subtract).then_inc(flag("kv_split"), 1)
        for k in range(2):
            dve.wait_ge(flag("kvq_hi"), 3 * l + 2 + k)
            nc.vector.tensor_tensor(c_ql[:, k, 0:T], c_q[:, k, 0:T], c_qh[:, k, 0:T].bitcast(F32), ALU.subtract).then_inc(flag("q_split"), 1)
        for i in range(3):
            next_lo(dve, L.base + L2_IN + i)
        R = slice(NOPE, QK)
        cos2, sin2 = sc("cos2", SEQ)[R, :], sc("sin2", SEQ)[R, :]
        dve.wait_ge(flag("kr_rot"), l + 1)
        rot = normed[R, 0, 0:SEQ]
        link(nc.vector.tensor_tensor(rot, psum[R, 6, 0:SEQ], sin2, ALU.mult))
        link(nc.vector.tensor_tensor(c_kr[R, 0:SEQ], c_kr[R, 0:SEQ], cos2, ALU.mult))
        nc.vector.tensor_tensor(c_kr[R, 0:SEQ], c_kr[R, 0:SEQ], rot, ALU.add).then_inc(flag("kr_rotated"), 1)
        dve.wait_ge(flag("kr_rotated"), l + 1)
        nc.vector.tensor_copy(c_K[R, :, :], c_kr[R, :].unsqueeze(1).broadcast_to([QK - NOPE, HEADS, TB])).then_inc(flag("K_ready"), 1)
        for g in range(2):
            dve.wait_ge(flag("q_rot"), 2 * l + g + 1)
            q = c_Q[R, 4 * g:4 * g + 4, 0:SEQ]
            turned = psum[R, 4 + 2 * g:6 + 2 * g, :].rearrange("p b c -> p (b c)").rearrange("p (h t) -> p h t", h=4)
            t = normed[R, :, :].rearrange("p a b -> p (a b)").rearrange("p (h t) -> p h t", h=4)
            four = lambda ap: ap.unsqueeze(1).broadcast_to([QK - NOPE, 4, SEQ])
            link(nc.vector.tensor_tensor(t, turned, four(sin2), ALU.mult))
            link(nc.vector.tensor_tensor(q, q, four(cos2), ALU.mult))
            link(nc.vector.tensor_tensor(q, q, t, ALU.add))
            dve.sem_inc(flag("q_rotated"), 1)
        do_taps(8)

        def top(i):
            st = L.items[i][0]
            n = 4 if st == 0 else 2
            dve.wait_ge(flag("s_ps"), L.at + i + 1)
            link(nc.vector.tensor_reduce(c_soft[:, 0, i:i + 1], psum[:, i % 2, 0:n * P], AX.X, ALU.max))
            nc.vector.tensor_scalar(c_soft[:, 1, i:i + 1], c_soft[:, 0, i:i + 1], -SM_SCALE, None, ALU.mult).then_inc(flag("s_max"), 1)

        def normalised(i):
            n = 4 if L.items[i][0] == 0 else 2
            dve.wait_ge(flag("p_exp"), L.at + i + 1)
            link(nc.vector.reciprocal(c_soft[:, 3, i:i + 1], c_soft[:, 2, i:i + 1]))
            nc.vector.tensor_scalar(c_p[:, i % 2, 0:n * P], c_p[:, i % 2, 0:n * P], c_soft[:, 3, i:i + 1], None,
                                    ALU.mult).then_inc(flag("p_ready"), 1)

        def pair_out(i):
            if i >= 0 and i % 4 == 3:
                st, h, _ = L.items[i]
                dve.wait_ge(flag("o_item"), L.at + i + 1)
                nc.vector.tensor_copy(c_o[:, h // 2, st * SEQ:(st + 1) * SEQ], bank(4 + (i // 4) % 2, SEQ)).then_inc(flag("o_pair_read"), 1)

        def branch_dve(step):
            if step == "conf_mean":
                while taps:
                    do_taps(8)
                dve.sem_inc(flag("branches_done"), 1)
            if step == "center":
                dve.wait_ge(flag("conf_mean_ps"), l + 1)
                for i in range(2):
                    nc.vector.scalar_tensor_tensor(c_conf[:, i, 0:T], bank(6, T), -1.0 / (2 * P), c_conf[:, i, 0:T], ALU.mult,
                                                   ALU.add).then_inc(flag("conf_centered"), 1)
                nc.vector.tensor_tensor(c_sc[:, :, 0:T], c_sc[:, :, 0:T], c_b[:, :, 0:T], ALU.mult).then_inc(flag("sc_done"), 1)
            if step == "silu":
                dve.wait_ge(flag("branch_rstd"), 2 * l + 1)
                for i in range(2):
                    nc.vector.tensor_tensor(c_conf[:, i, 0:T], c_conf[:, i, 0:T], rstd[:, 0:T], ALU.mult).then_inc(flag("conf_scaled"), 1)
                dve.wait_ge(flag("sc_rstd"), l + 1)
                for i in range(2):
                    nc.vector.scalar_tensor_tensor(c_sc[:, i, 0:T], c_sc[:, i, 0:T], pcol("g_branch", KT * l + 6 + i), c_rstd[:, 0:T],
                                                   ALU.mult, ALU.mult).then_inc(flag("branch_normed"), 1)
            if step == "last":
                dve.wait_ge(flag("branch_rstd"), 2 * l + 2)
                for i in range(2):
                    nc.vector.scalar_tensor_tensor(c_conf[:, i, 0:T], c_conf[:, i, 0:T], pcol("g_branch", KT * l + 4 + i), rstd[:, 0:T],
                                                   ALU.mult, ALU.mult).then_inc(flag("branch_normed"), 1)

        top(0)
        top(1)
        normalised(0)
        for i in range(len(L.items)):
            if i in HOOKS:
                branch_dve(HOOKS[i])
            if i + 2 < len(L.items):
                top(i + 2)
            if i + 1 < len(L.items):
                normalised(i + 1)
            pair_out(i - 1)
        pair_out(len(L.items) - 1)
        dve.wait_ge(flag("attn_rstd"), l + 1)
        for k in range(4):
            nc.vector.scalar_tensor_tensor(c_o[:, k, 0:T], c_o[:, k, 0:T], pcol("g_branch", KT * l + k), rstd[:, 0:T], ALU.mult,
                                           ALU.mult).then_inc(flag("normed_f32"), 1)
        for k in range(4):
            split_dve(dve, L.split + 1, k, T, c_o)
        dve.wait_ge(flag("branch_normed"), 4 * (l + 1))
        for k in range(4, KT):
            dve.sem_inc(flag("normed_f32"), 1)
        for k in range(4, KT):
            dve.wait_ge(split_hi, KT * (L.split + 2) + k + 1)
            nc.vector.tensor_tensor(x_lo[:, k, 0:T], merged(k, T), x_hi[:, k, 0:T].bitcast(F32), ALU.subtract).then_inc(x_ready, 1)
        for k in range(KT):
            u = L.base + L2_IN + 3 + k
            wait_unit(dve, u)
            next_lo(dve, u)

    def coef_dve(dve, link):
        dve.wait_ge(mod_used, MOD_UNITS)
        for l in range(DEPTH):
            n = N_MOD * KT
            c = coef[:, l].rearrange("p m k s -> p (m k) s")
            raw = psum[:, MODBANK, 2 * n * l:2 * n * (l + 1)].rearrange("p (m s) -> p m s", s=2)
            link(nc.vector.tensor_tensor(c, raw, pcol("b_mod", n * l, n).unsqueeze(2).broadcast_to([P, n, 2]), ALU.add))
            for part, g in ((1, "g_pre_mix"), (4, "g_pre_mlp")):
                gain = pcol(g, KT * l, KT).unsqueeze(2).broadcast_to([P, KT, 2])
                link(nc.vector.scalar_tensor_tensor(coef[:, l, part], coef[:, l, part], 1.0, gain, ALU.add, ALU.mult))
            for part, g in ((2, "g_post_mix"), (5, "g_post_mlp")):
                gain = pcol(g, KT * l, KT).unsqueeze(2).broadcast_to([P, KT, 2])
                link(nc.vector.tensor_tensor(coef[:, l, part], coef[:, l, part], gain, ALU.mult))

    LAYERS = [Layer(l) for l in range(DEPTH)]

    with nc.Block() as block:

        @block.sync
        def _(sp):
            for s in range(2):
                sp.dma_start(raw_ring[:, s, :], weights[s]).then_inc(raw_loaded[s], 16)
            sp.dma_start(x[:, :, 0:SEQ], xT_in).then_inc(x_loaded, 16)
            sp.dma_start(par[:, :], params_in).then_inc(par_loaded, 16)
            sp.wait_ge(par_loaded, 16)
            sp.dma_start(shared[:, :], shared_in).then_inc(par_loaded, 16)
            sp.dma_start(h_const[:, :], hyb_in).then_inc(hyb_loaded, 16)
            for s in range(2, RAW_SLOTS):
                sp.dma_start(raw_ring[:, s, :], weights[s]).then_inc(raw_loaded[s], 16)
            sp.dma_start(x[:, :, SEQ:TB], ctxT_in).then_inc(ctx_loaded, 16)

            def load(n, s, tail=None):
                sp.wait_ge(lo_ready, n - RAW_SLOTS + 1)
                src = weights[n] if isinstance(n, int) else weights[bass.ds(n, 1)].rearrange("o p c -> (o p) c")
                sp.dma_start(raw_ring[:, s, :], src).then_inc(raw_loaded[s], 16)

            def load_units(a, b):
                while a < b and a % RAW_SLOTS:
                    load(a, a % RAW_SLOTS)
                    a += 1
                full = (b - a) // RAW_SLOTS
                if full > 1:
                    with sp.Fori(0, full) as i:
                        for s in range(RAW_SLOTS):
                            load(i * RAW_SLOTS + (a + s), s)
                    a += full * RAW_SLOTS
                for n in range(a, b):
                    load(n, n % RAW_SLOTS)

            at = RAW_SLOTS
            for name, after in MOD_AFTER:
                upto = after + RAW_SLOTS + LEAD + 1
                load_units(at, upto)
                at = upto
                first, count = MOD_AT[name]
                for m in range(first, first + count):
                    if m >= MOD_SLOTS:
                        sp.wait_ge(mod_used, m - MOD_SLOTS + 1)
                    sp.dma_start(mod_ring[:, m % MOD_SLOTS, :], mod_weights[m]).then_inc(mod_loaded[m % MOD_SLOTS], 16)
            load_units(at, LOADED)
            sp.wait_ge(flag("x_updated"), KT + 4 * KT)
            sp.dma_start(out, x[:, :, 0:SEQ]).then_inc(flag("stored"), 16)
            sp.wait_ge(flag("stored"), 16)

        @block.gpsimd
        def _(pool):
            def round_unit(s, loaded):
                pool.wait_ge(raw_loaded[s], loaded)
                pool.sem_inc(rounding, 1)
                nc.gpsimd.tensor_scalar(hi_ring[:, s % SPLIT_SLOTS, :], raw_ring[:, s, :], 1.0, 0.0, ALU.mult, ALU.add).then_inc(hi_ready, 1)

            for s in range(RAW_SLOTS):
                if s >= SPLIT_SLOTS:
                    pool.wait_ge(unit_done, s - SPLIT_SLOTS + 1)
                round_unit(s, 16)
            with pool.Fori(1, LOADED // RAW_SLOTS) as i:
                for s in range(RAW_SLOTS):
                    pool.wait_ge(unit_done, i * RAW_SLOTS + (s - SPLIT_SLOTS + 1))
                    round_unit(s, i * 16 + 16)

        @block.scalar
        def _(act):
            link = Link(act, act_step)
            hyb_act(act, link)
            squares_act(act, 0, SEQ, y, "centered", 0)
            norm_rstd_act(act, link, 0, SEQ, 0)
            split_act(act, 0, SEQ, x)
            mlp_act(act, 0, U_MLP1, SEQ)
            squares_act(act, 1, SEQ, y, "centered", KT)
            norm_rstd_act(act, link, 1, SEQ, 0)
            split_act(act, 1, SEQ, x)
            rec_act(act, link, 1)
            squares_act(act, 2, SEQ, y, "centered", 2 * KT)
            norm_rstd_act(act, link, 2, SEQ, 0)
            split_act(act, 3, SEQ, x)
            mlp_act(act, 1, U_MLP2, SEQ)
            squares_act(act, 3, SEQ, y, "centered", 3 * KT)
            norm_rstd_act(act, link, 3, SEQ, 0)
            act.wait_ge(ctx_loaded, 16)
            for L in LAYERS:
                squares_act(act, L.norm, TB, x, "x_updated", L.updated - KT)
                norm_rstd_act(act, link, L.norm, TB, 1)
                split_act(act, L.split, TB, y)
                l2_act(act, link, L)
                norm_rstd_act(act, link, L.norm + 1, L.T, 1)
                squares_act(act, L.norm + 2, L.T, x, "x_updated", L.updated)
                norm_rstd_act(act, link, L.norm + 2, L.T, 1)
                split_act(act, L.split + 2, L.T, y)
                base = L.base + L2_IN + 3 + KT
                mlp_act(act, 2 + L.l, base, L.T)
                for k in range(KT):
                    wait_drained(act, base + MLP_UNITS - KT + k)
                    nc.scalar.activation(sq[:, k, 0:L.T], y[:, k, 0:L.T], ACT.Square).then_inc(flag("norm_sq"), 1)
                norm_rstd_act(act, link, L.norm + 3, L.T, 1)

        @block.vector
        def _(dve):
            link = Link(dve, dve_step)
            hyb_dve(dve, link)
            layer_norm_dve(dve, link, 0, 0, "ln1_g", "ln1_b", 0)
            link(nc.vector.tensor_scalar(y[:, :, 0:SEQ], x[:, :, 0:SEQ], ALPHA, None, ALU.mult))
            mlp_dve(dve, 0, U_MLP1, SEQ)
            layer_norm_dve(dve, link, 1, 1, "ln2_g", "ln2_b", 1)
            rec_dve(dve, link, 1)
            layer_norm_dve(dve, link, 2, 2, "ln1_g", "ln1_b", 3)
            link(nc.vector.tensor_scalar(y[:, :, 0:SEQ], x[:, :, 0:SEQ], ALPHA, None, ALU.mult))
            mlp_dve(dve, 1, U_MLP2, SEQ)
            layer_norm_dve(dve, link, 3, 3, "ln2_g", "ln2_b", None)
            coef_dve(dve, link)
            for L in LAYERS:
                modulated_dve(dve, link, L.norm, TB, L.l, 0, L.split)
                l2_dve(dve, link, L)
                gated_dve(dve, link, L.norm + 1, L.T, L.l, 2)
                modulated_dve(dve, link, L.norm + 2, L.T, L.l, 3, L.split + 2)
                dve.wait_ge(x_ready, KT * (L.split + 4))
                link(nc.vector.memset(y[:, :, 0:L.T], 0.0))
                mlp_dve(dve, 2 + L.l, L.base + L2_IN + 3 + KT, L.T)
                gated_dve(dve, link, L.norm + 3, L.T, L.l, 5)

        @block.tensor
        def _(pe):
            hyb_pe(pe)
            mod_units(pe, *MOD_AT["ln1"])
            norm_pe(pe, 0, SEQ, (0, U_HOUT))
            mlp_pe(pe, 0, U_MLP1, SEQ, 0)
            mod_units(pe, *MOD_AT["ln2"])
            norm_pe(pe, 1, SEQ, (1, U_REC - KT))
            rec_pe(pe, 1)
            mod_units(pe, *MOD_AT["ln3"])
            norm_pe(pe, 2, SEQ, (2, U_ROUT))
            mlp_pe(pe, 1, U_MLP2, SEQ, 3)
            mod_units(pe, *MOD_AT["ln4"])
            norm_pe(pe, 3, SEQ, (3, U_L2 - KT))
            for L in LAYERS:
                norm_pe(pe, L.norm, TB)
                l2_pe(pe, L)
                norm_pe(pe, L.norm + 1, L.T)
                norm_pe(pe, L.norm + 2, L.T)
                mlp_pe(pe, 2 + L.l, L.base + L2_IN + 3 + KT, L.T, L.split + 2)
                norm_pe(pe, L.norm + 3, L.T)


_MOD_PLAN = [("hyb", U_HOUT - 1, 56), ("ln1", U_MLP1 - 1, 8), ("ln2", U_REC - 1, 8), ("rec", U_ROUT - 1, 8),
             ("ln3", U_MLP2 - 1, 8), ("ln4", U_L2 - 1, 8)]
MOD_AFTER = [(_name, _after) for _name, _after, _ in _MOD_PLAN]
MOD_AT, _at = {}, 0
for _name, _, _count in _MOD_PLAN:
    MOD_AT[_name] = (_at, _count)
    _at += _count
assert _at == MOD_UNITS
LOADED = (UNITS + LEAD + RAW_SLOTS - 1) // RAW_SLOTS * RAW_SLOTS


def _tiles(v):
    return np.asarray(v).reshape(-1, P).T


def _unit(w, rows, cols):
    part = w[rows, :][:, cols]
    return part.reshape(-1, P, part.shape[1]).transpose(1, 0, 2).reshape(P, -1)


def _column_units(w, start, count, rows=slice(0, D)):
    return [_unit(w, rows, slice(start + P * m, start + P * (m + 1))) for m in range(count)]


def _mlp_stream(w1, w2):
    out = []
    for q in range(QUARTERS):
        out += _column_units(w1, q * D, KT)
        out += _column_units(w2, 0, KT, slice(q * D, (q + 1) * D))
    return out


def _weight_stream(i):
    w = i["hyb_w_in"][0]
    qa = 8 * A_DH
    kb, qb, vb, z = 1280, 768, 1792, 2304
    s = _column_units(w, kb, 4) + _column_units(w, qb, 4) + _column_units(w, vb, 4)
    for t in range(4):
        heads = np.concatenate([w[:, t * A_DH:(t + 1) * A_DH], w[:, (t + 4) * A_DH:(t + 5) * A_DH]], axis=1)
        s += _column_units(heads, 0, 1)
    s += _column_units(w, qa, 2) + _column_units(w, z, 4)
    s += _column_units(i["hyb_w_out"][0], 0, KT)
    s += _mlp_stream(i["mlp_w1"][0], i["mlp_w2"][0])
    s += _column_units(i["rec_w_in"][0], 0, KT)
    for b in range(GATES):
        s.append(np.concatenate([_unit(i[name][0, b], slice(0, 2 * P), slice(m * P, (m + 1) * P))
                                 for name in ("rec_w_a", "rec_w_x") for m in range(2)], axis=1))
    s += _column_units(i["rec_w_in"][0], D, KT)
    s += _column_units(i["rec_w_out"][0], 0, KT)
    s += _mlp_stream(i["mlp_w1"][1], i["mlp_w2"][1])
    for l in range(DEPTH):
        w = i["w_in_2"][l]
        conf, sc = 416, 928
        s += _column_units(w, conf + 256, 2) + _column_units(w, conf, 2)
        s += _column_units(w, sc + 256, 2) + _column_units(w, sc + 512, 2) + _column_units(w, sc, 2)
        s += _column_units(w, 256, 1)
        kr = np.zeros((D, P), np.float32)
        kr[:, NOPE:QK] = w[:, 384:416]
        s += _column_units(kr, 0, 1) + _column_units(w, 0, 2)
        kv = i["w_kv_b_2"][l].reshape(P, HEADS, NOPE + DV)
        s.append(np.concatenate([kv[:, :, :NOPE].reshape(P, -1), kv[:, :, NOPE:].reshape(P, -1)], axis=1))
        q = i["w_q_b_2"][l].reshape(2, P, HEADS, QK).transpose(1, 2, 0, 3)
        for half in range(2):
            part = np.zeros((P, D), np.float32)
            part[:, 0:8 * QK] = q[:, 4 * half:4 * half + 4].reshape(P, -1)
            s.append(part)
        s += _column_units(i["w_o_2"][l], 0, KT)
        s += _mlp_stream(i["w_mlp_in_2"][l], i["w_mlp_out_2"][l])
    assert len(s) == UNITS
    s += [np.zeros((P, D), np.float32)] * (LOADED - UNITS)
    return np.stack(s)


def _params(i):
    bc = lambda v: np.broadcast_to(np.asarray(v).reshape(1, -1), (P, np.size(v)))
    conv = lambda w, order: np.asarray(w).reshape(w.shape[0], -1, P)[:, order].transpose(2, 1, 0).reshape(P, -1)
    both = lambda name: np.concatenate([_tiles(i[name][l]) for l in range(DEPTH)], axis=1)
    n12 = [4, 5, 6, 7, 0, 1, 2, 3, 8, 9, 10, 11]
    p = {
        "hyb_conv": conv(i["hyb_conv_w"][0], n12), "norm_w": _tiles(i["hyb_norm_w"][0]), "sinks": bc(i["hyb_sinks"][0]),
        "a_log": bc(i["hyb_a_log"][0]), "dt_bias": bc(i["hyb_dt_bias"][0]),
        "rec_conv": conv(i["rec_conv_w"][0], list(range(KT))), "rec_conv_b": _tiles(i["rec_conv_b"][0]),
        "b_a": _tiles(i["rec_b_a"][0]), "b_x": _tiles(i["rec_b_x"][0]), "lam": _tiles(i["rec_lambda"][0]),
        "ln1_g": both("ln1_g"), "ln1_b": both("ln1_b"), "ln2_g": both("ln2_g"), "ln2_b": both("ln2_b"),
        "cond": np.stack([_tiles(i["c_2"][0]), _tiles(i["c_ctx_2"])], axis=2).reshape(P, -1),
        "b_mod": both("b_mod_2"), "g_pre_mix": both("g_pre_mix_2"), "g_post_mix": both("g_post_mix_2"),
        "g_pre_mlp": both("g_pre_mlp_2"), "g_post_mlp": both("g_post_mlp_2"), "g_q": both("g_q_2"), "g_kv": both("g_kv_2"),
        "conf_w": np.concatenate([conv(i["conf_dw_w_2"][l], [0, 1]) for l in range(DEPTH)], axis=1),
        "conf_b": both("conf_dw_b_2"), "conf_g": both("conf_ln_g_2"), "conf_beta": both("conf_ln_b_2"),
        "sc_w": np.concatenate([conv(i["sc_dw_w_2"][l], [0, 1]) for l in range(DEPTH)], axis=1),
        "g_branch": both("g_branch_2"),
        "tail": _unit(i["hyb_w_in"][0], slice(0, D), slice(2816, 2824)),
    }
    for name, width in _PARAM_WIDTHS:
        assert p[name].shape == (P, width), (name, p[name].shape, width)
    return np.ascontiguousarray(np.concatenate([p[name] for name, _ in _PARAM_WIDTHS], axis=1))


def _constants():
    f = np.float32
    a = np.arange(P)
    half = A_DH // 2
    inv = (f(10000.0) ** (-np.arange(half, dtype=f) / f(half))).astype(f)
    ang = np.arange(SEQ, dtype=f)[None, :] * inv[a % half][:, None]
    rot1 = np.zeros((P, P), f)
    for to in range(P):
        if to % A_DH < half:
            rot1[to + half, to] = -1
        else:
            rot1[to - half, to] = 1
    j, i = a[:, None], a[None, :]
    up = []
    for s in DN_BLOCKS:
        up.append(((j // (2 * s) == i // (2 * s)) & (j % (2 * s) < s) & (i % (2 * s) >= s)).astype(f))
    window = np.zeros((P, 2 * P), f)
    window[:, 0:P][~(i > j)] = -1e30
    window[:, P:][~(i <= j)] = -1e30
    hyb = {"rot1": rot1, "tri": (j <= i).astype(f), "incl": (i <= j).astype(f), "low1": up[0].T, "up": np.concatenate(up, axis=1),
           "cos1": np.cos(ang), "sin1": np.sin(ang), "window": window}
    axis = (QK - NOPE) // 2
    inv = (f(1.0) / (f(10000.0) ** (np.arange(0, axis, 2, dtype=f) / f(axis)))).astype(f)
    t = np.arange(SEQ)
    cos2, sin2, rot2 = np.ones((P, SEQ), f), np.zeros((P, SEQ), f), np.zeros((P, P), f)
    for d in range(QK - NOPE):
        pos = (t // 64 if d < axis else t % 64).astype(f)
        angle = (pos * inv[d % (axis // 2)]).astype(f)
        cos2[NOPE + d], sin2[NOPE + d] = np.cos(angle), np.sin(angle)
        if d % axis < axis // 2:
            rot2[NOPE + d + axis // 2, NOPE + d] = -1
        else:
            rot2[NOPE + d - axis // 2, NOPE + d] = 1
    shared = {"ident": np.eye(P, dtype=f), "rot2": rot2, "cos2": cos2, "sin2": sin2}
    pack = lambda d, widths: np.ascontiguousarray(np.concatenate([d[n] for n, _ in widths], axis=1).astype(f))
    return pack(shared, _SHARED), pack(hyb, _HYB)


def _features_first(a):
    return np.ascontiguousarray(a.T.reshape(KT, P, -1).transpose(1, 0, 2))


def layout(inputs):
    i = {name: np.asarray(v) for name, v in inputs.items()}
    shared, hyb = _constants()
    mod = np.stack([unit for l in range(DEPTH) for unit in _column_units(i["w_mod_2"][l], 0, N_MOD * KT)])
    return {"xT": _features_first(i["x"][0]), "ctxT": _features_first(i["ctx_2"][0]), "weights": _weight_stream(i),
            "mod_weights": mod, "params": _params(i), "shared_consts": shared, "hyb_consts": hyb}


def kernel(**inputs):
    import concourse.bacc as bacc
    from concourse.bass_utils import run_bass_kernel_spmd

    nc = bacc.Bacc("TRN2", target_bir_lowering=False, num_devices=1)
    arrays = layout(inputs)
    args = [nc.dram_tensor(name, a.shape, F32, kind="ExternalInput").ap() for name, a in arrays.items()]
    out = nc.dram_tensor("outT", (P, KT, SEQ), F32, kind="ExternalOutput").ap()
    program(nc, *args, out)
    result = run_bass_kernel_spmd(nc, [arrays], core_ids=[0]).results[0]["outT"]
    return np.asarray(result).transpose(1, 0, 2).reshape(D, SEQ).T.reshape(1, SEQ, D)
```

```python
import math

import numpy as np

import concourse.bass as bass
from concourse import mybir

F32 = mybir.dt.float32
F32R = mybir.dt.float32r
ALU = mybir.AluOpType
ACT = mybir.ActivationFunctionType
AX = mybir.AxisListType

P = 128
D = 1024
KT = D // P
SEQ = 256
CTX = 256
TB = SEQ + CTX
D_FF = 4096
DEPTH = 2
QUARTERS = D_FF // D
ALPHA = (2 * DEPTH) ** 0.25
LN_EPS = 1e-5
EPS = 1e-6

A_DH = 64
A_HEADS = 8
B_HEADS = 4
B_TAPS = 4
PAIRS = 2 * B_HEADS
DN_BLOCKS = [1, 2, 4, 8, 16, 32, 64]

HEADS = 8
QK = 96
NOPE = 64
DV = 64
SM_SCALE = 1.0 / math.sqrt(QK)
CONF_K = 31
SC_K = 3
N_MOD = 6

RAW_SLOTS = 8
SPLIT_SLOTS = 4
LEAD = SPLIT_SLOTS - 1
FIRST = 2
BANKS = 4
HYB_IN = 22
GATES = 4
L2_IN = 14
MLP_UNITS = 2 * KT * QUARTERS
MOD_UNITS = DEPTH * N_MOD * KT

_CHAIN = [("v_tok", 2), ("gram", 2), ("qk", 1), ("AT", 2)]
_CHAIN += [(f"{part}{level}", 1 if part == "MT" else 2) for level in range(1, 7) for part in ("MT", "TMT")]
_CHAIN += [("wT", 2), ("S", 1), ("wS", 2), ("o", 3), ("o_sums", 4), ("scores0", 3), ("probs0", 1), ("scores1", 3), ("probs1", 1),
           ("merge", 3)]
_NORM = lambda n: [(f"mean{n}", 2), (f"norm{n}", 4)]
_STREAM = [HYB_IN] + _CHAIN + [KT] + _NORM(0) + [MLP_UNITS] + _NORM(1) + [KT, GATES, ("gates", 4), KT, ("scan", 20), KT] + _NORM(2)
_STREAM += [MLP_UNITS] + _NORM(3)
_at, _starts, MOD_RANGE = 0, [], {}
for _item in _STREAM:
    _n = _item if isinstance(_item, int) else _item[1]
    if isinstance(_item, int):
        _starts.append(_at)
    else:
        MOD_RANGE[_item[0]] = range(_at, _at + _n)
    _at += _n
U_HYB, U_HOUT, U_MLP1, U_REC, U_GATES, U_RGELU, U_ROUT, U_MLP2 = _starts
U_L2 = _at
MOD_INDEX = {u: m for m, u in enumerate(u for r in MOD_RANGE.values() for u in r)}
assert len(MOD_INDEX) == MOD_UNITS, len(MOD_INDEX)
L2_UNITS = L2_IN + 3 + KT + MLP_UNITS
UNITS = U_L2 + DEPTH * L2_UNITS

_PARAM_WIDTHS = [
    ("hyb_conv", 12 * B_TAPS), ("norm_w", 1), ("sinks", A_HEADS), ("a_log", B_HEADS), ("dt_bias", B_HEADS),
    ("rec_conv", KT * B_TAPS), ("rec_conv_b", KT), ("b_a", KT), ("b_x", KT), ("lam", KT),
    ("ln1_g", 2 * KT), ("ln1_b", 2 * KT), ("ln2_g", 2 * KT), ("ln2_b", 2 * KT),
    ("cond", 2 * KT), ("b_mod", DEPTH * N_MOD * KT),
    ("g_pre_mix", 2 * KT), ("g_post_mix", 2 * KT), ("g_pre_mlp", 2 * KT), ("g_post_mlp", 2 * KT),
    ("g_q", 4), ("g_kv", 2), ("conf_w", DEPTH * 2 * CONF_K), ("conf_b", 4), ("conf_g", 4), ("conf_beta", 4),
    ("sc_w", DEPTH * 2 * SC_K), ("g_branch", 2 * KT), ("tail", KT * 8),
]
PCOL, _at = {}, 0
for _name, _width in _PARAM_WIDTHS:
    PCOL[_name] = _at
    _at += _width
N_PARAMS = _at

_SHARED = [("ident", P), ("rot2", P), ("cos2", SEQ), ("sin2", SEQ)]
_HYB = [("rot1", P), ("tri", P), ("incl", P), ("low1", P), ("up", 7 * P), ("cos1", SEQ), ("sin1", SEQ), ("window", 2 * P)]


def _columns(widths):
    at, out = 0, {}
    for name, width in widths:
        out[name] = at
        at += width
    return out, at


SCOL, N_SHARED = _columns(_SHARED)
HCOL, N_HYB = _columns(_HYB)


def program(nc, xT_in, ctxT_in, weights, params_in, shared_in, hyb_in, out):
    psum = nc.alloc_psum_tensor("psum", [P, 8, 512], F32)
    MODBANK = 7

    raw_ring = nc.alloc_sbuf_tensor("raw_ring", [P, RAW_SLOTS, D], F32)
    hi_ring = nc.alloc_sbuf_tensor("hi_ring", [P, SPLIT_SLOTS, D], F32R)
    lo_ring = nc.alloc_sbuf_tensor("lo_ring", [P, SPLIT_SLOTS, D], F32R)
    x = nc.alloc_sbuf_tensor("x", [P, KT, TB], F32)
    X_AT = (nc.sbuf_base + 31) // 32 * 32
    x_hi = nc.alloc_sbuf_tensor("x_hi", [P, KT, TB], F32R)
    x_lo = nc.alloc_sbuf_tensor("x_lo", [P, KT, TB], F32R)
    par = nc.alloc_sbuf_tensor("par", [P, N_PARAMS], F32)
    shared = nc.alloc_sbuf_tensor("shared", [P, N_SHARED], F32)
    ones = nc.alloc_sbuf_tensor("ones", [P, P], F32)
    eps = nc.alloc_sbuf_tensor("eps", [P, 2], F32)
    stat = nc.alloc_sbuf_tensor("stat", [P, TB], F32)
    rstd = nc.alloc_sbuf_tensor("rstd", [P, TB], F32)
    normed = nc.alloc_sbuf_tensor("normed", [P, 2, TB], F32)
    coef = nc.alloc_sbuf_tensor("coef", [P, DEPTH, N_MOD, KT, 2], F32)
    silu_c = nc.alloc_sbuf_tensor("silu_c", [P, KT, 2], F32)
    cond = nc.alloc_sbuf_tensor("cond", [P, KT, 4], F32R)
    mod_rows = nc.alloc_sbuf_tensor("mod_rows", [P, 2 * P], F32)
    mod_sums = nc.alloc_sbuf_tensor("mod_sums", [P, MOD_UNITS * 4], F32)
    LAM_AT = (nc.sbuf_base + 31) // 32 * 32
    nc.alloc_sbuf_tensor("lam_place", [P, 6, KT], F32)
    SOFT_AT = (nc.sbuf_base + 31) // 32 * 32
    nc.alloc_sbuf_tensor("soft_place", [P, 4, 32], F32)
    Y0 = (nc.sbuf_base + 63) // 64 * 64
    Y_BYTES = KT * TB * 4
    M0 = Y0 + Y_BYTES
    END = nc.sbuf_usable_end

    class Region:

        def __init__(self, start, end):
            self.at, self.end = start, end

        def __call__(self, name, shape, dtype=F32):
            n = 4 * int(np.prod(shape[1:]))
            t = nc.alloc_sbuf_tensor_at(name, shape, dtype, offset=self.at)
            self.at += (n + 31) // 32 * 32
            assert self.at <= self.end, (name, self.at, self.end)
            return t

    y = Region(Y0, M0)("y", [P, KT, TB])
    r = Region(M0, END)
    hid_hi = r("hid_hi", [P, KT, TB], F32R)
    hid_lo = r("hid_lo", [P, KT, TB], F32R)
    relu = r("relu", [P, 2, TB])
    relu2 = r("relu2", [P, 2, TB])
    sq = r("sq", [P, KT, TB])

    h_conv = Region(Y0, M0)("h_conv", [P, 12, SEQ])
    r = Region(M0, END)
    h_const = r("h_const", [P, N_HYB])
    h_pad_at = r.at
    h_pad = r("h_pad", [P, 12, SEQ + B_TAPS - 1])
    h_pad_end = r.at
    h_qk = r("h_qk", [P, 5, SEQ])
    h_vT = r("h_vT", [P, SEQ])
    h_v = r("h_v", [P, 2, P])
    h_z = r("h_z", [P, B_HEADS, SEQ])
    h_lg = r("h_lg", [P, 2, 8])
    h_small = r("h_small", [P, 16, PAIRS])
    h_decay = r("h_decay", [P, PAIRS, P])
    h_expg = r("h_expg", [P, B_HEADS, P])
    h_gb = r("h_gb", [P, PAIRS, P])
    h_late = r.at
    h_vb = r("h_vb", [P, PAIRS, P])
    h_kbe_at = r.at
    h_kbe = r("h_kbe", [P, B_HEADS, P])
    h_ktail = r("h_ktail", [P, B_HEADS, P])
    h_wT = r("h_wT", [P, B_HEADS, P])
    h_S = r("h_S", [P, B_HEADS, P])
    h_qg = r("h_qg", [P, B_HEADS, P])
    h_soft = r("h_soft", [P, 5, 2 * 4])
    h_vn = Region(h_kbe_at, END)("h_vn", [P, B_HEADS, P])
    r = Region(h_late, END)
    h_sq = r("h_sq", [P, 4, SEQ])
    h_rs = r("h_rs", [P, 4, SEQ])
    h_o = h_gb[:, :, :].rearrange("p a b -> p (a b)").rearrange("p (h t) -> p h t", h=B_HEADS)
    r = Region(h_pad_at, h_pad_end)
    h_rot = r("h_rot", [P, 5, SEQ])
    r = Region(h_pad_at, h_pad_end)
    h_p = r("h_p", [P, 4, 3 * P])
    h_pT = r("h_pT", [P, 4, 3 * P])
    X0 = X_AT
    r = Region(X0, X0 + 2 * KT * TB * 4)
    h_A = r("h_A", [P, PAIRS, P])
    h_AT = r("h_AT", [P, PAIRS, P])
    h_T = r("h_T", [P, PAIRS, P])
    h_TT = r("h_TT", [P, PAIRS, P])
    h_M = r("h_M", [P, PAIRS, P])
    h_Q = r("h_Q", [P, PAIRS, P])
    h_qkT = r("h_qkT", [P, PAIRS, P])
    h_u = r("h_u", [P, PAIRS, P])

    def pcol(name, i=0, n=1):
        return par[:, PCOL[name] + i:PCOL[name] + i + n]

    def hc(name, n=P, i=0):
        return h_const[:, HCOL[name] + i:HCOL[name] + i + n]

    def sc(name, n=P):
        return shared[:, SCOL[name]:SCOL[name] + n]

    ident = sc("ident")

    def bc(ap, n):
        return ap.unsqueeze(1).broadcast_to([P, n, ap.shape[1]])

    def bank(b, n=512):
        return psum[:, b, 0:n]

    def cells(b, n, w):
        return psum[:, b:b + (n * w + 511) // 512, :].rearrange("p b c -> p (b c)")[:, 0:n * w].rearrange("p (n w) -> p n w", w=w)

    def sem(name):
        return nc.alloc_semaphore(name)

    raw_loaded = [sem(f"raw_loaded{s}") for s in range(RAW_SLOTS)]
    rounding = sem("rounding")
    hi_ready, lo_ready, unit_done = sem("hi_ready"), sem("lo_ready"), sem("unit_done")
    drained = [sem(f"drained{b}") for b in range(BANKS)]
    x_loaded, shared_loaded, par_loaded, hyb_loaded, ctx_loaded = sem("x_loaded"), sem("shared_loaded"), sem("par_loaded"), sem("hyb_loaded"), sem("ctx_loaded")
    consts_set, split_hi, x_ready = sem("consts_set"), sem("split_hi"), sem("x_ready")
    pe_step, act_step, dve_step = sem("pe_step"), sem("act_step"), sem("dve_step")
    flags = {}

    def flag(name):
        if name not in flags:
            flags[name] = sem(name)
        return flags[name]

    class Link:

        def __init__(self, engine, step):
            self.engine, self.step, self.count = engine, step, 0

        def __call__(self, instruction):
            instruction.then_inc(self.step, 1)
            self.count += 1
            self.engine.wait_ge(self.step, self.count)

    now = {"exp": False}

    def exp_set():
        if not now["exp"]:
            nc.scalar.preload_act_table_set("natural_log_exp_and_others")
            now["exp"] = True

    def other_set():
        now["exp"] = False

    HYB_TILES = 12


    def lo_split(dve, u, n=None):
        n = u if n is None else n
        dve.wait_ge(hi_ready, n + 1)
        nc.vector.tensor_tensor(lo_ring[:, u % SPLIT_SLOTS, :], raw_ring[:, u % RAW_SLOTS, :],
                                hi_ring[:, u % SPLIT_SLOTS, :].bitcast(F32), ALU.subtract).then_inc(lo_ready, 1)

    def next_lo(dve, u):
        if u + LEAD < UNITS:
            lo_split(dve, u + LEAD)

    def unit(pe, u, hi, lo, T, first=None, n=None, turn=None):
        n = u if n is None else n
        turn = u // BANKS if turn is None else turn
        pe.wait_ge(lo_ready, n + 1)
        if u >= BANKS:
            pe.wait_ge(drained[u % BANKS], turn)
        s = u % SPLIT_SLOTS
        for k in range(KT):
            if first:
                first(k)
            w_hi, w_lo = hi_ring[:, s, k * P:(k + 1) * P], lo_ring[:, s, k * P:(k + 1) * P]
            nc.tensor.matmul(bank(u % BANKS, T), w_hi, hi[:, k, 0:T], start=(k == 0), stop=False)
            nc.tensor.matmul(bank(u % BANKS, T), w_hi, lo[:, k, 0:T], start=False, stop=False)
            last = nc.tensor.matmul(bank(u % BANKS, T), w_lo, hi[:, k, 0:T], start=False, stop=(k == KT - 1))
        last.then_inc(unit_done, 1)

    def first_units(pe, u, hi, lo, T, first, n=None, turn=lambda u: u // BANKS):
        n = u if n is None else n
        pe.wait_ge(lo_ready, n + FIRST)
        for v in range(u, u + FIRST):
            pe.wait_ge(drained[v % BANKS], turn(v))
        for k in range(KT):
            first(k)
            for v in range(u, u + FIRST):
                s = v % SPLIT_SLOTS
                w_hi, w_lo = hi_ring[:, s, k * P:(k + 1) * P], lo_ring[:, s, k * P:(k + 1) * P]
                nc.tensor.matmul(bank(v % BANKS, T), w_hi, hi[:, k, 0:T], start=(k == 0), stop=False)
                nc.tensor.matmul(bank(v % BANKS, T), w_hi, lo[:, k, 0:T], start=False, stop=False)
                last = nc.tensor.matmul(bank(v % BANKS, T), w_lo, hi[:, k, 0:T], start=False, stop=(k == KT - 1))
                if k == KT - 1:
                    last.then_inc(unit_done, 1)

    def wait_unit(engine, u, n=None):
        engine.wait_ge(unit_done, (u if n is None else n) + 1)

    def wait_drained(engine, u, turn=None):
        engine.wait_ge(drained[u % BANKS], (u // BANKS if turn is None else turn) + 1)

    def turn_group(pe, g):
        pe.wait_ge(flag("rows_read"), g + 1)
        if g:
            pe.wait_ge(flag("group_copied"), g)
        for j in range(2):
            c = 256 + 8 * (g % 4) + 4 * j
            last = nc.tensor.transpose(psum[:, MODBANK, c:c + 4], mod_rows[0:4, j * P:(j + 1) * P], ident[0:4, 0:4])
        last.then_inc(flag("group_turned"), 1)

    def mods(pe, place):
        for u in MOD_RANGE[place]:
            g, half = divmod(MOD_INDEX[u], 2)
            pe.wait_ge(lo_ready, u + 1)
            pe.wait_ge(drained[u % BANKS], u // BANKS)
            if half == 0 and g:
                pe.wait_ge(flag("rows_read"), g)
                if g >= 2:
                    pe.wait_ge(flag("group_copied"), g - 1)
            for k in range(4):
                q = 4 * half + k
                w_hi, w_lo = (ring[:, u % SPLIT_SLOTS, 2 * k * P:2 * (k + 1) * P] for ring in (hi_ring, lo_ring))
                nc.tensor.matmul(psum[0:4, MODBANK, 0:2 * P], cond[:, q, 0:4], w_hi, start=(q == 0), stop=False)
                last = nc.tensor.matmul(psum[0:2, MODBANK, 0:2 * P], cond[:, q, 0:2], w_lo, start=False,
                                        stop=(q == KT - 1))
            last.then_inc(unit_done, 1)
            pe.sem_inc(drained[u % BANKS], 1)
            if half and g:
                turn_group(pe, g - 1)

    def copy_group(dve, g):
        dve.wait_ge(flag("group_turned"), g + 1)
        c = 256 + 8 * (g % 4)
        nc.vector.tensor_copy(mod_sums[:, 8 * g:8 * g + 8], psum[:, MODBANK, c:c + 8]).then_inc(flag("group_copied"), 1)

    def pass_mod(dve, u):
        g, half = divmod(MOD_INDEX[u], 2)
        if half:
            wait_unit(dve, u)
            if g:
                dve.wait_ge(flag("group_turned"), g)
            nc.vector.tensor_copy(mod_rows[0:4, :], psum[0:4, MODBANK, 0:2 * P]).then_inc(flag("rows_read"), 1)
            if g:
                copy_group(dve, g - 1)
        next_lo(dve, u)

    def next_mods(dve, place):
        for u in MOD_RANGE[place]:
            pass_mod(dve, u)

    BETA, ABS, EXP_ABS, NEG, S1, S2, POLY, RELU_A, G_STEP, EXP_A, G, EXP_G, TAIL, BETA_G, TMP, A_IN = range(16)

    def row(i, a=0, b=PAIRS):
        return h_small[:, i, a:b]

    def row2(i):
        return h_small[:, i, :].rearrange("p (t h) -> p t h", t=2)

    HALVES = [range(0, PAIRS // 2), range(PAIRS // 2, PAIRS)]
    LEVELS = len(DN_BLOCKS) - 1

    q_h, k_h, v_h = h_conv[:, 4:8, :], h_conv[:, 0:4, :], h_conv[:, 8:12, :]

    def pair_cols(tiles, p):
        t, h = divmod(p, B_HEADS)
        return tiles[:, h, t * P:(t + 1) * P]

    def hyb_pe(pe):
        pe.wait_ge(x_loaded, 16)
        pe.wait_ge(par_loaded, 16)
        for t in range(2):
            for k in range(KT):
                last = nc.tensor.matmul(psum[:, 4, 8 * t:8 * t + 8], x[:, k, t * P:(t + 1) * P], pcol("tail", 8 * k, 8),
                                        start=(k == 0), stop=(k == KT - 1))
        last.then_inc(flag("logits"), 1)
        for u in range(HYB_IN):
            unit(pe, u, x_hi, x_lo, SEQ, first=(lambda k: pe.wait_ge(x_ready, k + 1)) if u == 0 else None)
            if u == 5:
                pe.wait_ge(hyb_loaded, 16)
                pe.wait_ge(flag("g_ready"), 1)
                nc.tensor.matmul(psum[:, 4, 16:24], hc("tri"), row(G_STEP), start=True, stop=True).then_inc(flag("cumsum"), 1)
            if u == 9:
                pe.wait_ge(flag("gb_ready"), 1)
                pe.wait_ge(shared_loaded, 16)
                for p in range(PAIRS):
                    last = nc.tensor.transpose(cells(5, PAIRS, P)[:, p, :], h_gb[:, p, :], ident)
                last.then_inc(flag("g_rows"), 1)
            if u in (12, 16):
                n = 1 if u == 12 else 2
                pe.wait_ge(flag("conv_squares"), 4 * n)
                pe.wait_ge(flag("banks56_read"), n)
                for i in range(4):
                    last = nc.tensor.matmul(cells(5, 4, SEQ)[:, i, :], ones[:, :], h_sq[:, i, :], start=True, stop=True)
                last.then_inc(flag("conv_sums"), 1)
            if u == 17:
                pe.wait_ge(flag("banks56_read"), 3)
                for i in range(5):
                    wait_drained(pe, 12 + i)
                    last = nc.tensor.matmul(cells(4, 5, SEQ)[:, i, :], hc("rot1"), h_qk[:, i, :], start=True, stop=True)
                last.then_inc(flag("rotated_halves"), 1)
        for u in range(HYB_IN - BANKS, HYB_IN):
            wait_drained(pe, u)
        for t in range(2):
            last = nc.tensor.transpose(cells(0, 2, P)[:, t, :], h_vT[:, t * P:(t + 1) * P], ident)
        last.then_inc(flag("v_rows"), 1)
        pe.wait_ge(flag("conv_silu"), 12)
        for p in range(PAIRS):
            last = nc.tensor.transpose(cells(1, PAIRS, P)[:, p, :], pair_cols(v_h, p), ident)
        last.then_inc(flag("v_tok"), 1)
        pe.wait_ge(flag("cond_split"), 1)
        mods(pe, "v_tok")
        pe.wait_ge(flag("qk_rotated"), 1)
        pe.wait_ge(flag("conv_normed"), 1)
        for p in range(PAIRS):
            last = nc.tensor.transpose(cells(3, PAIRS, P)[:, p, :], pair_cols(k_h, p), ident)
        last.then_inc(flag("k_tok"), 1)
        for p in range(PAIRS):
            last = nc.tensor.matmul(cells(5, PAIRS, P)[:, p, :], pair_cols(k_h, p), pair_cols(k_h, p), start=True, stop=True)
        last.then_inc(flag("gram"), 1)
        mods(pe, "gram")
        pe.wait_ge(flag("vb_ready"), 1)
        pe.wait_ge(flag("conv_normed"), 2)
        for p in range(PAIRS):
            last = nc.tensor.matmul(cells(1, PAIRS, P)[:, p, :], pair_cols(q_h, p), pair_cols(k_h, p), start=True, stop=True)
        last.then_inc(flag("qk"), 1)
        mods(pe, "qk")
        pe.wait_ge(flag("A_ready"), 1)
        for p in range(PAIRS):
            last = nc.tensor.transpose(cells(5, PAIRS, P)[:, p, :], h_A[:, p, :], ident)
        last.then_inc(flag("AT_ps"), 1)
        mods(pe, "AT")
        pe.wait_ge(flag("qk_decayed"), 1)
        for p in range(PAIRS):
            last = nc.tensor.transpose(cells(3, PAIRS, P)[:, p, :], h_Q[:, p, :], ident)
        last.then_inc(flag("qkT_ps"), 1)
        pe.wait_ge(flag("qkT_ready"), 1)
        for level in range(1, len(DN_BLOCKS)):
            for part, half in enumerate(HALVES):
                pe.wait_ge(flag("M_ready"), 2 * level + part - 1)
                pe.wait_ge(flag("T_ready"), 2 * level - 2 + part if level > 1 else 1)
                for p in half:
                    last = nc.tensor.matmul(cells(0, PAIRS, P)[:, p, :], h_M[:, p, :], h_T[:, p, :], start=True, stop=True)
                last.then_inc(flag("MT_ps"), 1)
            mods(pe, f"MT{level}")
            for part, half in enumerate(HALVES):
                pe.wait_ge(flag("MT_ready"), 2 * level + part - 1)
                if level > 1:
                    pe.wait_ge(flag("TT_ready"), 2 * level + part - 3)
                for p in half:
                    last = nc.tensor.matmul(cells(2, PAIRS, P)[:, p, :], h_TT[:, p, :], h_Q[:, p, :], start=True, stop=True)
                last.then_inc(flag("TMT_ps"), 1)
            for part, half in enumerate(HALVES):
                pe.wait_ge(flag("T_ready"), 2 * level + part)
                for p in half:
                    last = nc.tensor.transpose(cells(5, PAIRS, P)[:, p, :], h_T[:, p, :], ident)
                last.then_inc(flag("TT_ps"), 1)
            mods(pe, f"TMT{level}")
        pe.wait_ge(flag("TT_ready"), 2 * LEVELS)
        for p in range(PAIRS):
            last = nc.tensor.matmul(cells(0, PAIRS, P)[:, p, :], h_TT[:, p, :], h_vb[:, p, :], start=True, stop=True)
        last.then_inc(flag("u_ps"), 1)
        for h in range(B_HEADS):
            last = nc.tensor.matmul(bank(2)[:, h * P:(h + 1) * P], h_kbe[:, h, :], h_TT[:, B_HEADS + h, :], start=True, stop=True)
        last.then_inc(flag("wT_ps"), 1)
        mods(pe, "wT")
        pe.wait_ge(flag("u_ready"), 1)
        for h in range(B_HEADS):
            last = nc.tensor.matmul(bank(3)[:, h * P:(h + 1) * P], h_ktail[:, h, :], h_u[:, h, :], start=True, stop=True)
        last.then_inc(flag("S_ps"), 1)
        mods(pe, "S")
        pe.wait_ge(flag("wT_ready"), 1)
        pe.wait_ge(flag("S_ready"), 1)
        for h in range(B_HEADS):
            last = nc.tensor.matmul(bank(4)[:, h * P:(h + 1) * P], h_wT[:, h, :], h_S[:, h, :], start=True, stop=True)
        last.then_inc(flag("wS_ps"), 1)
        mods(pe, "wS")
        pe.wait_ge(flag("vn_ready"), 1)
        pe.wait_ge(flag("qg_ready"), 1)
        for h in range(B_HEADS):
            o = cells(5, B_HEADS, SEQ)[:, h, :]
            nc.tensor.matmul(o[:, 0:P], h_u[:, h, :], h_qkT[:, h, :], start=True, stop=True)
            nc.tensor.matmul(o[:, P:SEQ], h_S[:, h, :], h_qg[:, h, :], start=True, stop=False)
            last = nc.tensor.matmul(o[:, P:SEQ], h_vn[:, h, :], h_qkT[:, B_HEADS + h, :], start=False, stop=True)
        last.then_inc(flag("o_ps"), 1)
        mods(pe, "o")
        pe.wait_ge(flag("o_squares"), 1)
        for h in range(B_HEADS):
            last = nc.tensor.matmul(cells(0, B_HEADS, SEQ)[:, h, :], ones[:, :], h_sq[:, h, :], start=True, stop=True)
        last.then_inc(flag("o_sums"), 1)
        mods(pe, "o_sums")
        for f in range(2):
            a = f * A_DH
            if f:
                pe.wait_ge(flag("a_pT_ready"), f)
            for t in range(4):
                nc.tensor.matmul(bank(2)[:, t * P:(t + 1) * P], h_qk[a:a + A_DH, t, 0:P], h_qk[a:a + A_DH, 4, 0:P],
                                 start=True, stop=True)
            for t in range(4):
                last = nc.tensor.matmul(cells(3, 4, SEQ)[:, t, :], h_qk[a:a + A_DH, t, P:SEQ], h_qk[a:a + A_DH, 4, :],
                                        start=True, stop=True)
            last.then_inc(flag("a_scores"), 1)
            mods(pe, f"scores{f}")
            pe.wait_ge(flag("a_probs"), f + 1)
            for j in range(12):
                last = nc.tensor.transpose(cells(2, 12, P)[:, j, :], h_p[:, j // 3, (j % 3) * P:(j % 3 + 1) * P], ident)
            last.then_inc(flag("a_pT_ps"), 1)
            mods(pe, f"probs{f}")
            pe.wait_ge(flag("a_pT_ready"), f + 1)
            pe.wait_ge(flag("v_rows_read"), 1)
            pe.wait_ge(flag("o_read"), 1)
            for t in range(4):
                h = f * 4 + t
                b = (h % 2) * A_DH
                o = psum[b:b + A_DH, 5 + h // 4, :].rearrange("p (n w) -> p n w", n=2)[:, (h // 2) % 2, :]
                v = [h_v[:, j, a:a + A_DH] for j in range(2)]
                nc.tensor.matmul(o[:, 0:P], v[0], h_pT[:, t, 0:P], start=True, stop=True)
                nc.tensor.matmul(o[:, P:SEQ], v[0], h_pT[:, t, P:2 * P], start=True, stop=False)
                last = nc.tensor.matmul(o[:, P:SEQ], v[1], h_pT[:, t, 2 * P:3 * P], start=False, stop=True)
            last.then_inc(flag("a_out_ps"), 1)
        mods(pe, "merge")
        for u in range(U_HOUT, U_HOUT + KT):
            unit(pe, u, x_hi, x_lo, SEQ, first=(lambda k: pe.wait_ge(flag("merged"), 2)) if u == U_HOUT else None)

    def hyb_act(act, link):
        act.wait_ge(consts_set, 1)
        act.wait_ge(par_loaded, 16)
        other_set()
        nc.scalar.activation(silu_c[:, :, :].rearrange("p k s -> p (k s)"), pcol("cond", 0, 2 * KT), ACT.Silu).then_inc(flag("silu_c"), 1)
        act.wait_ge(flag("silu_c"), 1)
        nc.scalar.activation(cond[:, :, 0:2], silu_c[:, :, :], ACT.Copy).then_inc(flag("cond_hi"), 1)
        act.wait_ge(x_loaded, 16)
        for k in range(KT):
            nc.scalar.activation(x_hi[:, k, 0:SEQ], x[:, k, 0:SEQ], ACT.Copy).then_inc(split_hi, 1)
        exp_set()
        nc.scalar.activation(row(EXP_A, 0, 4), pcol("a_log", 0, 4), ACT.Exp).then_inc(flag("exp_abs"), 1)

        def silu(i):
            act.wait_ge(flag("conv_done"), i + 1)
            other_set()
            nc.scalar.activation(h_conv[:, i, :], h_conv[:, i, :], ACT.Silu).then_inc(flag("conv_silu"), 1)
            if i < 8:
                act.wait_ge(flag("conv_silu"), i + 1)
                if i >= 4:
                    act.wait_ge(flag("conv_sums"), 1)
                nc.scalar.activation(h_sq[:, i % 4, :], h_conv[:, i, :], ACT.Square).then_inc(flag("conv_squares"), 1)

        def conv_rstd(n):
            act.wait_ge(flag("conv_sums"), n + 1)
            if n:
                act.wait_ge(flag("conv_normed"), n)
            exp_set()
            link(nc.scalar.activation(h_rs[:, :, :].rearrange("p a b -> p (a b)"), psum[:, 5:7, :].rearrange("p a b -> p (a b)"),
                                      ACT.Ln, bias=eps[:, 1:2]))
            exp_set()
            nc.scalar.activation(h_rs[:, :, :], h_rs[:, :, :], ACT.Exp, scale=-0.5).then_inc(flag("banks56_read"), 1)

        pending = []
        for u in range(HYB_IN):
            wait_unit(act, u)
            if u < HYB_TILES:
                nc.scalar.activation(h_pad[:, u, B_TAPS - 1:], bank(u % BANKS, SEQ), ACT.Copy).then_inc(drained[u % BANKS], 1)
                if 1 <= u <= 4:
                    silu(u - 1)
            elif u < 17:
                nc.scalar.activation(h_qk[:, u - 12, :], bank(u % BANKS, SEQ), ACT.Copy).then_inc(drained[u % BANKS], 1)
            elif u == 17:
                nc.scalar.activation(h_vT[:, :], bank(u % BANKS, SEQ), ACT.Copy).then_inc(drained[u % BANKS], 1)
            else:
                other_set()
                nc.scalar.activation(h_z[:, u - 18, :], bank(u % BANKS, SEQ), ACT.Silu).then_inc(drained[u % BANKS], 1)
            if u == 1:
                act.wait_ge(flag("abs_a"), 1)
                exp_set()
                nc.scalar.activation(row(EXP_ABS), row(ABS), ACT.Exp).then_inc(flag("exp_abs"), 1)
                exp_set()
                nc.scalar.activation(row2(BETA), h_lg[:, :, 0:4], ACT.Exp, scale=-1.0).then_inc(flag("exp_abs"), 1)
            if u == 8:
                act.wait_ge(flag("gb_ready"), 1)
                exp_set()
                nc.scalar.activation(row(EXP_G), row(G), ACT.Exp).then_inc(flag("exp_g"), 1)
            if u == 11:
                act.wait_ge(flag("decay_in"), 1)
                exp_set()
                nc.scalar.activation(h_decay[:, :, :], h_decay[:, :, :], ACT.Exp, scale=-1.0).then_inc(flag("exp_g"), 1)
                exp_set()
                nc.scalar.activation(row(TAIL, 0, 4), row(TAIL, 0, 4), ACT.Exp).then_inc(flag("exp_g"), 1)
                exp_set()
                nc.scalar.activation(h_expg[:, :, :], cells(5, PAIRS, P)[:, 4:8, :], ACT.Exp).then_inc(flag("banks56_read"), 1)
            if u == 13:
                conv_rstd(0)
                for i in range(4, 8):
                    silu(i)
            if u == 15:
                for i in range(8, 12):
                    silu(i)
            if u == 17:
                conv_rstd(1)
        act.wait_ge(flag("v_rows"), 1)
        nc.scalar.activation(h_v[:, :, :], cells(0, 2, P), ACT.Copy).then_inc(flag("v_rows_read"), 1)
        act.wait_ge(flag("AT_ps"), 1)
        nc.scalar.activation(h_AT[:, :, :], cells(5, PAIRS, P), ACT.Copy).then_inc(flag("AT_ready"), 1)
        act.wait_ge(flag("qkT_ps"), 1)
        nc.scalar.activation(h_qkT[:, :, :], cells(3, PAIRS, P), ACT.Copy).then_inc(flag("qkT_ready"), 1)
        for level in range(1, len(DN_BLOCKS)):
            for dst, b, done, ready in ((h_Q, 0, "MT_ps", "MT_ready"), (h_TT, 5, "TT_ps", "TT_ready")):
                for part, half in enumerate(HALVES):
                    act.wait_ge(flag(done), 2 * level + part - 1)
                    nc.scalar.activation(dst[:, half[0]:half[-1] + 1, :], cells(b + part, PAIRS // 2, P), ACT.Copy).then_inc(flag(ready), 1)
        act.wait_ge(flag("u_ps"), 1)
        nc.scalar.activation(h_u[:, :, :], cells(0, PAIRS, P), ACT.Copy).then_inc(flag("u_ready"), 1)
        act.wait_ge(flag("S_ps"), 1)
        nc.scalar.activation(h_S[:, :, :], cells(3, 4, P), ACT.Copy).then_inc(flag("S_ready"), 1)
        act.wait_ge(flag("o_ps"), 1)
        nc.scalar.activation(h_sq[:, :, :], cells(5, 4, SEQ), ACT.Square).then_inc(flag("o_squares"), 1)
        act.wait_ge(flag("o_sums"), 1)
        exp_set()
        link(nc.scalar.activation(h_rs[:, :, :], cells(0, 4, SEQ), ACT.Ln, bias=eps[:, 1:2], scale=1.0 / P))
        exp_set()
        nc.scalar.activation(h_rs[:, :, :], h_rs[:, :, :], ACT.Exp, scale=-0.5).then_inc(flag("o_rstd"), 1)
        for f in range(2):
            act.wait_ge(flag("a_max"), f + 1)
            for i in range(8):
                t, b = i % 4, i // 4
                part = h_p[:, t, 0:P] if b == 0 else h_p[:, t, P:3 * P]
                exp_set()
                nc.scalar.activation(part, part, ACT.Exp, bias=h_soft[:, 1, i:i + 1],
                                     accum_out=h_soft[:, 2, i:i + 1]).then_inc(flag("a_exp"), 1)
            exp_set()
            nc.scalar.activation(h_soft[:, 3, :], h_soft[:, 3, :], ACT.Exp).then_inc(flag("a_exp"), 1)
            act.wait_ge(flag("a_pT_ps"), f + 1)
            nc.scalar.activation(h_pT[:, :, :].rearrange("p t c -> p (t c)").rearrange("p (j c) -> p j c", c=P), cells(2, 12, P),
                                 ACT.Copy).then_inc(flag("a_pT_ready"), 1)
        act.wait_ge(flag("o_gated"), 1)
        nc.scalar.activation(x_hi[:, 4:8, 0:SEQ], h_o, ACT.Copy).then_inc(flag("merged_hi"), 1)
        act.wait_ge(flag("a_out_ps"), 2)
        nc.scalar.activation(x_hi[:, 0:4, 0:SEQ], cells(5, 4, SEQ), ACT.Copy).then_inc(flag("merged_hi"), 1)

    def hyb_dve(dve, link):
        link(nc.vector.memset(ones[:, :], 1.0))
        link(nc.vector.memset(eps[:, 0:1], LN_EPS))
        nc.vector.memset(eps[:, 1:2], EPS).then_inc(consts_set, 1)
        link(nc.vector.memset(h_pad[:, :, 0:B_TAPS - 1], 0.0))
        dve.wait_ge(x_loaded, 16)
        lo_split(dve, 0)
        for k in range(KT):
            dve.wait_ge(split_hi, k + 1)
            nc.vector.tensor_tensor(x_lo[:, k, 0:SEQ], x[:, k, 0:SEQ], x_hi[:, k, 0:SEQ].bitcast(F32), ALU.subtract).then_inc(x_ready, 1)
        for u in range(1, LEAD):
            lo_split(dve, u)
        dve.wait_ge(par_loaded, 16)
        dve.wait_ge(flag("cond_hi"), 1)
        nc.vector.tensor_tensor(cond[:, :, 2:4], silu_c[:, :, :], cond[:, :, 0:2].bitcast(F32), ALU.subtract).then_inc(flag("cond_split"), 1)
        dve.wait_ge(flag("logits"), 1)
        link(nc.vector.tensor_copy(h_lg[:, :, :].rearrange("p t c -> p (t c)"), psum[:, 4, 0:16]))
        link(nc.vector.tensor_tensor(row2(A_IN), h_lg[:, :, 4:8], bc(pcol("dt_bias", 0, 4), 2), ALU.add))
        nc.vector.scalar_tensor_tensor(row(ABS), row(A_IN), -1.0, row(A_IN), ALU.mult, ALU.min).then_inc(flag("abs_a"), 1)

        def conv(i):
            wait_drained(dve, i)
            tap = lambda j: pcol("hyb_conv", i * B_TAPS + j)
            link(nc.vector.tensor_scalar(h_conv[:, i, :], h_pad[:, i, 0:SEQ], tap(0), None, ALU.mult))
            for j in range(1, B_TAPS):
                last = nc.vector.scalar_tensor_tensor(h_conv[:, i, :], h_pad[:, i, j:j + SEQ], tap(j), h_conv[:, i, :],
                                                      ALU.mult, ALU.add)
                if j < B_TAPS - 1:
                    link(last)
            last.then_inc(flag("conv_done"), 1)

        def log_decay():
            dve.wait_ge(flag("exp_abs"), 3)
            link(nc.vector.tensor_scalar(row(TMP), row(BETA), 1.0, None, ALU.add))
            link(nc.vector.reciprocal(row(BETA), row(TMP)))
            log1p_series(link, row(EXP_ABS), row(S1), row(S2), row(POLY))
            link(nc.vector.tensor_scalar(row(RELU_A), row(A_IN), 0.0, None, ALU.max))
            link(nc.vector.scalar_tensor_tensor(row(TMP), row(POLY), 2.0, row(RELU_A), ALU.mult, ALU.add))
            nc.vector.scalar_tensor_tensor(row2(G_STEP), row2(TMP), -1.0, bc(row(EXP_A, 0, 4), 2), ALU.mult,
                                           ALU.mult).then_inc(flag("g_ready"), 1)

        def normalise(n):
            dve.wait_ge(flag("banks56_read"), n + 2)
            part = q_h if n else k_h
            nc.vector.scalar_tensor_tensor(part, part, float(P) ** -0.5 if n else 1.0, h_rs[:, :, :], ALU.mult,
                                           ALU.mult).then_inc(flag("conv_normed"), 1)

        for u in range(HYB_IN):
            if u < HYB_TILES:
                conv(u)
            else:
                wait_unit(dve, u - 1)
            next_lo(dve, u)
            if u == 2:
                log_decay()
            if u == 6:
                dve.wait_ge(flag("cumsum"), 1)
                link(nc.vector.tensor_copy(row(G), psum[:, 4, 16:24]))
                for p in range(PAIRS):
                    last = nc.vector.tensor_scalar(h_gb[:, p, :], ones[:, :], row(G, p, p + 1), None, ALU.mult)
                last.then_inc(flag("gb_ready"), 1)
            if u == 10:
                dve.wait_ge(flag("g_rows"), 1)
                rows = cells(5, PAIRS, P)
                for p in range(PAIRS):
                    nc.vector.tensor_scalar(h_decay[:, p, :], rows[:, p, :], row(G, p, p + 1), 0.0, ALU.subtract, ALU.max)
                nc.vector.tensor_tensor(row(TAIL, 0, 4), rows[:, 0:4, P - 1], row(G, 0, 4), ALU.subtract).then_inc(flag("decay_in"), 1)
            if u == 12:
                dve.wait_ge(flag("exp_g"), 3)
                dve.wait_ge(hyb_loaded, 16)
                nc.vector.tensor_tensor(row(BETA_G), row(BETA), row(EXP_G), ALU.mult)
                link(nc.vector.tensor_tensor(h_decay[:, :, :], h_decay[:, :, :], bc(hc("incl"), PAIRS), ALU.mult))
            if u == 15:
                normalise(0)
            if u == 18:
                dve.wait_ge(flag("rotated_halves"), 1)
                normalise(1)
                link(nc.vector.tensor_tensor(h_rot[:, :, :], cells(4, 5, SEQ), bc(hc("sin1", SEQ), 5), ALU.mult))
                link(nc.vector.tensor_tensor(h_qk[:, :, :], h_qk[:, :, :], bc(hc("cos1", SEQ), 5), ALU.mult))
                nc.vector.tensor_tensor(h_qk[:, :, :], h_qk[:, :, :], h_rot[:, :, :], ALU.add).then_inc(flag("qk_rotated"), 1)
        dve.wait_ge(flag("v_tok"), 1)
        for p in range(PAIRS):
            last = nc.vector.tensor_scalar(h_vb[:, p, :], cells(1, PAIRS, P)[:, p, :], row(BETA, p, p + 1), None, ALU.mult)
        last.then_inc(flag("vb_ready"), 1)
        next_mods(dve, "v_tok")
        dve.wait_ge(flag("k_tok"), 1)
        for p in range(PAIRS):
            h = p % B_HEADS
            dst, by = (h_ktail[:, h, :], row(TAIL, h, h + 1)) if p < B_HEADS else (h_kbe[:, h, :], row(BETA_G, p, p + 1))
            nc.vector.tensor_scalar(dst, cells(3, PAIRS, P)[:, p, :], by, None, ALU.mult)
        dve.wait_ge(flag("gram"), 1)
        for p in range(PAIRS):
            last = nc.vector.scalar_tensor_tensor(h_A[:, p, :], cells(5, PAIRS, P)[:, p, :], row(BETA, p, p + 1),
                                                  h_decay[:, p, :], ALU.mult, ALU.mult)
        last.then_inc(flag("A_ready"), 1)
        next_mods(dve, "gram")
        dve.wait_ge(flag("qk"), 1)
        nc.vector.tensor_tensor(h_Q[:, :, :], cells(1, PAIRS, P), h_decay[:, :, :], ALU.mult).then_inc(flag("qk_decayed"), 1)
        nc.vector.tensor_tensor(h_qg[:, :, :], q_h[:, :, P:SEQ], h_expg[:, :, :], ALU.mult).then_inc(flag("qg_ready"), 1)
        next_mods(dve, "qk")
        dve.wait_ge(flag("A_ready"), 1)
        link(nc.vector.tensor_tensor(h_T[:, :, :], h_A[:, :, :], bc(hc("low1"), PAIRS), ALU.mult))
        link(nc.vector.tensor_tensor(h_T[:, :, :], bc(ident, PAIRS), h_T[:, :, :], ALU.subtract))
        dve.wait_ge(flag("AT_ready"), 1)
        link(nc.vector.tensor_tensor(h_TT[:, :, :], h_AT[:, :, :], bc(hc("up"), PAIRS), ALU.mult))
        nc.vector.tensor_tensor(h_TT[:, :, :], bc(ident, PAIRS), h_TT[:, :, :], ALU.subtract).then_inc(flag("T_ready"), 1)
        next_mods(dve, "AT")
        def lower(level, part):
            c = slice(HALVES[part][0], HALVES[part][-1] + 1)
            nc.vector.tensor_tensor(h_M[:, c, :], h_AT[:, c, :], bc(hc("up", P, level * P), PAIRS // 2), ALU.mult).then_inc(flag("M_ready"), 1)

        for part in range(2):
            lower(1, part)
        for level in range(1, len(DN_BLOCKS)):
            for part in range(2):
                dve.wait_ge(flag("MT_ps"), 2 * level + part - 1)
                if level < LEVELS:
                    lower(level + 1, part)
            next_mods(dve, f"MT{level}")
            for part, half in enumerate(HALVES):
                dve.wait_ge(flag("TMT_ps"), 2 * level + part - 1)
                c = slice(half[0], half[-1] + 1)
                nc.vector.tensor_tensor(h_T[:, c, :], h_T[:, c, :], cells(2 + part, PAIRS // 2, P), ALU.subtract).then_inc(flag("T_ready"), 1)
            next_mods(dve, f"TMT{level}")
        dve.wait_ge(flag("wT_ps"), 1)
        nc.vector.tensor_copy(h_wT[:, :, :], cells(2, 4, P)).then_inc(flag("wT_ready"), 1)
        next_mods(dve, "wT")
        next_mods(dve, "S")
        dve.wait_ge(flag("u_ready"), 1)
        dve.wait_ge(flag("wS_ps"), 1)
        nc.vector.tensor_tensor(h_vn[:, :, :], h_u[:, B_HEADS:, :], cells(4, 4, P), ALU.subtract).then_inc(flag("vn_ready"), 1)
        next_mods(dve, "wS")
        next_mods(dve, "o")
        dve.wait_ge(flag("o_rstd"), 1)
        nc.vector.tensor_tensor(h_o, cells(5, 4, SEQ), h_rs[:, :, :], ALU.mult).then_inc(flag("o_read"), 1)
        dve.wait_ge(flag("o_read"), 1)
        wait_drained(dve, HYB_IN - 1)
        nc.vector.scalar_tensor_tensor(h_o, h_o, pcol("norm_w"), h_z[:, :, :], ALU.mult, ALU.mult).then_inc(flag("o_gated"), 1)
        next_mods(dve, "o_sums")
        for f in range(2):
            dve.wait_ge(flag("a_scores"), f + 1)
            sinks = pcol("sinks", 4 * f, 4)
            mask = hc("window", 2 * P)
            nc.vector.scalar_tensor_tensor(h_p[:, :, 0:P], cells(2, 4, P), A_DH ** -0.5, bc(mask[:, P:2 * P], 4), ALU.mult, ALU.add)
            link(nc.vector.scalar_tensor_tensor(h_p[:, :, P:3 * P], cells(3, 4, SEQ), A_DH ** -0.5, bc(mask, 4), ALU.mult, ALU.add))
            nc.vector.tensor_reduce(h_soft[:, 0, 0:4], h_p[:, :, 0:P], AX.X, ALU.max)
            link(nc.vector.tensor_reduce(h_soft[:, 0, 4:8], h_p[:, :, P:3 * P], AX.X, ALU.max))
            two = lambda i: h_soft[:, i, :].rearrange("p (b t) -> p b t", b=2)
            link(nc.vector.tensor_tensor(two(0), two(0), bc(sinks, 2), ALU.max))
            nc.vector.tensor_tensor(two(3), bc(sinks, 2), two(0), ALU.subtract)
            nc.vector.tensor_scalar(h_soft[:, 1, :], h_soft[:, 0, :], -1.0, None, ALU.mult).then_inc(flag("a_max"), 1)
            next_mods(dve, f"scores{f}")
            dve.wait_ge(flag("a_exp"), 9 * (f + 1))
            link(nc.vector.tensor_tensor(h_soft[:, 4, :], h_soft[:, 2, :], h_soft[:, 3, :], ALU.add))
            link(nc.vector.reciprocal(h_soft[:, 0, :], h_soft[:, 4, :]))
            for b, part in enumerate((h_p[:, :, 0:P], h_p[:, :, P:3 * P])):
                by = h_soft[:, 0, 4 * b:4 * b + 4].unsqueeze(2).broadcast_to([P, 4, part.shape[2]])
                last = nc.vector.tensor_tensor(part, part, by, ALU.mult)
            last.then_inc(flag("a_probs"), 1)
            next_mods(dve, f"probs{f}")
        dve.wait_ge(flag("merged_hi"), 1)
        nc.vector.tensor_tensor(x_lo[:, 4:8, 0:SEQ], h_o, x_hi[:, 4:8, 0:SEQ].bitcast(F32), ALU.subtract).then_inc(flag("merged"), 1)
        dve.wait_ge(flag("merged_hi"), 2)
        nc.vector.tensor_tensor(x_lo[:, 0:4, 0:SEQ], cells(5, 4, SEQ), x_hi[:, 0:4, 0:SEQ].bitcast(F32),
                                ALU.subtract).then_inc(flag("merged"), 1)
        next_mods(dve, "merge")
        for u in range(U_HOUT, U_HOUT + KT):
            k = u - U_HOUT
            wait_unit(dve, u)
            nc.vector.scalar_tensor_tensor(y[:, k, 0:SEQ], x[:, k, 0:SEQ], ALPHA, bank(u % BANKS, SEQ), ALU.mult,
                                           ALU.add).then_inc(drained[u % BANKS], 1)
            next_lo(dve, u)

    def log1p_series(link, e, s, s2, poly):
        link(nc.vector.tensor_scalar(s2, e, 2.0, None, ALU.add))
        link(nc.vector.reciprocal(s, s2))
        link(nc.vector.tensor_tensor(s, s, e, ALU.mult))
        link(nc.vector.tensor_tensor(s2, s, s, ALU.mult))
        link(nc.vector.tensor_scalar(poly, s2, 1.0 / 17, None, ALU.mult))
        for c in (15, 13, 11, 9, 7, 5, 3):
            link(nc.vector.scalar_tensor_tensor(poly, poly, 1.0 / c, s2, ALU.add, ALU.mult))
        link(nc.vector.scalar_tensor_tensor(poly, poly, 1.0, s, ALU.add, ALU.mult))

    def norm_pe(pe, n, T, mean=None):
        if mean:
            for k in range(KT):
                wait_drained(pe, mean[1] + k)
                last = nc.tensor.matmul(bank(4, T), ones[:, :], y[:, k, 0:T], start=(k == 0), stop=(k == KT - 1))
            last.then_inc(flag("mean_ps"), 1)
            mods(pe, f"mean{mean[0]}")
        for k in range(KT):
            pe.wait_ge(flag("norm_sq"), KT * n + k + 1)
            last = nc.tensor.matmul(bank(5, T), ones[:, :], sq[:, k, 0:T], start=(k == 0), stop=(k == KT - 1))
        last.then_inc(flag("norm_sum"), 1)
        if mean:
            mods(pe, f"norm{mean[0]}")
            if mean[0] == 3:
                turn_group(pe, MOD_UNITS // 2 - 1)

    def norm_rstd_act(act, link, n, T, e):
        act.wait_ge(flag("norm_sum"), n + 1)
        exp_set()
        link(nc.scalar.activation(stat[:, 0:T], bank(5, T), ACT.Ln, bias=eps[:, e:e + 1], scale=1.0 / D))
        exp_set()
        nc.scalar.activation(rstd[:, 0:T], stat[:, 0:T], ACT.Exp, scale=-0.5).then_inc(flag("norm_rstd"), 1)

    def squares_act(act, n, T, src, name, at):
        for k in range(KT):
            act.wait_ge(flag(name), at + k + 1)
            nc.scalar.activation(sq[:, k, 0:T], src[:, k, 0:T], ACT.Square).then_inc(flag("norm_sq"), 1)

    def split_act(act, s, T, src):
        for k in range(KT):
            act.wait_ge(flag("normed_f32"), KT * s + k + 1)
            nc.scalar.activation(x_hi[:, k, 0:T], src[:, k, 0:T], ACT.Copy).then_inc(split_hi, 1)

    def split_dve(dve, s, k, T, src):
        dve.wait_ge(split_hi, KT * (s + 1) + k + 1)
        nc.vector.tensor_tensor(x_lo[:, k, 0:T], src[:, k, 0:T], x_hi[:, k, 0:T].bitcast(F32), ALU.subtract).then_inc(x_ready, 1)

    LN_AFTER = (1, 3, 5, 7)

    def layer_norm_dve(dve, link, n, ln, g, b, s):
        T = SEQ
        dve.wait_ge(flag("mean_ps"), ln + 1)
        for k in range(KT):
            nc.vector.scalar_tensor_tensor(y[:, k, 0:T], bank(4, T), -1.0 / D, y[:, k, 0:T], ALU.mult, ALU.add).then_inc(flag("centered"), 1)
        next_mods(dve, f"mean{ln}")
        dve.wait_ge(flag("norm_rstd"), n + 1)
        for k in range(KT):
            link(nc.vector.tensor_tensor(normed[:, k % 2, 0:T], y[:, k, 0:T], rstd[:, 0:T], ALU.mult))
            last = nc.vector.tensor_scalar(x[:, k, 0:T], normed[:, k % 2, 0:T], pcol(g, ln // 2 * KT + k), pcol(b, ln // 2 * KT + k),
                                           ALU.mult, ALU.add)
            if s is None:
                last.then_inc(flag("x_updated"), 1)
            else:
                last.then_inc(flag("normed_f32"), 1)
                if k:
                    split_dve(dve, s, k - 1, T, x)
                if k in LN_AFTER:
                    pass_mod(dve, MOD_RANGE[f"norm{ln}"][LN_AFTER.index(k)])
        if s is not None:
            split_dve(dve, s, KT - 1, T, x)
        else:
            next_mods(dve, f"norm{ln}")

    def streams(T):
        return [(i, slice(i * SEQ, (i + 1) * SEQ)) for i in range(T // SEQ)]

    def modulated_dve(dve, link, n, T, l, part, s):
        dve.wait_ge(flag("norm_rstd"), n + 1)
        for k in range(KT):
            link(nc.vector.tensor_tensor(normed[:, k % 2, 0:T], x[:, k, 0:T], rstd[:, 0:T], ALU.mult))
            for i, c in streams(T):
                last = nc.vector.tensor_scalar(y[:, k, c], normed[:, k % 2, c], coef[:, l, part + 1, k, i:i + 1],
                                               coef[:, l, part, k, i:i + 1], ALU.mult, ALU.add)
            last.then_inc(flag("normed_f32"), 1)
            if k:
                split_dve(dve, s, k - 1, T, y)
        split_dve(dve, s, KT - 1, T, y)

    def gated_dve(dve, link, n, T, l, part):
        dve.wait_ge(flag("norm_rstd"), n + 1)
        for k in range(KT):
            link(nc.vector.tensor_tensor(normed[:, k % 2, 0:T], y[:, k, 0:T], rstd[:, 0:T], ALU.mult))
            for i, c in streams(T):
                last = nc.vector.scalar_tensor_tensor(x[:, k, c], normed[:, k % 2, c], coef[:, l, part, k, i:i + 1], x[:, k, c],
                                                      ALU.mult, ALU.add)
            last.then_inc(flag("x_updated"), 1)

    def mlp_pe(pe, m, base, T, s):
        with pe.Fori(0, QUARTERS) as i:
            turn = lambda u: i * 4 + u // BANKS
            first_units(pe, base, x_hi, x_lo, T, lambda k: pe.wait_ge(x_ready, KT * (s + 1) + k + 1), i * 16 + base, turn)
            for u in range(base + FIRST, base + KT):
                unit(pe, u, x_hi, x_lo, T, n=i * 16 + u, turn=turn(u))
            for j in range(KT):
                u = base + KT + j
                unit(pe, u, hid_hi, hid_lo, T,
                     first=(lambda k: pe.wait_ge(flag("hidden_ready"), i * KT + (KT * QUARTERS * m + k + 1))) if j == 0 else None,
                     n=i * 16 + u, turn=turn(u))

    def mlp_act(act, m, base, T):
        with act.Fori(0, QUARTERS) as i:
            for j in range(KT):
                u = base + j
                turn = i * 4 + u // BANKS
                wait_unit(act, u, i * 16 + u)
                if j >= 2:
                    act.wait_ge(flag("hidden_ready"), i * KT + (KT * QUARTERS * m + j - 1))
                nc.scalar.activation(relu[:, j % 2, 0:T], bank(u % BANKS, T), ACT.Relu).then_inc(drained[u % BANKS], 1)
                wait_drained(act, u, turn)
                nc.scalar.activation(hid_hi[:, j, 0:T], relu[:, j % 2, 0:T], ACT.Square).then_inc(flag("hidden_hi"), 1)

    def mlp_dve(dve, m, base, T):
        with dve.Fori(0, QUARTERS) as i:
            for j in range(KT):
                u = base + j
                dve.wait_ge(flag("hidden_hi"), i * KT + (KT * QUARTERS * m + j + 1))
                nc.vector.tensor_tensor(relu2[:, j % 2, 0:T], relu[:, j % 2, 0:T], relu[:, j % 2, 0:T], ALU.mult).then_inc(flag("hidden_sq"), 1)
                dve.wait_ge(flag("hidden_sq"), i * KT + (KT * QUARTERS * m + j + 1))
                nc.vector.tensor_tensor(hid_lo[:, j, 0:T], relu2[:, j % 2, 0:T], hid_hi[:, j, 0:T].bitcast(F32),
                                        ALU.subtract).then_inc(flag("hidden_ready"), 1)
                lo_split(dve, u + LEAD, i * 16 + (u + LEAD))
            for j in range(KT):
                u = base + KT + j
                wait_unit(dve, u, i * 16 + u)
                nc.vector.tensor_tensor(y[:, j, 0:T], bank(u % BANKS, T), y[:, j, 0:T], ALU.add).then_inc(drained[u % BANKS], 1)
                lo_split(dve, u + LEAD, i * 16 + (u + LEAD))

    r = Region(M0, END)
    r_pad = r("r_pad", [P, KT, SEQ + B_TAPS - 1])
    r_x = r("r_x", [P, KT, SEQ])
    r_hi = r("r_hi", [P, KT, SEQ], F32R)
    r_lo = r("r_lo", [P, KT, SEQ], F32R)
    r_t = r("r_t", [P, KT, SEQ])
    r_i = r("r_i", [P, KT, SEQ])
    r_gate = r("r_gate", [P, KT, SEQ])
    r = Region(Y0, M0)
    r_s = r("r_s", [P, KT, SEQ])
    r_q = r("r_q", [P, KT, SEQ])
    r_lam = nc.alloc_sbuf_tensor_at("r_lam", [P, 6, KT], F32, offset=LAM_AT)

    def rec_pe(pe, s):
        first_units(pe, U_REC, x_hi, x_lo, SEQ, lambda k: pe.wait_ge(x_ready, KT * (s + 1) + k + 1))
        for u in range(U_REC + FIRST, U_REC + KT):
            unit(pe, u, x_hi, x_lo, SEQ)
        for b in range(GATES):
            u = U_GATES + b
            pe.wait_ge(lo_ready, u + 1)
            pe.wait_ge(drained[u % BANKS], u // BANKS)
            if b >= 2:
                pe.wait_ge(flag("gate_i_read"), b - 1)
            pe.wait_ge(flag("r_ready"), 2 * b + 2)
            for g, dst in enumerate((bank(u % BANKS), bank(4 + b % 2))):
                for m in range(2):
                    o = dst[:, m * SEQ:(m + 1) * SEQ]
                    for k in range(2):
                        c = (g * 4 + m * 2 + k) * P
                        w_hi, w_lo = hi_ring[:, u % SPLIT_SLOTS, c:c + P], lo_ring[:, u % SPLIT_SLOTS, c:c + P]
                        nc.tensor.matmul(o, w_hi, r_hi[:, 2 * b + k, :], start=(k == 0), stop=False)
                        nc.tensor.matmul(o, w_hi, r_lo[:, 2 * b + k, :], start=False, stop=False)
                        last = nc.tensor.matmul(o, w_lo, r_hi[:, 2 * b + k, :], start=False, stop=(k == 1))
            last.then_inc(unit_done, 1)
        mods(pe, "gates")
        for u in range(U_RGELU, U_RGELU + KT):
            unit(pe, u, x_hi, x_lo, SEQ)
        mods(pe, "scan")
        first_units(pe, U_ROUT, x_hi, x_lo, SEQ, lambda k: pe.wait_ge(x_ready, KT * (s + 2) + k + 1))
        for u in range(U_ROUT + FIRST, U_ROUT + KT):
            unit(pe, u, x_hi, x_lo, SEQ)

    def rec_act(act, link, s):
        act.wait_ge(flag("lam_abs"), 1)
        exp_set()
        nc.scalar.activation(r_lam[:, 1, :], r_lam[:, 0, :], ACT.Exp).then_inc(flag("lam_exp"), 1)
        act.wait_ge(flag("pads_set"), 1)
        for k in range(KT + 1):
            if k < KT:
                u = U_REC + k
                wait_unit(act, u)
                nc.scalar.activation(r_pad[:, k, B_TAPS - 1:], bank(u % BANKS, SEQ), ACT.Copy).then_inc(drained[u % BANKS], 1)
            if k:
                act.wait_ge(flag("r_conv"), k)
                nc.scalar.activation(r_hi[:, k - 1, :], r_x[:, k - 1, :], ACT.Copy).then_inc(flag("r_hi_ready"), 1)
        for b in range(GATES):
            u = U_GATES + b
            wait_unit(act, u)
            for m in range(2):
                k = 2 * b + m
                other_set()
                last = nc.scalar.activation(r_t[:, k, :], bank(u % BANKS)[:, m * SEQ:(m + 1) * SEQ], ACT.Sigmoid, bias=pcol("b_a", k))
            last.then_inc(drained[u % BANKS], 1)
            for m in range(2):
                k = 2 * b + m
                other_set()
                last = nc.scalar.activation(r_i[:, k, :], bank(4 + b % 2)[:, m * SEQ:(m + 1) * SEQ], ACT.Sigmoid, bias=pcol("b_x", k))
            last.then_inc(flag("gate_i_read"), 1)
            act.wait_ge(flag("gate_i_read"), b + 1)
            act.wait_ge(flag("lam_ready"), 1)
            for k in (2 * b, 2 * b + 1):
                other_set()
                nc.scalar.activation(r_s[:, k, :], r_t[:, k, :], ACT.Tanh, scale=r_lam[:, 5, k:k + 1]).then_inc(flag("r_tanh"), 1)
        act.wait_ge(flag("r_tanh"), KT)
        for k in range(KT):
            exp_set()
            nc.scalar.activation(r_t[:, k, :], r_t[:, k, :], ACT.Exp, scale=r_lam[:, 4, k:k + 1]).then_inc(flag("r_decay"), 1)
        for h in range(2):
            c = slice(4 * h, 4 * h + 4)
            other_set()
            nc.scalar.activation(r_s[:, c, :], r_s[:, c, :], ACT.Sqrt, scale=-1.0).then_inc(flag("r_sqrt"), 1)
        for k in range(KT):
            u = U_RGELU + k
            wait_unit(act, u)
            other_set()
            nc.scalar.activation(r_gate[:, k, :], bank(u % BANKS, SEQ), ACT.Gelu_apprx_tanh).then_inc(drained[u % BANKS], 1)
        split_act(act, s + 1, SEQ, r_q)

    def rec_dve(dve, link, s):
        nc.vector.memset(r_pad[:, :, 0:B_TAPS - 1], 0.0).then_inc(flag("pads_set"), 1)
        dve.wait_ge(flag("pads_set"), 1)
        lam = pcol("lam", 0, KT)
        nc.vector.scalar_tensor_tensor(r_lam[:, 0, :], lam, -1.0, lam, ALU.mult, ALU.min).then_inc(flag("lam_abs"), 1)
        dve.wait_ge(flag("lam_exp"), 1)
        log1p_series(link, r_lam[:, 1, :], r_lam[:, 2, :], r_lam[:, 3, :], r_lam[:, 4, :])
        link(nc.vector.tensor_scalar(r_lam[:, 0, :], lam, -1.0, 0.0, ALU.mult, ALU.max))
        link(nc.vector.scalar_tensor_tensor(r_lam[:, 2, :], r_lam[:, 4, :], 2.0, r_lam[:, 0, :], ALU.mult, ALU.add))
        link(nc.vector.tensor_scalar(r_lam[:, 4, :], r_lam[:, 2, :], -8.0, None, ALU.mult))
        nc.vector.tensor_scalar(r_lam[:, 5, :], r_lam[:, 2, :], -4.0, None, ALU.mult).then_inc(flag("lam_ready"), 1)

        def lo(k):
            dve.wait_ge(flag("r_hi_ready"), k + 1)
            nc.vector.tensor_tensor(r_lo[:, k, :], r_x[:, k, :], r_hi[:, k, :].bitcast(F32), ALU.subtract).then_inc(flag("r_ready"), 1)

        for k in range(KT):
            u = U_REC + k
            wait_drained(dve, u)
            tap = lambda j: pcol("rec_conv", k * B_TAPS + j)
            link(nc.vector.tensor_scalar(r_x[:, k, :], r_pad[:, k, 0:SEQ], tap(0), pcol("rec_conv_b", k), ALU.mult, ALU.add))
            for j in range(1, B_TAPS):
                last = nc.vector.scalar_tensor_tensor(r_x[:, k, :], r_pad[:, k, j:j + SEQ], tap(j), r_x[:, k, :], ALU.mult, ALU.add)
                if j < B_TAPS - 1:
                    link(last)
            last.then_inc(flag("r_conv"), 1)
            if k:
                lo(k - 1)
            next_lo(dve, u)
        lo(KT - 1)
        for b in range(GATES):
            next_lo(dve, U_GATES + b)
        turns = list(range(U_GATES + GATES, U_ROUT))

        def pass_units(n):
            for _ in range(min(n, len(turns))):
                u = turns.pop(0)
                (pass_mod if u in MOD_INDEX else next_lo)(dve, u)

        for k in range(KT):
            dve.wait_ge(flag("gate_i_read"), k // 2 + 1)
            link(nc.vector.tensor_tensor(r_i[:, k, :], r_i[:, k, :], r_x[:, k, :], ALU.mult))
            pass_units(1)
        for k in range(KT):
            dve.wait_ge(flag("r_decay"), k + 1)
            dve.wait_ge(flag("r_sqrt"), k // 4 + 1)
            link(nc.vector.scalar_tensor_tensor(r_s[:, k, :], r_t[:, k, :], 1.0, r_s[:, k, :], ALU.add, ALU.mult))
            link(nc.vector.tensor_tensor(r_s[:, k, :], r_s[:, k, :], r_i[:, k, :], ALU.mult))
            link(nc.vector.tensor_tensor_scan(r_q[:, k, :], r_t[:, k, :], r_s[:, k, :], 0.0, ALU.mult, ALU.add))
            pass_units(3)
        for k in range(KT):
            wait_drained(dve, U_RGELU + k)
            nc.vector.tensor_tensor(r_q[:, k, :], r_q[:, k, :], r_gate[:, k, :], ALU.mult).then_inc(flag("normed_f32"), 1)
        for k in range(KT):
            if k == 0:
                wait_unit(dve, U_RGELU + KT - 1)
            split_dve(dve, s + 1, k, SEQ, r_q)
            pass_units(1)
        assert not turns
        for k in range(KT):
            u = U_ROUT + k
            wait_unit(dve, u)
            nc.vector.scalar_tensor_tensor(y[:, k, 0:SEQ], x[:, k, 0:SEQ], ALPHA, bank(u % BANKS, SEQ), ALU.mult,
                                           ALU.add).then_inc(drained[u % BANKS], 1)
            next_lo(dve, u)

    PAD = CONF_K // 2
    r = Region(M0, END)
    c_conf = r("c_conf", [P, 2, TB])
    c_u_at = r.at
    c_u = r("c_u", [P, 2, 2, SEQ + 2 * PAD])
    c_sc = r("c_sc", [P, 2, TB])
    c_ch = r("c_ch", [P, 2, 2, SEQ + 2])
    c_b = r("c_b", [P, 2, TB])
    c_K = r("c_K", [P, HEADS, TB])
    c_Q_at = r.at
    c_Q = r("c_Q", [P, HEADS, TB])
    c_att_sq = Region(c_Q_at, END)("c_att_sq", [P, 4, TB])
    c_sq = Region(c_u_at, END)("c_sq", [P, 2, TB])
    r = Region(Y0, M0)
    c_kv = r("c_kv", [P, TB])
    c_kr = r("c_kr", [P, TB])
    c_q = r("c_q", [P, 2, TB])
    c_o = r("c_o", [P, 4, TB])
    r = Region(X0, X0 + 2 * KT * TB * 4)
    c_qh = r("c_qh", [P, 2, TB], F32R)
    c_ql = r("c_ql", [P, 2, TB], F32R)
    c_kh = r("c_kh", [P, TB], F32R)
    c_kl = r("c_kl", [P, TB], F32R)
    c_v = r("c_v", [P, 4, TB])
    c_pT = r("c_pT", [P, 2, 2 * TB])
    c_stat = r("c_stat", [P, TB])
    c_rstd = r("c_rstd", [P, TB])
    c_p = Region(X0, X0 + 4 * TB * 4)("c_p", [P, 2, 2, TB])
    c_soft = nc.alloc_sbuf_tensor_at("c_soft", [P, 4, 32], F32, offset=SOFT_AT)
    c_sq3 = Region(Y0 + 4 * TB * 4, M0)("c_sq3", [P, 3, TB])
    CONF_TAPS = [(i, j) for i in range(2) for j in range(CONF_K)]
    ORDER = ["g0", "a0", "g1", "a1", "kv", "kr", "q0", "q1", "c0", "h0", "c1", "h1", "b0", "b1"]
    KV_SUM, Q_SUM = 6, 9

    STEPS = ["conf_mean", "center", "sums", "rstd", "silu", "again", "last"]

    class Layer:

        def __init__(self, l):
            self.l = l
            self.base = U_L2 + l * L2_UNITS
            self.T = TB if l == 0 else SEQ
            self.S = self.T // SEQ
            self.split = 4 + 3 * l
            self.norm = 4 + 4 * l
            self.updated = KT + 2 * KT * l
            self.heads = [(st, h) for st in range(self.S) for h in range(HEADS)]
            self.at = 0 if l == 0 else 2 * HEADS
            self.hooks = dict(zip(range(8, 15) if l == 0 else range(2, 9), STEPS))
            self.taps = 4 if l == 0 else 8
            self.jobs = 2 * HEADS + 4

        def width(self, name):
            return TB if name in ("kv", "kr") else self.T


    def l2_pe(pe, L):
        l, T, S = L.l, L.T, L.S
        assert all(L.width(name) == T for name in ORDER[:FIRST])
        first_units(pe, L.base, x_hi, x_lo, T, lambda k: pe.wait_ge(x_ready, KT * (L.split + 1) + k + 1))
        for j, name in enumerate(ORDER):
            if j >= FIRST:
                unit(pe, L.base + j, x_hi, x_lo, L.width(name))
            if j == KV_SUM:
                pe.wait_ge(flag("kvq_sq"), 3 * l + 1)
                nc.tensor.matmul(bank(4, TB), ones[:, :], c_sq3[:, 0, :], start=True, stop=True).then_inc(flag("kv_sum"), 1)
                wait_drained(pe, L.base + ORDER.index("kr"))
                nc.tensor.matmul(psum[0:QK, 6, 0:SEQ], sc("rot2")[0:QK, 0:QK], c_kr[0:QK, 0:SEQ], start=True,
                                 stop=True).then_inc(flag("kr_rot"), 1)
            if j == Q_SUM:
                pe.wait_ge(flag("kvq_sq"), 3 * l + 3)
                nc.tensor.matmul(bank(5, T), ones[:, :], c_sq3[:, 1, 0:T], start=True, stop=False)
                nc.tensor.matmul(bank(5, T), ones[:, :], c_sq3[:, 2, 0:T], start=False, stop=True).then_inc(flag("q_sum"), 1)
        for u in range(L.base + L2_IN - BANKS, L.base + L2_IN):
            wait_drained(pe, u)
        job = L.jobs * l

        def place(j):
            if j >= job + BANKS:
                pe.wait_ge(flag("job_read"), j - BANKS + 1)
            return psum[:, j % BANKS, :]

        u = L.base + L2_IN
        s = u % SPLIT_SLOTS
        pe.wait_ge(lo_ready, u + 1)
        pe.wait_ge(flag("kv_split"), l + 1)
        for h in range(HEADS):
            o = place(job + h)[0:NOPE, 0:TB]
            w_hi, w_lo = (ring[:, s, h * NOPE:(h + 1) * NOPE] for ring in (hi_ring, lo_ring))
            nc.tensor.matmul(o, w_hi, c_kh[:, :], start=True, stop=False)
            nc.tensor.matmul(o, w_hi, c_kl[:, :], start=False, stop=False)
            nc.tensor.matmul(o, w_lo, c_kh[:, :], start=False, stop=True).then_inc(flag("job_done"), 1)
        for t in range(4):
            o = place(job + HEADS + t)
            c = slice(t * P, (t + 1) * P)
            w_hi, w_lo = (ring[:, s, 512:1024] for ring in (hi_ring, lo_ring))
            nc.tensor.matmul(o, c_kh[:, c], w_hi, start=True, stop=False)
            nc.tensor.matmul(o, c_kh[:, c], w_lo, start=False, stop=False)
            nc.tensor.matmul(o, c_kl[:, c], w_hi, start=False, stop=True).then_inc(unit_done if t == 3 else flag("job_done"), 1)
        for half in range(2):
            u = L.base + L2_IN + 1 + half
            s = u % SPLIT_SLOTS
            pe.wait_ge(lo_ready, u + 1)
            pe.wait_ge(flag("q_split"), 2 * l + 2)
            for h in range(4):
                o = place(job + HEADS + 4 + 4 * half + h)[0:QK, 0:T]
                for k in range(2):
                    c = (2 * h + k) * QK
                    w_hi, w_lo = hi_ring[:, s, c:c + QK], lo_ring[:, s, c:c + QK]
                    nc.tensor.matmul(o, w_hi, c_qh[:, k, 0:T], start=(k == 0), stop=False)
                    nc.tensor.matmul(o, w_hi, c_ql[:, k, 0:T], start=False, stop=False)
                    last = nc.tensor.matmul(o, w_lo, c_qh[:, k, 0:T], start=False, stop=(k == 1))
                last.then_inc(unit_done if h == 3 else flag("job_done"), 1)
        pe.wait_ge(flag("K_ready"), l + 1)
        for g in range(2):
            for h in range(4):
                pe.wait_ge(flag("job_read"), L.jobs * (l + 1) - HEADS + 4 * g + h + 1)
                last = nc.tensor.matmul(psum[0:QK, 4 + 2 * g + h // 2, (h % 2) * SEQ:(h % 2 + 1) * SEQ], sc("rot2")[0:QK, 0:QK],
                                        c_Q[0:QK, 4 * g + h, 0:SEQ], start=True, stop=True)
            last.then_inc(flag("q_rot"), 1)
        pe.wait_ge(flag("q_rotated"), 2 * l + 1)
        pe.wait_ge(flag("K_ready"), l + 1)

        def keys(st):
            return (0, 4) if st == 0 else (2, 2)

        def scores(i):
            st, h = L.heads[i]
            first, n = keys(st)
            if i == 4:
                pe.wait_ge(flag("q_rotated"), 2 * l + 2)
            if i >= 2:
                pe.wait_ge(flag("p_exp"), 2 * (L.at + i - 1))
            for b in range(2):
                q = c_Q[0:QK, h, st * SEQ + b * P:st * SEQ + (b + 1) * P]
                last = nc.tensor.matmul(psum[:, 2 * (i % 2) + b, 0:n * P], q, c_K[0:QK, h, first * P:(first + n) * P], start=True, stop=True)
            last.then_inc(flag("s_ps"), 1)

        def turned(i):
            n = keys(L.heads[i][0])[1]
            if i:
                pe.wait_ge(flag("pT_ready"), L.at + i)
            pe.wait_ge(flag("p_ready"), L.at + i + 1)
            for k in range(n):
                for b in range(2):
                    last = nc.tensor.transpose(cells(4, 8, P)[:, 2 * k + b, :], c_p[:, i % 2, b, k * P:(k + 1) * P], ident)
            last.then_inc(flag("pT_ps"), 1)

        def out_of(i):
            st, h = L.heads[i]
            first, n = keys(st)
            if i == 0:
                pe.wait_ge(flag("q_rotated"), 2 * l + 2)
            if i % 2 == 0 and i:
                pe.wait_ge(flag("o_heads_read"), L.at // 2 + i // 2)
            pe.wait_ge(flag("pT_ready"), L.at + i + 1)
            r0 = (h % 2) * DV
            o = psum[r0:r0 + DV, 6, 0:SEQ]
            for k in range(n):
                last = nc.tensor.matmul(o, c_v[:, first + k, h * DV:(h + 1) * DV], c_pT[:, i % 2, k * SEQ:(k + 1) * SEQ],
                                        start=(k == 0), stop=(k == n - 1))
            last.then_inc(flag("o_head"), 1)

        def branch_pe(step):
            if step == "conf_mean":
                pe.wait_ge(flag("branches_done"), l + 1)
                for i in range(2):
                    last = nc.tensor.matmul(bank(7, T), ones[:, :], c_conf[:, i, 0:T], start=(i == 0), stop=(i == 1))
                last.then_inc(flag("conf_mean_ps"), 1)
            if step in ("sums", "again"):
                n = 3 * l + (1 if step == "sums" else 3)
                if step == "again":
                    pe.wait_ge(flag("sc_rstd"), l + 1)
                pe.wait_ge(flag("branch_sq"), n)
                for i in range(2):
                    last = nc.tensor.matmul(bank(7, T), ones[:, :], c_sq[:, i, 0:T], start=(i == 0), stop=(i == 1))
                last.then_inc(flag("branch_sum"), 1)
            if step == "rstd":
                pe.wait_ge(flag("branch_sq"), 3 * l + 2)
                pe.wait_ge(flag("branch_rstd"), 2 * l + 1)
                for i in range(2):
                    last = nc.tensor.matmul(bank(7, T), ones[:, :], c_b[:, i, 0:T], start=(i == 0), stop=(i == 1))
                last.then_inc(flag("sc_sum"), 1)

        scores(0)
        scores(1)
        for i in range(len(L.heads)):
            if i in L.hooks:
                branch_pe(L.hooks[i])
            turned(i)
            if i + 2 < len(L.heads):
                scores(i + 2)
            if i:
                out_of(i - 1)
        out_of(len(L.heads) - 1)
        if len(L.heads) in L.hooks:
            branch_pe(L.hooks[len(L.heads)])
        for i in range(4):
            pe.wait_ge(flag("attn_sq"), 4 * l + i + 1)
            last = nc.tensor.matmul(bank(6, T), ones[:, :], c_att_sq[:, i, 0:T], start=(i == 0), stop=(i == 3))
        last.then_inc(flag("attn_sum"), 1)
        out = L.base + L2_IN + 3
        first_units(pe, out, x_hi, x_lo, T, lambda k: pe.wait_ge(x_ready, KT * (L.split + 2) + k + 1))
        for u in range(out + FIRST, out + KT):
            unit(pe, u, x_hi, x_lo, T)

    def l2_act(act, link, L):
        l, T, S = L.l, L.T, L.S
        for j, name in enumerate(ORDER):
            u = L.base + j
            i = int(name[1]) if name[1] in "01" else 0
            if j in (KV_SUM + 1, Q_SUM + 1):
                which = "kv" if j == KV_SUM + 1 else "q"
                W, b, n = (TB, 4, P) if which == "kv" else (T, 5, 2 * P)
                act.wait_ge(flag(which + "_sum"), l + 1)
                if which == "q":
                    act.wait_ge(flag("kvq_normed"), 3 * l + 1)
                exp_set()
                link(nc.scalar.activation(stat[:, 0:W], bank(b, W), ACT.Ln, bias=eps[:, 1:2], scale=1.0 / n))
                exp_set()
                nc.scalar.activation(rstd[:, 0:W], stat[:, 0:W], ACT.Exp, scale=-0.5).then_inc(flag("kvq_rstd"), 1)
            if name[0] in "ah":
                continue
            wait_unit(act, u)
            W = L.width(name)
            dst, f = {"g": (c_conf[:, i, 0:W], ACT.Sigmoid), "c": (c_sc[:, i, 0:W], ACT.Copy), "b": (c_b[:, i, 0:W], ACT.Copy),
                      "q": (c_q[:, i, 0:W], ACT.Copy), "k": ((c_kv if name == "kv" else c_kr)[:, 0:W], ACT.Copy)}[name[0]]
            if name in ("kv", "q0", "q1"):
                n = ("kv", "q0", "q1").index(name)
                nc.scalar.activation(c_sq3[:, n, 0:W], bank(u % BANKS, W), ACT.Square).then_inc(flag("kvq_sq"), 1)
            if f == ACT.Sigmoid:
                other_set()
            nc.scalar.activation(dst, bank(u % BANKS, W), f).then_inc(drained[u % BANKS], 1)
        wait_unit(act, L.base + L2_IN - 1)
        act.wait_ge(flag("kvq_normed"), 3 * l + 1)
        nc.scalar.activation(c_kh[:, :], c_kv[:, :], ACT.Copy).then_inc(flag("kvq_hi"), 1)
        for k in range(2):
            act.wait_ge(flag("kvq_normed"), 3 * l + 2 + k)
            nc.scalar.activation(c_qh[:, k, 0:T], c_q[:, k, 0:T], ACT.Copy).then_inc(flag("kvq_hi"), 1)
        for j in range(L.jobs):
            ends = (HEADS + 3, HEADS + 7, HEADS + 11)
            if j in ends:
                wait_unit(act, L.base + L2_IN + ends.index(j))
            else:
                act.wait_ge(flag("job_done"), (L.jobs - 3) * l + j + 1 - sum(j > e for e in ends))
            src = psum[:, j % BANKS, :]
            if j < HEADS:
                args = c_K[0:NOPE, j, :], src[0:NOPE, 0:TB]
            elif j < HEADS + 4:
                args = c_v[:, j - HEADS, :], src
            else:
                args = c_Q[0:QK, j - HEADS - 4, 0:T], src[0:QK, 0:T]
            nc.scalar.activation(*args, ACT.Copy).then_inc(flag("job_read"), 1)
        act.wait_ge(flag("job_read"), L.jobs * (l + 1))
        for i in range(3):
            act.sem_inc(drained[(L.base + L2_IN + i) % BANKS], 1)

        def exp(i):
            n = 4 if L.heads[i][0] == 0 else 2
            act.wait_ge(flag("s_max"), L.at + i + 1)
            if i >= 2:
                act.wait_ge(flag("pT_ps"), L.at + i - 1)
            for b in range(2):
                c = slice(2 * i + b, 2 * i + b + 1)
                exp_set()
                nc.scalar.activation(c_p[:, i % 2, b, 0:n * P], psum[:, 2 * (i % 2) + b, 0:n * P], ACT.Exp, bias=c_soft[:, 1, c],
                                     scale=SM_SCALE, accum_out=c_soft[:, 2, c]).then_inc(flag("p_exp"), 1)

        def branch_act(step):
            if step == "center":
                for i in range(2):
                    act.wait_ge(flag("conf_centered"), 2 * l + i + 1)
                    last = nc.scalar.activation(c_sq[:, i, 0:T], c_conf[:, i, 0:T], ACT.Square)
                last.then_inc(flag("branch_sq"), 1)
                act.wait_ge(flag("sc_done"), l + 1)
                nc.scalar.activation(c_b[:, :, 0:T], c_sc[:, :, 0:T], ACT.Square).then_inc(flag("branch_sq"), 1)
            if step in ("rstd", "last"):
                act.wait_ge(flag("branch_sum"), 2 * l + (1 if step == "rstd" else 2))
                exp_set()
                link(nc.scalar.activation(stat[:, 0:T], bank(7, T), ACT.Ln, bias=eps[:, 1:2], scale=1.0 / (2 * P)))
                exp_set()
                nc.scalar.activation(rstd[:, 0:T], stat[:, 0:T], ACT.Exp, scale=-0.5).then_inc(flag("branch_rstd"), 1)
            if step == "rstd":
                act.wait_ge(flag("sc_sum"), l + 1)
                exp_set()
                link(nc.scalar.activation(c_stat[:, 0:T], bank(7, T), ACT.Ln, bias=eps[:, 1:2], scale=1.0 / (2 * P)))
                exp_set()
                nc.scalar.activation(c_rstd[:, 0:T], c_stat[:, 0:T], ACT.Exp, scale=-0.5).then_inc(flag("sc_rstd"), 1)
            if step == "silu":
                for i in range(2):
                    act.wait_ge(flag("conf_scaled"), 2 * l + i + 1)
                    other_set()
                    link(nc.scalar.activation(c_conf[:, i, 0:T], c_conf[:, i, 0:T], ACT.Silu, scale=pcol("conf_g", 2 * l + i),
                                              bias=pcol("conf_beta", 2 * l + i)))
                    last = nc.scalar.activation(c_sq[:, i, 0:T], c_conf[:, i, 0:T], ACT.Square)
                last.then_inc(flag("branch_sq"), 1)

        exp(0)
        exp(1)
        for i in range(len(L.heads)):
            if i in L.hooks:
                branch_act(L.hooks[i])
            n = 4 if L.heads[i][0] == 0 else 2
            act.wait_ge(flag("pT_ps"), L.at + i + 1)
            if i >= 2:
                act.wait_ge(flag("o_head"), L.at + i - 1)
            nc.scalar.activation(c_pT[:, i % 2, 0:n * SEQ], cells(4, 8, P)[:, 0:2 * n, :].rearrange("p a b -> p (a b)"),
                                 ACT.Copy).then_inc(flag("pT_ready"), 1)
            if i + 2 < len(L.heads):
                exp(i + 2)
        if len(L.heads) in L.hooks:
            branch_act(L.hooks[len(L.heads)])
        for i in range(4):
            act.wait_ge(flag("o_heads_read"), (L.at + len(L.heads)) // 2)
            nc.scalar.activation(c_att_sq[:, i, 0:T], c_o[:, i, 0:T], ACT.Square).then_inc(flag("attn_sq"), 1)
        act.wait_ge(flag("attn_sum"), l + 1)
        act.wait_ge(flag("branch_normed"), 4 * (l + 1))
        exp_set()
        link(nc.scalar.activation(stat[:, 0:T], bank(6, T), ACT.Ln, bias=eps[:, 1:2], scale=1.0 / (4 * P)))
        exp_set()
        nc.scalar.activation(rstd[:, 0:T], stat[:, 0:T], ACT.Exp, scale=-0.5).then_inc(flag("attn_rstd"), 1)
        for k in range(KT):
            act.wait_ge(flag("normed_f32"), KT * (L.split + 1) + k + 1)
            nc.scalar.activation(x_hi[:, k, 0:T], merged(k, T), ACT.Copy).then_inc(split_hi, 1)
        for k in range(KT):
            u = L.base + L2_IN + 3 + k
            wait_unit(act, u)
            nc.scalar.activation(y[:, k, 0:T], bank(u % BANKS, T), ACT.Copy).then_inc(flag("y_ready"), 1)
            nc.scalar.activation(sq[:, k, 0:T], bank(u % BANKS, T), ACT.Square).then_inc(flag("norm_sq"), 1)
            act.wait_ge(flag("y_ready"), KT * l + k + 1)
            act.wait_ge(flag("norm_sq"), KT * (L.norm + 1) + k + 1)
            act.sem_inc(drained[u % BANKS], 1)

    def merged(k, T):
        return c_o[:, k, 0:T] if k < 4 else (c_conf[:, k - 4, 0:T] if k < 6 else c_sc[:, k - 6, 0:T])

    tap_done = []

    def l2_dve(dve, link, L):
        l, T, S = L.l, L.T, L.S
        link(nc.vector.memset(c_u[:, :, :, 0:PAD], 0.0))
        link(nc.vector.memset(c_u[:, :, :, PAD + SEQ:], 0.0))
        link(nc.vector.memset(c_ch[:, :, :, 0:1], 0.0))
        link(nc.vector.memset(c_ch[:, :, :, SEQ + 1:], 0.0))
        if l:
            dve.wait_ge(flag("norm_sum"), L.norm + 1)

        def split(ap):
            return ap.rearrange("p (s t) -> p s t", s=S)

        R = slice(NOPE, QK)
        cos2, sin2 = sc("cos2", SEQ)[R, :], sc("sin2", SEQ)[R, :]
        taps = []

        def conf_tap(i, j):
            acc, src = split(c_conf[:, i, 0:T]), c_u[:, i, 0:S, j:j + SEQ]
            w = pcol("conf_w", (2 * l + i) * CONF_K + j)
            if j == 0:
                return nc.vector.tensor_scalar(acc, src, w, pcol("conf_b", 2 * l + i), ALU.mult, ALU.add)
            return nc.vector.scalar_tensor_tensor(acc, src, w, acc, ALU.mult, ALU.add)

        def sc_tap(i, j):
            acc, src = split(c_sc[:, i, 0:T]), c_ch[:, i, 0:S, j:j + SEQ]
            w = pcol("sc_w", (2 * l + i) * SC_K + j)
            if j == 0:
                return nc.vector.tensor_scalar(acc, src, w, None, ALU.mult)
            return nc.vector.scalar_tensor_tensor(acc, src, w, acc, ALU.mult, ALU.add)

        tap_of = {}

        def do_taps(n):
            for _ in range(min(n, len(taps))):
                f, i, j = taps.pop(0)
                other = next((q for q, t in enumerate(taps) if t[:2] != (f, i)), 0)
                if taps:
                    taps.insert(0, taps.pop(other))
                if (f, i) in tap_of:
                    dve.wait_ge(flag("taps"), tap_of[f, i])
                tap_done.append(0)
                tap_of[f, i] = len(tap_done)
                f(i, j).then_inc(flag("taps"), 1)

        for j, name in enumerate(ORDER):
            u = L.base + j
            i = int(name[1]) if name[1] in "01" else 0
            if name[0] in "ah":
                wait_drained(dve, u - 1)
                wait_unit(dve, u)
                src = split(bank(u % BANKS, T))
                if name[0] == "a":
                    nc.vector.tensor_tensor(c_u[:, i, 0:S, PAD:PAD + SEQ], src, split(c_conf[:, i, 0:T]),
                                            ALU.mult).then_inc(drained[u % BANKS], 1)
                    wait_drained(dve, u)
                    taps.extend((conf_tap, i, k) for k in range(CONF_K))
                else:
                    nc.vector.tensor_tensor(c_ch[:, i, 0:S, 1:1 + SEQ], src, split(c_sc[:, i, 0:T]),
                                            ALU.mult).then_inc(drained[u % BANKS], 1)
                    wait_drained(dve, u)
                    taps.extend((sc_tap, i, k) for k in range(SC_K))
            next_lo(dve, u)
            if j == KV_SUM + 2:
                dve.wait_ge(flag("kvq_rstd"), 2 * l + 1)
                wait_drained(dve, L.base + ORDER.index("kv"))
                nc.vector.scalar_tensor_tensor(c_kv[:, :], c_kv[:, :], pcol("g_kv", l), rstd[:, :], ALU.mult,
                                               ALU.mult).then_inc(flag("kvq_normed"), 1)
                dve.wait_ge(flag("kr_rot"), l + 1)
                rot = normed[R, 0, 0:SEQ]
                link(nc.vector.tensor_tensor(rot, psum[R, 6, 0:SEQ], sin2, ALU.mult))
                link(nc.vector.tensor_tensor(c_kr[R, 0:SEQ], c_kr[R, 0:SEQ], cos2, ALU.mult))
                link(nc.vector.tensor_tensor(c_kr[R, 0:SEQ], c_kr[R, 0:SEQ], rot, ALU.add))
                nc.vector.tensor_copy(c_K[R, :, :], c_kr[R, :].unsqueeze(1).broadcast_to([QK - NOPE, HEADS, TB])).then_inc(flag("K_ready"), 1)
            if j == Q_SUM + 3:
                dve.wait_ge(flag("kvq_rstd"), 2 * l + 2)
                wait_drained(dve, L.base + ORDER.index("q1"))
                for k in range(2):
                    nc.vector.scalar_tensor_tensor(c_q[:, k, 0:T], c_q[:, k, 0:T], pcol("g_q", 2 * l + k), rstd[:, 0:T], ALU.mult,
                                                   ALU.mult).then_inc(flag("kvq_normed"), 1)
            elif j < L2_IN - 1:
                do_taps(4)
        dve.wait_ge(flag("kvq_hi"), 3 * l + 1)
        nc.vector.tensor_tensor(c_kl[:, :], c_kv[:, :], c_kh[:, :].bitcast(F32), ALU.subtract).then_inc(flag("kv_split"), 1)
        for k in range(2):
            dve.wait_ge(flag("kvq_hi"), 3 * l + 2 + k)
            nc.vector.tensor_tensor(c_ql[:, k, 0:T], c_q[:, k, 0:T], c_qh[:, k, 0:T].bitcast(F32), ALU.subtract).then_inc(flag("q_split"), 1)
        for i in range(3):
            next_lo(dve, L.base + L2_IN + i)
            do_taps(6)

        def top(i):
            n = 4 if L.heads[i][0] == 0 else 2
            dve.wait_ge(flag("s_ps"), L.at + i + 1)
            two = slice(2 * i, 2 * i + 2)
            link(nc.vector.tensor_reduce(c_soft[:, 0, two], psum[:, 2 * (i % 2):2 * (i % 2) + 2, 0:n * P], AX.X, ALU.max))
            nc.vector.tensor_scalar(c_soft[:, 1, two], c_soft[:, 0, two], -SM_SCALE, None, ALU.mult).then_inc(flag("s_max"), 1)

        def normalised(i):
            n = 4 if L.heads[i][0] == 0 else 2
            dve.wait_ge(flag("p_exp"), 2 * (L.at + i + 1))
            link(nc.vector.reciprocal(c_soft[:, 3, 2 * i:2 * i + 2], c_soft[:, 2, 2 * i:2 * i + 2]))
            for b in range(2):
                last = nc.vector.tensor_scalar(c_p[:, i % 2, b, 0:n * P], c_p[:, i % 2, b, 0:n * P],
                                               c_soft[:, 3, 2 * i + b:2 * i + b + 1], None, ALU.mult)
            last.then_inc(flag("p_ready"), 1)

        def pair_out(i):
            if i >= 0 and i % 2:
                st, h = L.heads[i]
                dve.wait_ge(flag("o_head"), L.at + i + 1)
                nc.vector.tensor_copy(c_o[:, h // 2, st * SEQ:(st + 1) * SEQ], bank(6, SEQ)).then_inc(flag("o_heads_read"), 1)

        def branch_dve(step):
            if step == "conf_mean":
                do_taps(len(taps))
                dve.wait_ge(flag("taps"), len(tap_done))
                dve.sem_inc(flag("branches_done"), 1)
            if step == "center":
                dve.wait_ge(flag("conf_mean_ps"), l + 1)
                for i in range(2):
                    nc.vector.scalar_tensor_tensor(c_conf[:, i, 0:T], bank(7, T), -1.0 / (2 * P), c_conf[:, i, 0:T], ALU.mult,
                                                   ALU.add).then_inc(flag("conf_centered"), 1)
                nc.vector.tensor_tensor(c_sc[:, :, 0:T], c_sc[:, :, 0:T], c_b[:, :, 0:T], ALU.mult).then_inc(flag("sc_done"), 1)
            if step == "silu":
                dve.wait_ge(flag("branch_rstd"), 2 * l + 1)
                for i in range(2):
                    nc.vector.tensor_tensor(c_conf[:, i, 0:T], c_conf[:, i, 0:T], rstd[:, 0:T], ALU.mult).then_inc(flag("conf_scaled"), 1)
                dve.wait_ge(flag("sc_rstd"), l + 1)
                for i in range(2):
                    nc.vector.scalar_tensor_tensor(c_sc[:, i, 0:T], c_sc[:, i, 0:T], pcol("g_branch", KT * l + 6 + i), c_rstd[:, 0:T],
                                                   ALU.mult, ALU.mult).then_inc(flag("branch_normed"), 1)
            if step == "last":
                dve.wait_ge(flag("branch_rstd"), 2 * l + 2)
                for i in range(2):
                    nc.vector.scalar_tensor_tensor(c_conf[:, i, 0:T], c_conf[:, i, 0:T], pcol("g_branch", KT * l + 4 + i), rstd[:, 0:T],
                                                   ALU.mult, ALU.mult).then_inc(flag("branch_normed"), 1)

        def rotate(g):
            dve.wait_ge(flag("q_rot"), 2 * l + g + 1)
            q = c_Q[R, 4 * g:4 * g + 4, 0:SEQ]
            turned = psum[R, 4 + 2 * g:6 + 2 * g, :].rearrange("p b c -> p (b c)").rearrange("p (h t) -> p h t", h=4)
            t = normed[R, :, :].rearrange("p a b -> p (a b)").rearrange("p (h t) -> p h t", h=4)
            four = lambda ap: ap.unsqueeze(1).broadcast_to([QK - NOPE, 4, SEQ])
            link(nc.vector.tensor_tensor(t, turned, four(sin2), ALU.mult))
            link(nc.vector.tensor_tensor(q, q, four(cos2), ALU.mult))
            link(nc.vector.tensor_tensor(q, q, t, ALU.add))
            dve.sem_inc(flag("q_rotated"), 1)

        rotate(0)
        top(0)
        top(1)
        normalised(0)
        rotate(1)
        for i in range(len(L.heads)):
            if i in L.hooks:
                branch_dve(L.hooks[i])
            if i + 1 < len(L.heads):
                normalised(i + 1)
            if i + 2 < len(L.heads):
                top(i + 2)
            pair_out(i - 1)
            do_taps(L.taps)
        pair_out(len(L.heads) - 1)
        if len(L.heads) in L.hooks:
            branch_dve(L.hooks[len(L.heads)])
        dve.wait_ge(flag("attn_rstd"), l + 1)
        for k in range(4):
            nc.vector.scalar_tensor_tensor(c_o[:, k, 0:T], c_o[:, k, 0:T], pcol("g_branch", KT * l + k), rstd[:, 0:T], ALU.mult,
                                           ALU.mult).then_inc(flag("normed_f32"), 1)
        for k in range(4):
            split_dve(dve, L.split + 1, k, T, c_o)
        dve.wait_ge(flag("branch_normed"), 4 * (l + 1))
        for k in range(4, KT):
            dve.sem_inc(flag("normed_f32"), 1)
        for k in range(4, KT):
            dve.wait_ge(split_hi, KT * (L.split + 2) + k + 1)
            nc.vector.tensor_tensor(x_lo[:, k, 0:T], merged(k, T), x_hi[:, k, 0:T].bitcast(F32), ALU.subtract).then_inc(x_ready, 1)
        for k in range(KT):
            u = L.base + L2_IN + 3 + k
            wait_unit(dve, u)
            next_lo(dve, u)

    def coef_dve(dve, link):
        copy_group(dve, MOD_UNITS // 2 - 1)
        dve.wait_ge(flag("group_copied"), MOD_UNITS // 2)
        for l in range(DEPTH):
            n = N_MOD * KT
            c = coef[:, l].rearrange("p m k s -> p (m k) s")
            sums = mod_sums[:, 4 * n * l:4 * n * (l + 1)].rearrange("p (m a s) -> p m a s", a=2, s=2)
            link(nc.vector.tensor_tensor(c, sums[:, :, 0], sums[:, :, 1], ALU.add))
            link(nc.vector.tensor_tensor(c, c, pcol("b_mod", n * l, n).unsqueeze(2).broadcast_to([P, n, 2]), ALU.add))
            for part, g in ((1, "g_pre_mix"), (4, "g_pre_mlp")):
                gain = pcol(g, KT * l, KT).unsqueeze(2).broadcast_to([P, KT, 2])
                link(nc.vector.scalar_tensor_tensor(coef[:, l, part], coef[:, l, part], 1.0, gain, ALU.add, ALU.mult))
            for part, g in ((2, "g_post_mix"), (5, "g_post_mlp")):
                gain = pcol(g, KT * l, KT).unsqueeze(2).broadcast_to([P, KT, 2])
                link(nc.vector.tensor_tensor(coef[:, l, part], coef[:, l, part], gain, ALU.mult))

    LAYERS = [Layer(l) for l in range(DEPTH)]

    with nc.Block() as block:

        @block.sync
        def _(sp):
            def first_turn(a, b):
                for s in range(a, b):
                    sp.dma_start(raw_ring[:, s, :], weights[s]).then_inc(raw_loaded[s], 16)

            sp.dma_start(x[:, :, 0:SEQ], xT_in).then_inc(x_loaded, 16)
            first_turn(0, 1)
            sp.dma_start(par[:, :], params_in).then_inc(par_loaded, 16)
            first_turn(1, 5)
            sp.dma_start(h_const[:, :], hyb_in).then_inc(hyb_loaded, 16)
            first_turn(5, 7)
            sp.dma_start(shared[:, :], shared_in).then_inc(shared_loaded, 16)
            first_turn(7, RAW_SLOTS)
            sp.dma_start(x[:, :, SEQ:TB], ctxT_in).then_inc(ctx_loaded, 16)

            def load(n, s, tail=None):
                sp.wait_ge(lo_ready, n - RAW_SLOTS + 1)
                src = weights[n] if isinstance(n, int) else weights[bass.ds(n, 1)].rearrange("o p c -> (o p) c")
                sp.dma_start(raw_ring[:, s, :], src).then_inc(raw_loaded[s], 16)

            def load_units(a, b):
                while a < b and a % RAW_SLOTS:
                    load(a, a % RAW_SLOTS)
                    a += 1
                full = (b - a) // RAW_SLOTS
                if full > 1:
                    with sp.Fori(0, full) as i:
                        for s in range(RAW_SLOTS):
                            load(i * RAW_SLOTS + (a + s), s)
                    a += full * RAW_SLOTS
                for n in range(a, b):
                    load(n, n % RAW_SLOTS)

            load_units(RAW_SLOTS, LOADED)
            sp.wait_ge(flag("x_updated"), KT + 4 * KT)
            sp.dma_start(out, x[:, :, 0:SEQ]).then_inc(flag("stored"), 16)
            sp.wait_ge(flag("stored"), 16)

        @block.gpsimd
        def _(pool):
            def round_unit(s, loaded):
                pool.wait_ge(raw_loaded[s], loaded)
                pool.sem_inc(rounding, 1)
                nc.gpsimd.tensor_scalar(hi_ring[:, s % SPLIT_SLOTS, :], raw_ring[:, s, :], 1.0, 0.0, ALU.mult, ALU.add).then_inc(hi_ready, 1)

            for s in range(RAW_SLOTS):
                if s >= SPLIT_SLOTS:
                    pool.wait_ge(unit_done, s - SPLIT_SLOTS + 1)
                round_unit(s, 16)
            with pool.Fori(1, LOADED // RAW_SLOTS) as i:
                for s in range(RAW_SLOTS):
                    pool.wait_ge(unit_done, i * RAW_SLOTS + (s - SPLIT_SLOTS + 1))
                    round_unit(s, i * 16 + 16)

        @block.scalar
        def _(act):
            link = Link(act, act_step)
            hyb_act(act, link)
            squares_act(act, 0, SEQ, y, "centered", 0)
            norm_rstd_act(act, link, 0, SEQ, 0)
            split_act(act, 0, SEQ, x)
            mlp_act(act, 0, U_MLP1, SEQ)
            squares_act(act, 1, SEQ, y, "centered", KT)
            norm_rstd_act(act, link, 1, SEQ, 0)
            split_act(act, 1, SEQ, x)
            rec_act(act, link, 1)
            squares_act(act, 2, SEQ, y, "centered", 2 * KT)
            norm_rstd_act(act, link, 2, SEQ, 0)
            split_act(act, 3, SEQ, x)
            mlp_act(act, 1, U_MLP2, SEQ)
            squares_act(act, 3, SEQ, y, "centered", 3 * KT)
            norm_rstd_act(act, link, 3, SEQ, 0)
            act.wait_ge(ctx_loaded, 16)
            for L in LAYERS:
                squares_act(act, L.norm, TB, x, "x_updated", L.updated - KT)
                norm_rstd_act(act, link, L.norm, TB, 1)
                split_act(act, L.split, TB, y)
                l2_act(act, link, L)
                norm_rstd_act(act, link, L.norm + 1, L.T, 1)
                squares_act(act, L.norm + 2, L.T, x, "x_updated", L.updated)
                norm_rstd_act(act, link, L.norm + 2, L.T, 1)
                split_act(act, L.split + 2, L.T, y)
                base = L.base + L2_IN + 3 + KT
                mlp_act(act, 2 + L.l, base, L.T)
                for k in range(KT):
                    wait_drained(act, base + MLP_UNITS - KT + k)
                    nc.scalar.activation(sq[:, k, 0:L.T], y[:, k, 0:L.T], ACT.Square).then_inc(flag("norm_sq"), 1)
                norm_rstd_act(act, link, L.norm + 3, L.T, 1)

        @block.vector
        def _(dve):
            link = Link(dve, dve_step)
            hyb_dve(dve, link)
            layer_norm_dve(dve, link, 0, 0, "ln1_g", "ln1_b", 0)
            link(nc.vector.tensor_scalar(y[:, :, 0:SEQ], x[:, :, 0:SEQ], ALPHA, None, ALU.mult))
            mlp_dve(dve, 0, U_MLP1, SEQ)
            layer_norm_dve(dve, link, 1, 1, "ln2_g", "ln2_b", 1)
            rec_dve(dve, link, 1)
            layer_norm_dve(dve, link, 2, 2, "ln1_g", "ln1_b", 3)
            link(nc.vector.tensor_scalar(y[:, :, 0:SEQ], x[:, :, 0:SEQ], ALPHA, None, ALU.mult))
            mlp_dve(dve, 1, U_MLP2, SEQ)
            layer_norm_dve(dve, link, 3, 3, "ln2_g", "ln2_b", None)
            coef_dve(dve, link)
            for L in LAYERS:
                modulated_dve(dve, link, L.norm, TB, L.l, 0, L.split)
                l2_dve(dve, link, L)
                gated_dve(dve, link, L.norm + 1, L.T, L.l, 2)
                modulated_dve(dve, link, L.norm + 2, L.T, L.l, 3, L.split + 2)
                dve.wait_ge(x_ready, KT * (L.split + 4))
                link(nc.vector.memset(y[:, :, 0:L.T], 0.0))
                mlp_dve(dve, 2 + L.l, L.base + L2_IN + 3 + KT, L.T)
                gated_dve(dve, link, L.norm + 3, L.T, L.l, 5)

        @block.tensor
        def _(pe):
            hyb_pe(pe)
            norm_pe(pe, 0, SEQ, (0, U_HOUT))
            mlp_pe(pe, 0, U_MLP1, SEQ, 0)
            norm_pe(pe, 1, SEQ, (1, U_MLP1 + MLP_UNITS - KT))
            rec_pe(pe, 1)
            norm_pe(pe, 2, SEQ, (2, U_ROUT))
            mlp_pe(pe, 1, U_MLP2, SEQ, 3)
            norm_pe(pe, 3, SEQ, (3, U_MLP2 + MLP_UNITS - KT))
            for L in LAYERS:
                norm_pe(pe, L.norm, TB)
                l2_pe(pe, L)
                norm_pe(pe, L.norm + 1, L.T)
                norm_pe(pe, L.norm + 2, L.T)
                mlp_pe(pe, 2 + L.l, L.base + L2_IN + 3 + KT, L.T, L.split + 2)
                norm_pe(pe, L.norm + 3, L.T)


LOADED = (UNITS + LEAD + RAW_SLOTS - 1) // RAW_SLOTS * RAW_SLOTS


def _tiles(v):
    return np.asarray(v).reshape(-1, P).T


def _unit(w, rows, cols):
    part = w[rows, :][:, cols]
    return part.reshape(-1, P, part.shape[1]).transpose(1, 0, 2).reshape(P, -1)


def _column_units(w, start, count, rows=slice(0, D)):
    return [_unit(w, rows, slice(start + P * m, start + P * (m + 1))) for m in range(count)]


def _halves(w, cols):
    return [_unit(w, slice(h * D // 2, (h + 1) * D // 2), cols) for h in range(2)]


def _mlp_stream(w1, w2):
    out = []
    for q in range(QUARTERS):
        out += _column_units(w1, q * D, KT)
        out += _column_units(w2, 0, KT, slice(q * D, (q + 1) * D))
    return out


def _weight_stream(i):
    w = i["hyb_w_in"][0]
    qa = 8 * A_DH
    kb, qb, vb, z = 1280, 768, 1792, 2304
    s = _column_units(w, kb, 4) + _column_units(w, qb, 4) + _column_units(w, vb, 4)
    for t in range(4):
        heads = np.concatenate([w[:, t * A_DH:(t + 1) * A_DH], w[:, (t + 4) * A_DH:(t + 5) * A_DH]], axis=1)
        s += _column_units(heads, 0, 1)
    s += _column_units(w, qa, 2) + _column_units(w, z, 4)
    s += _column_units(i["hyb_w_out"][0], 0, KT)
    s += _mlp_stream(i["mlp_w1"][0], i["mlp_w2"][0])
    s += _column_units(i["rec_w_in"][0], 0, KT)
    for b in range(GATES):
        s.append(np.concatenate([_unit(i[name][0, b], slice(0, 2 * P), slice(m * P, (m + 1) * P))
                                 for name in ("rec_w_a", "rec_w_x") for m in range(2)], axis=1))
    s += _column_units(i["rec_w_in"][0], D, KT)
    s += _column_units(i["rec_w_out"][0], 0, KT)
    s += _mlp_stream(i["mlp_w1"][1], i["mlp_w2"][1])
    for l in range(DEPTH):
        w = i["w_in_2"][l]
        conf, sc = 416, 928
        kr = np.zeros((D, P), np.float32)
        kr[:, NOPE:QK] = w[:, 384:416]
        for t in range(2):
            s += _column_units(w, conf + 256 + t * P, 1) + _column_units(w, conf + t * P, 1)
        s += _column_units(w, 256, 1) + _column_units(kr, 0, 1) + _column_units(w, 0, 2)
        for t in range(2):
            s += _column_units(w, sc + 256 + t * P, 1) + _column_units(w, sc + 512 + t * P, 1)
        s += _column_units(w, sc, 2)
        kv = i["w_kv_b_2"][l].reshape(P, HEADS, NOPE + DV)
        s.append(np.concatenate([kv[:, :, :NOPE].reshape(P, -1), kv[:, :, NOPE:].reshape(P, -1)], axis=1))
        q = i["w_q_b_2"][l].reshape(2, P, HEADS, QK).transpose(1, 2, 0, 3)
        for half in range(2):
            part = np.zeros((P, D), np.float32)
            part[:, 0:8 * QK] = q[:, 4 * half:4 * half + 4].reshape(P, -1)
            s.append(part)
        s += _column_units(i["w_o_2"][l], 0, KT)
        s += _mlp_stream(i["w_mlp_in_2"][l], i["w_mlp_out_2"][l])
    main = iter(s)
    mod = [unit for l in range(DEPTH) for g in range(N_MOD * KT // 2)
           for unit in _halves(i["w_mod_2"][l], slice(2 * P * g, 2 * P * (g + 1)))]
    s = [mod[MOD_INDEX[u]] if u in MOD_INDEX else next(main) for u in range(UNITS)]
    assert next(main, None) is None
    return np.stack(s + [np.zeros((P, D), np.float32)] * (LOADED - UNITS))


def _params(i):
    bc = lambda v: np.broadcast_to(np.asarray(v).reshape(1, -1), (P, np.size(v)))
    conv = lambda w, order: np.asarray(w).reshape(w.shape[0], -1, P)[:, order].transpose(2, 1, 0).reshape(P, -1)
    both = lambda name: np.concatenate([_tiles(i[name][l]) for l in range(DEPTH)], axis=1)
    n12 = [4, 5, 6, 7, 0, 1, 2, 3, 8, 9, 10, 11]
    p = {
        "hyb_conv": conv(i["hyb_conv_w"][0], n12), "norm_w": _tiles(i["hyb_norm_w"][0]), "sinks": bc(i["hyb_sinks"][0]),
        "a_log": bc(i["hyb_a_log"][0]), "dt_bias": bc(i["hyb_dt_bias"][0]),
        "rec_conv": conv(i["rec_conv_w"][0], list(range(KT))), "rec_conv_b": _tiles(i["rec_conv_b"][0]),
        "b_a": _tiles(i["rec_b_a"][0]), "b_x": _tiles(i["rec_b_x"][0]), "lam": _tiles(i["rec_lambda"][0]),
        "ln1_g": both("ln1_g"), "ln1_b": both("ln1_b"), "ln2_g": both("ln2_g"), "ln2_b": both("ln2_b"),
        "cond": np.stack([_tiles(i["c_2"][0]), _tiles(i["c_ctx_2"])], axis=2).reshape(P, -1),
        "b_mod": both("b_mod_2"), "g_pre_mix": both("g_pre_mix_2"), "g_post_mix": both("g_post_mix_2"),
        "g_pre_mlp": both("g_pre_mlp_2"), "g_post_mlp": both("g_post_mlp_2"), "g_q": both("g_q_2"), "g_kv": both("g_kv_2"),
        "conf_w": np.concatenate([conv(i["conf_dw_w_2"][l], [0, 1]) for l in range(DEPTH)], axis=1),
        "conf_b": both("conf_dw_b_2"), "conf_g": both("conf_ln_g_2"), "conf_beta": both("conf_ln_b_2"),
        "sc_w": np.concatenate([conv(i["sc_dw_w_2"][l], [0, 1]) for l in range(DEPTH)], axis=1),
        "g_branch": both("g_branch_2"),
        "tail": _unit(i["hyb_w_in"][0], slice(0, D), slice(2816, 2824)),
    }
    for name, width in _PARAM_WIDTHS:
        assert p[name].shape == (P, width), (name, p[name].shape, width)
    return np.ascontiguousarray(np.concatenate([p[name] for name, _ in _PARAM_WIDTHS], axis=1))


def _constants():
    f = np.float32
    a = np.arange(P)
    half = A_DH // 2
    inv = (f(10000.0) ** (-np.arange(half, dtype=f) / f(half))).astype(f)
    ang = np.arange(SEQ, dtype=f)[None, :] * inv[a % half][:, None]
    rot1 = np.zeros((P, P), f)
    for to in range(P):
        if to % A_DH < half:
            rot1[to + half, to] = -1
        else:
            rot1[to - half, to] = 1
    j, i = a[:, None], a[None, :]
    up = []
    for s in DN_BLOCKS:
        up.append(((j // (2 * s) == i // (2 * s)) & (j % (2 * s) < s) & (i % (2 * s) >= s)).astype(f))
    window = np.zeros((P, 2 * P), f)
    window[:, 0:P][~(i > j)] = -1e30
    window[:, P:][~(i <= j)] = -1e30
    hyb = {"rot1": rot1, "tri": (j <= i).astype(f), "incl": (i <= j).astype(f), "low1": up[0].T, "up": np.concatenate(up, axis=1),
           "cos1": np.cos(ang), "sin1": np.sin(ang), "window": window}
    axis = (QK - NOPE) // 2
    inv = (f(1.0) / (f(10000.0) ** (np.arange(0, axis, 2, dtype=f) / f(axis)))).astype(f)
    t = np.arange(SEQ)
    cos2, sin2, rot2 = np.ones((P, SEQ), f), np.zeros((P, SEQ), f), np.zeros((P, P), f)
    for d in range(QK - NOPE):
        pos = (t // 64 if d < axis else t % 64).astype(f)
        angle = (pos * inv[d % (axis // 2)]).astype(f)
        cos2[NOPE + d], sin2[NOPE + d] = np.cos(angle), np.sin(angle)
        if d % axis < axis // 2:
            rot2[NOPE + d + axis // 2, NOPE + d] = -1
        else:
            rot2[NOPE + d - axis // 2, NOPE + d] = 1
    shared = {"ident": np.eye(P, dtype=f), "rot2": rot2, "cos2": cos2, "sin2": sin2}
    pack = lambda d, widths: np.ascontiguousarray(np.concatenate([d[n] for n, _ in widths], axis=1).astype(f))
    return pack(shared, _SHARED), pack(hyb, _HYB)


def _features_first(a):
    return np.ascontiguousarray(a.T.reshape(KT, P, -1).transpose(1, 0, 2))


def layout(inputs):
    i = {name: np.asarray(v) for name, v in inputs.items()}
    shared, hyb = _constants()
    return {"xT": _features_first(i["x"][0]), "ctxT": _features_first(i["ctx_2"][0]), "weights": _weight_stream(i),
            "params": _params(i), "shared_consts": shared, "hyb_consts": hyb}


def kernel(**inputs):
    import concourse.bacc as bacc
    from concourse.bass_utils import run_bass_kernel_spmd

    nc = bacc.Bacc("TRN2", target_bir_lowering=False, num_devices=1)
    arrays = layout(inputs)
    args = [nc.dram_tensor(name, a.shape, F32, kind="ExternalInput").ap() for name, a in arrays.items()]
    out = nc.dram_tensor("outT", (P, KT, SEQ), F32, kind="ExternalOutput").ap()
    program(nc, *args, out)
    result = run_bass_kernel_spmd(nc, [arrays], core_ids=[0]).results[0]["outT"]
    return np.asarray(result).transpose(1, 0, 2).reshape(D, SEQ).T.reshape(1, SEQ, D)
```
